# Optimizing a Trainium2 kernel written in Bass

```python
import jax
import jax.numpy as jnp
from jax import lax
import numpy as np

D_MODEL = 1024
BATCH = 1
SEQ = 128
DEPTH = 2
DEC_BATCH = 1
DEC_SEQ = 256
PAST_LEN = 128

GRID_W = 64
N_MIXERS = 2
N_MLSTM_LAYERS = (DEPTH + 1) // 2
N_ATTN_LAYERS = DEPTH // 2
EPS = 1e-6

M_HEADS = 4
M_DQK = D_MODEL // (2 * M_HEADS)
M_DV = D_MODEL // M_HEADS
M_CHUNK = 128
M_CONV_W = 3
M_QK_DIM = 2 * M_HEADS * M_DQK
M_V_DIM = M_HEADS * M_DV
M_IN_DIM = M_QK_DIM + M_V_DIM + M_V_DIM + 4 * M_HEADS
M_F_BIAS_LO = 3.0
M_F_BIAS_HI = 6.0

A_HEADS = 16
A_KV_HEADS = 4
A_HEAD_DIM = D_MODEL // A_HEADS
A_ROPE_AXIS = A_HEAD_DIM // 2
ROPE_THETA = 10000.0
Q_BLOCK = 128
A_QKV_DIM = (A_HEADS + 2 * A_KV_HEADS) * A_HEAD_DIM

P_HEADS = 8
P_NKEYS = 128
P_NEXPERTS = P_NKEYS * P_NKEYS
P_DKEY = 256
P_TOPK = 16
P_TOKEN_BLOCK = 128

kernel_name = 'hybrid_mlstm_gqa_peer_diffusion_step'

def rms_norm(x, g):
    xf = x.astype(jnp.float32)
    y = xf * lax.rsqrt(jnp.mean(xf * xf, axis=-1, keepdims=True) + EPS)
    return (y * g.astype(jnp.float32)).astype(x.dtype)

def ada_mod(cond, w, b):
    m = jax.nn.silu(cond) @ w + b
    return jnp.split(m[..., None, :], 6, axis=-1)

def modulate(x, g, shift, scale):
    return rms_norm(x, g) * (1 + scale) + shift

def short_conv(x, w, b):
    c = x.shape[-1]
    y = lax.conv_general_dilated(x, w[:, None, :].astype(x.dtype), window_strides=(1,),
                                 padding=[((M_CONV_W - 1) // 2, M_CONV_W // 2)],
                                 dimension_numbers=('NWC', 'WIO', 'NWC'), feature_group_count=c)
    return jax.nn.silu(y + b)

def mlstm_project(h, w_in, conv_w, conv_b, gate_b):
    B, S, _ = h.shape
    p = h @ w_in
    qk, v, o, gates = jnp.split(p, [M_QK_DIM, M_QK_DIM + M_V_DIM, M_QK_DIM + 2 * M_V_DIM], axis=-1)
    q, k = jnp.split(short_conv(qk, conv_w, conv_b), 2, axis=-1)
    heads = lambda t, d: t.reshape(B, S, M_HEADS, d).transpose(0, 2, 1, 3).astype(jnp.float32)
    q = heads(q, M_DQK)
    k = heads(k, M_DQK) * (M_DQK ** -0.5)
    v = heads(v, M_DV)
    g = (gates + gate_b).astype(jnp.float32).reshape(B, S, 4, M_HEADS).transpose(2, 0, 3, 1)
    gf = (g[0], jax.nn.log_sigmoid(g[1]))
    gb = (g[2], jax.nn.log_sigmoid(g[3]))
    return q, k, v, o, gf, gb

def mlstm_chunk_scan(q, k, v, ig, lf, C0, n0, m0):
    B, NH, S, _ = q.shape
    nc = S // M_CHUNK
    chunks = lambda t: jnp.moveaxis(t.reshape(B, NH, nc, M_CHUNK, *t.shape[3:]), 2, 0)
    lower = jnp.tril(jnp.ones((M_CHUNK, M_CHUNK), dtype=bool))

    def step(carry, xs):
        C, n, m = carry
        qc, kc, vc, ic, fc = xs
        b = jnp.cumsum(fc, axis=-1)
        d = jnp.where(lower, b[..., :, None] - b[..., None, :] + ic[..., None, :], -jnp.inf)
        inter = b + m[..., None]
        m_t = jnp.maximum(inter, jnp.max(d, axis=-1))
        w = jnp.exp(d - m_t[..., None]) * jnp.einsum('bhtd,bhsd->bhts', qc, kc)
        a = jnp.exp(inter - m_t)
        num = a[..., None] * jnp.einsum('bhtd,bhdv->bhtv', qc, C) + jnp.einsum('bhts,bhsv->bhtv', w, vc)
        den = a * jnp.einsum('bhtd,bhd->bht', qc, n) + jnp.sum(w, axis=-1)
        h = num / jnp.maximum(jnp.abs(den), jnp.exp(-m_t))[..., None]
        b_end = b[..., -1]
        to_end = b_end[..., None] - b + ic
        m_new = jnp.maximum(b_end + m, jnp.max(to_end, axis=-1))
        decay = jnp.exp(b_end + m - m_new)
        we = jnp.exp(to_end - m_new[..., None])
        C_new = decay[..., None, None] * C + jnp.einsum('bhs,bhsd,bhsv->bhdv', we, kc, vc)
        n_new = decay[..., None] * n + jnp.einsum('bhs,bhsd->bhd', we, kc)
        return (C_new, n_new, m_new), h

    state, h = lax.scan(step, (C0, n0, m0), (chunks(q), chunks(k), chunks(v), chunks(ig), chunks(lf)))
    h = jnp.moveaxis(h, 0, 2).reshape(B, NH, S, -1)
    return h, state

def mlstm_bidirectional(q, k, v, gf, gb, init_f, init_b):
    flip = lambda t: jnp.flip(t, axis=2)
    hf, sf = mlstm_chunk_scan(q, k, v, gf[0], gf[1], *init_f)
    hb, sb = mlstm_chunk_scan(flip(q), flip(k), flip(v), flip(gb[0]), flip(gb[1]), *init_b)
    return hf + flip(hb), sf, sb

def mlstm_output(h, o, head_g, w_out):
    B, NH, S, DV = h.shape
    hn = h * lax.rsqrt(jnp.mean(h * h, axis=-1, keepdims=True) + EPS)
    hn = hn.transpose(0, 2, 1, 3).reshape(B, S, NH * DV).astype(o.dtype) * head_g
    return (hn * jax.nn.sigmoid(o)) @ w_out

def attn_project(h, w_qkv, q_g, k_g):
    B, S, _ = h.shape
    q, k, v = jnp.split(h @ w_qkv, [A_HEADS * A_HEAD_DIM, (A_HEADS + A_KV_HEADS) * A_HEAD_DIM], axis=-1)
    q = rms_norm(q.reshape(B, S, A_HEADS, A_HEAD_DIM), q_g).transpose(0, 2, 1, 3)
    k = rms_norm(k.reshape(B, S, A_KV_HEADS, A_HEAD_DIM), k_g).transpose(0, 2, 1, 3)
    v = v.reshape(B, S, A_KV_HEADS, A_HEAD_DIM).transpose(0, 2, 1, 3)
    return q, k, v

def axial_rope_tables(n_rows):
    rows = jnp.repeat(jnp.arange(n_rows, dtype=jnp.float32), GRID_W)
    cols = jnp.tile(jnp.arange(GRID_W, dtype=jnp.float32), n_rows)
    half = A_ROPE_AXIS // 2
    inv_freq = ROPE_THETA ** (-jnp.arange(half, dtype=jnp.float32) / half)
    ang = jnp.concatenate([rows[:, None] * inv_freq, cols[:, None] * inv_freq], axis=-1)
    return jnp.cos(ang), jnp.sin(ang)

def apply_axial_rope(x, cos, sin):
    B, H, S, HD = x.shape
    half = A_ROPE_AXIS // 2
    xa = x.reshape(B, H, S, 2, 2, half)
    x1, x2 = xa[..., 0, :], xa[..., 1, :]
    c = cos.reshape(S, 2, half).astype(x.dtype)
    s = sin.reshape(S, 2, half).astype(x.dtype)
    out = jnp.stack([x1 * c - x2 * s, x2 * c + x1 * s], axis=-2)
    return out.reshape(B, H, S, HD)

def block_attention(q, k, v):
    B, NQ, Sq, HD = q.shape
    G = NQ // A_KV_HEADS
    nb = Sq // Q_BLOCK
    qb = jnp.moveaxis(q.reshape(B, A_KV_HEADS, G, nb, Q_BLOCK, HD), 3, 0)
    scale = HD ** -0.5

    def one_block(qblk):
        s = jnp.einsum('bkgqd,bksd->bkgqs', qblk, k, preferred_element_type=jnp.float32) * scale
        p = jax.nn.softmax(s, axis=-1).astype(v.dtype)
        return jnp.einsum('bkgqs,bksd->bkgqd', p, v)

    o = jnp.moveaxis(lax.map(one_block, qb), 0, 3).reshape(B, NQ, Sq, HD)
    return o.transpose(0, 2, 1, 3).reshape(B, Sq, NQ * HD)

def peer_ffn(h, w_q, subkeys, u, v):
    B, S, D = h.shape
    xb_all = h.reshape((B * S) // P_TOKEN_BLOCK, P_TOKEN_BLOCK, D)

    def one_block(xb):
        q = (xb @ w_q).reshape(P_TOKEN_BLOCK, P_HEADS, 2, P_DKEY // 2)
        s = jnp.einsum('tphd,phnd->tphn', q, subkeys, preferred_element_type=jnp.float32)
        s1, i1 = lax.top_k(s[:, :, 0], P_TOPK)
        s2, i2 = lax.top_k(s[:, :, 1], P_TOPK)
        cand = (s1[..., :, None] + s2[..., None, :]).reshape(P_TOKEN_BLOCK, P_HEADS, P_TOPK * P_TOPK)
        cidx = (i1[..., :, None] * P_NKEYS + i2[..., None, :]).reshape(P_TOKEN_BLOCK, P_HEADS, P_TOPK * P_TOPK)
        top, pos = lax.top_k(cand, P_TOPK)
        eidx = jnp.take_along_axis(cidx, pos, axis=-1)
        g = jax.nn.softmax(top, axis=-1).astype(xb.dtype)
        act = jax.nn.gelu(jnp.einsum('tped,td->tpe', u[eidx], xb), approximate=False)
        return jnp.einsum('tpe,tped->td', g * act, v[eidx])

    return lax.map(one_block, xb_all).reshape(B, S, D)

def setup_inputs(seed: int = 0) -> dict:
    key = jax.random.key(seed)
    ks = jax.random.split(key, 28)
    nrm = lambda k, shape, s: jax.random.normal(k, shape, jnp.float32) * s
    f_bias = jnp.linspace(M_F_BIAS_LO, M_F_BIAS_HI, M_HEADS, dtype=jnp.float32)
    zeros_h = jnp.zeros((M_HEADS,), jnp.float32)
    gate_base = jnp.concatenate([zeros_h, f_bias, zeros_h, f_bias])
    return {
        'x_prompt': nrm(ks[0], (BATCH, SEQ, D_MODEL), 1.0),
        'x_sample': nrm(ks[1], (DEC_BATCH, DEC_SEQ, D_MODEL), 1.0),
        'state_mlstm_C': nrm(ks[2], (DEC_BATCH, N_MLSTM_LAYERS, 2, M_HEADS, M_DQK, M_DV), 0.1),
        'state_mlstm_n': nrm(ks[3], (DEC_BATCH, N_MLSTM_LAYERS, 2, M_HEADS, M_DQK), 0.1),
        'state_mlstm_m': nrm(ks[4], (DEC_BATCH, N_MLSTM_LAYERS, 2, M_HEADS), 1.0),
        'cache_attn_k': nrm(ks[5], (DEC_BATCH, N_ATTN_LAYERS, A_KV_HEADS, PAST_LEN, A_HEAD_DIM), 1.0),
        'cache_attn_v': nrm(ks[6], (DEC_BATCH, N_ATTN_LAYERS, A_KV_HEADS, PAST_LEN, A_HEAD_DIM), 1.0),
        'c': nrm(ks[7], (DEC_BATCH, D_MODEL), 1.0),
        'c_ctx': nrm(ks[8], (D_MODEL,), 1.0),
        'ada_w': nrm(ks[9], (DEPTH, D_MODEL, 6 * D_MODEL), D_MODEL ** -0.5),
        'ada_b': nrm(ks[10], (DEPTH, 6 * D_MODEL), 0.01),
        'norm_g': 1.0 + nrm(ks[11], (DEPTH, 2, D_MODEL), 0.01),
        'final_g': 1.0 + nrm(ks[12], (D_MODEL,), 0.01),
        'mlstm_w_in': nrm(ks[13], (N_MLSTM_LAYERS, D_MODEL, M_IN_DIM), D_MODEL ** -0.5),
        'mlstm_conv_w': nrm(ks[14], (N_MLSTM_LAYERS, M_CONV_W, M_QK_DIM), M_CONV_W ** -0.5),
        'mlstm_conv_b': nrm(ks[15], (N_MLSTM_LAYERS, M_QK_DIM), 0.01),
        'mlstm_gate_b': gate_base + nrm(ks[16], (N_MLSTM_LAYERS, 4 * M_HEADS), 0.01),
        'mlstm_head_g': 1.0 + nrm(ks[17], (N_MLSTM_LAYERS, M_V_DIM), 0.01),
        'mlstm_w_out': nrm(ks[18], (N_MLSTM_LAYERS, M_V_DIM, D_MODEL), M_V_DIM ** -0.5),
        'attn_w_qkv': nrm(ks[19], (N_ATTN_LAYERS, D_MODEL, A_QKV_DIM), D_MODEL ** -0.5),
        'attn_q_g': 1.0 + nrm(ks[20], (N_ATTN_LAYERS, A_HEAD_DIM), 0.01),
        'attn_k_g': 1.0 + nrm(ks[21], (N_ATTN_LAYERS, A_HEAD_DIM), 0.01),
        'attn_w_out': nrm(ks[22], (N_ATTN_LAYERS, A_HEADS * A_HEAD_DIM, D_MODEL), (A_HEADS * A_HEAD_DIM) ** -0.5),
        'peer_w_q': nrm(ks[23], (DEPTH, D_MODEL, P_HEADS * P_DKEY), D_MODEL ** -0.5),
        'peer_subkeys': nrm(ks[24], (DEPTH, P_HEADS, 2, P_NKEYS, P_DKEY // 2), (P_DKEY // 2) ** -0.5),
        'peer_u': nrm(ks[25], (DEPTH, P_NEXPERTS, D_MODEL), D_MODEL ** -0.5),
        'peer_v': nrm(ks[26], (DEPTH, P_NEXPERTS, D_MODEL), P_HEADS ** -0.5),
    }

def reference(x_prompt, x_sample, state_mlstm_C, state_mlstm_n, state_mlstm_m, cache_attn_k, cache_attn_v,
              c, c_ctx, ada_w, ada_b, norm_g, final_g, mlstm_w_in, mlstm_conv_w, mlstm_conv_b, mlstm_gate_b,
              mlstm_head_g, mlstm_w_out, attn_w_qkv, attn_q_g, attn_k_g, attn_w_out,
              peer_w_q, peer_subkeys, peer_u, peer_v):
    f32 = lambda t: t.astype(jnp.float32)

    x = x_prompt
    B = x.shape[0]
    st_C, st_n, st_m, kv_k, kv_v = [], [], [], [], []
    for i in range(DEPTH):
        j = i // N_MIXERS
        sh1, sc1, g1, sh2, sc2, g2 = ada_mod(c_ctx, ada_w[i], ada_b[i])
        h = modulate(x, norm_g[i, 0], sh1, sc1)
        if i % N_MIXERS == 0:
            q, k, v, o, gf, gb = mlstm_project(h, mlstm_w_in[j], mlstm_conv_w[j], mlstm_conv_b[j], mlstm_gate_b[j])
            zero = (jnp.zeros((B, M_HEADS, M_DQK, M_DV), jnp.float32),
                    jnp.zeros((B, M_HEADS, M_DQK), jnp.float32),
                    jnp.zeros((B, M_HEADS), jnp.float32))
            hm, sf, sb = mlstm_bidirectional(q, k, v, gf, gb, zero, zero)
            out = mlstm_output(hm, o, mlstm_head_g[j], mlstm_w_out[j])
            st_C.append(jnp.stack([sf[0], sb[0]], axis=1))
            st_n.append(jnp.stack([sf[1], sb[1]], axis=1))
            st_m.append(jnp.stack([sf[2], sb[2]], axis=1))
        else:
            q, k, v = attn_project(h, attn_w_qkv[j], attn_q_g[j], attn_k_g[j])
            out = block_attention(q, k, v) @ attn_w_out[j]
            kv_k.append(k)
            kv_v.append(v)
        x = x + g1 * out
        x = x + g2 * peer_ffn(modulate(x, norm_g[i, 1], sh2, sc2), peer_w_q[i], peer_subkeys[i], peer_u[i], peer_v[i])
    y_prompt = rms_norm(x, final_g)
    new_mlstm_C = jnp.stack(st_C, axis=1).astype(x.dtype)
    new_mlstm_n = jnp.stack(st_n, axis=1).astype(x.dtype)
    new_mlstm_m = jnp.stack(st_m, axis=1).astype(x.dtype)
    new_attn_k = jnp.stack(kv_k, axis=1)
    new_attn_v = jnp.stack(kv_v, axis=1)

    x = x_sample
    n_rows = x.shape[1] // GRID_W
    cos, sin = axial_rope_tables(n_rows)
    for i in range(DEPTH):
        j = i // N_MIXERS
        sh1, sc1, g1, sh2, sc2, g2 = ada_mod(c, ada_w[i], ada_b[i])
        h = modulate(x, norm_g[i, 1 - 1], sh1, sc1)
        if i % N_MIXERS == 0:
            q, k, v, o, gf, gb = mlstm_project(h, mlstm_w_in[j], mlstm_conv_w[j], mlstm_conv_b[j], mlstm_gate_b[j])
            init_f = (f32(state_mlstm_C[:, j, 0]), f32(state_mlstm_n[:, j, 0]), f32(state_mlstm_m[:, j, 0]))
            init_b = (f32(state_mlstm_C[:, j, 1]), f32(state_mlstm_n[:, j, 1]), f32(state_mlstm_m[:, j, 1]))
            hm, _, _ = mlstm_bidirectional(q, k, v, gf, gb, init_f, init_b)
            out = mlstm_output(hm, o, mlstm_head_g[j], mlstm_w_out[j])
        else:
            q, k, v = attn_project(h, attn_w_qkv[j], attn_q_g[j], attn_k_g[j])
            q = apply_axial_rope(q, cos, sin)
            k = apply_axial_rope(k, cos, sin)
            k_all = jnp.concatenate([cache_attn_k[:, j].astype(k.dtype), k], axis=2)
            v_all = jnp.concatenate([cache_attn_v[:, j].astype(v.dtype), v], axis=2)
            out = block_attention(q, k_all, v_all) @ attn_w_out[j]
        x = x + g1 * out
        x = x + g2 * peer_ffn(modulate(x, norm_g[i, 1], sh2, sc2), peer_w_q[i], peer_subkeys[i], peer_u[i], peer_v[i])
    y_sample = rms_norm(x, final_g)

    return (y_prompt, y_sample, new_mlstm_C, new_mlstm_n, new_mlstm_m, new_attn_k, new_attn_v)


_drawn_inputs = setup_inputs


def setup_inputs(seed=0):
    import zlib

    import numpy as np

    out = dict(_drawn_inputs(seed))
    spreads = {}
    factors = {'state_mlstm_n': 4.831,
     'norm_g': 2.961,
     'final_g': 5.724,
     'mlstm_conv_b': 4.866,
     'mlstm_head_g': 4.825,
     'attn_q_g': 8.0,
     'attn_k_g': 7.579}
    for name, (base, spread) in spreads.items():
        noise = np.random.default_rng([zlib.crc32(name.encode()), seed]).standard_normal(out[name].shape)
        drawn = base * np.exp(spread * noise) if base else spread * noise
        out[name] = jnp.asarray(drawn.astype(out[name].dtype))
    for name, factor in factors.items():
        out[name] = (out[name] * factor).astype(out[name].dtype)
    return out
```

```python
import concourse.bass as bass
from concourse import mybir
from contextlib import ExitStack
import numpy as np

F32 = mybir.dt.float32
U32 = mybir.dt.uint32
ALU = mybir.AluOpType
ACT = mybir.ActivationFunctionType
AX = mybir.AxisListType

P = 128
D = 1024
KC = D // P
EPS = 1e-6
DEPTH = 2
MH, DQK, DV = 4, 128, 256
KSCALE = DQK ** -0.5
AH, AKV, HD = 16, 4, 64
ASCALE = HD ** -0.5
QKV = (AH + 2 * AKV) * HD
PH, NKEYS, TOPK = 8, 128, 16
NSETS = 2 * PH
EXPERTS = NKEYS * NKEYS
SLOTS = PH * TOPK
GS = 4
GROUPS = SLOTS // GS
RING = 3
WC = 256
WRING = 3
BANKS = 6
NEG = -1.0e30

BLOCKS = {"P": [0], "S": [1, 2]}
COND = [0, 1, 1]

SMALL, _at = {}, 0
for _name, _n in [("ident", P), ("ones", P), ("tri", 2 * P), ("mask", 2 * P), ("iota", TOPK),
                  ("cos", 2 * 32), ("sin", 2 * 32), ("cond", 2 * KC), ("ada_b", DEPTH * 48),
                  ("norm_g", DEPTH * 2 * KC), ("final_g", KC), ("head_g", KC), ("conv_w", 3 * KC),
                  ("conv_b", KC), ("gate_b", 16), ("q_g", HD), ("k_g", HD), ("m0", 8), ("w_gate", KC * 16)]:
    SMALL[_name] = (_at, _n)
    _at += _n
NSMALL = _at


def plan():
    def mlstm(g):
        nb = len(BLOCKS[g])
        yield from (("NORM", 0, 0, b) for b in BLOCKS[g])
        yield from (("MLQK", g, h) for h in range(2))
        yield from (("MLV", g, h) for h in range(2))
        yield ("MLG", g)
        for d in range(2):
            order = list(range(nb))[::1 - 2 * d]
            for n, b in enumerate(order):
                yield ("MLA", g, d, b)
                yield ("MLB", g, d, b)
                if g == "P" or n < nb - 1:
                    yield ("MLC", g, d, b)
        yield ("MLN", g)
        yield from (("MLO", g, h) for h in range(2))
        yield ("T2", 0, g)
        yield from (("OUT", 0, g, h) for h in range(2))

    def attention(g):
        nb = len(BLOCKS[g])
        yield from (("NORM", 1, 0, b) for b in BLOCKS[g])
        yield from (("AQKV", g, h) for h in range(3))
        if g == "S":
            yield ("AC", g)
        yield from (("AN", g, b) for b in range(nb))
        yield from (("AT", g, b) for b in range(nb))
        yield from (("AS", g, b, kv) for b in range(nb) for kv in range(AKV))
        yield ("T2", 1, g)
        yield from (("OUT", 1, g, h) for h in range(2))

    def prep(l, g):
        yield from (("NORM", l, 1, b) for b in BLOCKS[g])
        yield from (("PQ", l, g, q) for q in range(4))
        for b in range(len(BLOCKS[g])):
            yield ("PS", l, g, b)
            yield from (("PT", l, g, b, q) for q in range(4))
            yield from (("PC", l, g, b, q) for q in range(2))
            yield ("PG", l, g, b)

    def spread(l, b, steps):
        steps = list(steps)
        done = 0
        for n, s in enumerate(steps):
            upto = (GROUPS - 2) * n // len(steps)
            if upto > done:
                yield ("GROUPS", l, b, done, upto)
                done = upto
            yield s
        yield ("GROUPS", l, b, done, GROUPS)
        yield ("FIN", l, b)

    yield ("MOD", 0, 0)
    yield ("INIT",)
    yield from (("MOD", 0, q) for q in range(1, 3))
    yield from mlstm("P")
    yield from prep(0, "P")
    yield from spread(0, 0, [*mlstm("S"), *prep(0, "S")])
    yield from spread(0, 1, [*(("MOD", 1, q) for q in range(3)), *attention("P"), *prep(1, "P")])
    yield from spread(0, 2, [])
    yield from spread(1, 0, [*attention("S"), *prep(1, "S")])
    yield ("YOUT", 0)
    yield from spread(1, 1, [])
    yield ("YOUT", 1)
    yield from spread(1, 2, [])
    yield ("YOUT", 2)


PLAN = list(plan())
PLAN[0], PLAN[1] = PLAN[1], PLAN[0]


def psum_tiles(s):
    k = s[0]
    nb = len(BLOCKS[s[1]]) if len(s) > 1 and s[1] in ("P", "S") else 0
    if k == "MOD":
        return "D" * 8
    if k == "NORM":
        return "AD"
    if k == "MLQK":
        return "AAAA"
    if k in ("MLV", "MLO", "AQKV"):
        return "A" * (2 * nb)
    if k == "MLG":
        return "DD"
    if k == "MLA":
        return "DDA"
    if k == "MLB":
        return "AD" * MH if s[1] == "S" else "D" * MH
    if k == "MLC":
        return "D" * (1 + MH)
    if k == "T2":
        return "A" * (2 * len(BLOCKS[s[2]]) + 2)
    if k == "OUT":
        return "D" * (2 * len(BLOCKS[s[2]]))
    if k == "PQ":
        return "AAAA"
    if k == "PS":
        return "DDDDAA"
    if k == "AC":
        return "A"
    if k == "AT":
        return "AAA"
    if k == "AS":
        return "AAAADDDDD"
    if k in ("FIN", "YOUT"):
        return "AA"
    return ""


def weight_tiles(s, A):
    k = s[0]

    def cols(w, first, n, per):
        w = w.rearrange("(k p) n -> p k n", p=P)
        return [(w[:, :, (first + j) * WC:(first + j + 1) * WC], per * (j + 1) - 1) for j in range(n)]

    if k == "MOD":
        w = A["ada_w"][s[1]].rearrange("(p k) n -> p k n", p=P)
        return [(w[:, :, (8 * s[2] + j) * WC:(8 * s[2] + j + 1) * WC], j) for j in range(8)]
    if k == "MLQK":
        return cols(A["mlstm_w_in"][0], 2 * s[2], 2, 2)
    if k == "MLV":
        return cols(A["mlstm_w_in"][0], 4 + 2 * s[2], 2, len(BLOCKS[s[1]]))
    if k == "MLO":
        return cols(A["mlstm_w_in"][0], 8 + 2 * s[2], 2, len(BLOCKS[s[1]]))
    if k == "AQKV":
        return cols(A["attn_w_qkv"][0], 2 * s[2], 2, len(BLOCKS[s[1]]))
    if k == "OUT":
        w = A["mlstm_w_out"] if s[1] == 0 else A["attn_w_out"]
        return cols(w[0], 2 * s[3], 2, len(BLOCKS[s[2]]))
    if k == "PQ":
        return cols(A["peer_w_q"][s[1]], 2 * s[3], 2, 2)
    if k == "PS":
        return [(A["subkeys"][s[1]].rearrange("p (k n) -> p k n", k=KC), 3)]
    return []


ACT_ENDS = ("INIT", "MLQK")


def dve_ends(s):
    return s[0] in ("MLV", "MLG", "MLB", "MLN", "MLO", "OUT", "PT", "PC", "PG", "AN", "FIN", "YOUT") \
        or (s[0] == "MOD" and s[2] != 1)


def trunk(nc, A, O):
    ctx = ExitStack()
    with ctx:
        def sb(name, shape, dt=F32):
            return ctx.enter_context(nc.sbuf_tensor(name, shape, dt))

        def sem(name):
            return ctx.enter_context(nc.semaphore(name))

        rows = sb("rows", [P, RING * GS, 2 * D])
        wt = sb("wt", [P, WRING, KC * WC])
        x = sb("x", [P, 3, D])
        xb = sb("xb", [P, 3, D])
        hT = sb("hT", [P, KC, 2 * P])
        small = sb("small", [P, NSMALL])
        diag = sb("diag", [P, RING * GS, P])
        eidx = sb("eidx", [P, 3, SLOTS], U32)
        gate = sb("gate", [P, 3, SLOTS])
        act_in = sb("act_in", [P, RING, GS])
        act_out = sb("act_out", [P, RING, GS])
        wv = sb("wv", [P, RING, GS])
        cs = sb("cs", [P, KC, 2])
        modT = sb("modT", [P, DEPTH, 48, 2])
        gain = sb("gain", [P, DEPTH, 2, KC, 2])
        st = sb("st", [P, 256])
        ARENA = 8448
        arena = sb("arena", [P, ARENA])

        def cst(name):
            a, n = SMALL[name]
            return small[:, a:a + n]

        ident, ones = cst("ident"), cst("ones")
        tri = cst("tri").rearrange("p (d n) -> p d n", d=2)
        mask = cst("mask").rearrange("p (d n) -> p d n", d=2)
        norm_g = cst("norm_g").rearrange("p (l w k) -> p l w k", l=DEPTH, w=2)
        ada_b = cst("ada_b").rearrange("p (l n) -> p l n", l=DEPTH)
        conv_w = cst("conv_w").rearrange("p (f j) -> p f j", j=3)
        w_gate = cst("w_gate").rearrange("p (k n) -> p k n", k=KC)

        def area(at, *shape):
            n = 1
            for v in shape:
                n *= v
            assert at + n <= ARENA, (at, shape)
            a = arena[:, at:at + n]
            if len(shape) == 2:
                a = a.rearrange("p (a b) -> p a b", b=shape[1])
            if len(shape) == 3:
                a = a.rearrange("p (a b c) -> p a b c", b=shape[1], c=shape[2])
            return a, at + n

        xn, at = area(0, D)
        raw, _ = area(at, KC, 2 * P + 2)
        hm, _ = area(at, 2, D)
        at += KC * (2 * P + 2)
        cv, at = area(at, KC, 2 * P)
        va, at = area(at, 2, MH, DV + 1)
        Cst, at = area(at, MH, DV + 1)
        W = xn[:, 0:512].rearrange("p (h n) -> p h n", n=P)
        WT = xn[:, 512:1024].rearrange("p (h n) -> p h n", n=P)
        Nn = sb("Nn", [P, MH, DV + 1])
        Nflat = Nn[:].rearrange("p a b -> p (a b)")
        gbc = Nflat[:, 0:D]
        qkv, at = area(D, 2, QKV)
        qTa, at = area(at, AH // 2, 2 * P)
        kTa, at = area(at, AKV, 3 * P)
        kdup, at = area(at, AKV, 2, HD)
        vc, at = area(at, AKV, HD)
        sq20 = area(D + 2 * QKV, 20 * HD)[0]
        prA = [hT[:].rearrange("p a b -> p (a b)")[:, i * 3 * P:(i + 1) * 3 * P] for i in range(4)]
        pTa = [xn[:, i * 3 * P:(i + 1) * 3 * P] for i in range(2)]
        qTp, at = area(D, NSETS, 2 * P)
        sc, at = area(at, NSETS, NKEYS)
        cand, at = area(at, PH // 2, TOPK * TOPK)
        top1 = Nflat[:, 0:256].rearrange("p (s k) -> p s k", k=TOPK)
        i1f = Nflat[:, 256:512].rearrange("p (s k) -> p s k", k=TOPK)
        topc = Nflat[:, 512:640].rearrange("p (s k) -> p s k", k=TOPK)
        pij = Nflat[:, 640:896].rearrange("p (a s) -> p a s", a=2)
        i1u = xn[:, 0:256].bitcast(U32).rearrange("p (s k) -> p s k", k=TOPK)
        posu = xn[:, 256:384].bitcast(U32).rearrange("p (s k) -> p s k", k=TOPK)
        piju = xn[:, 384:640].bitcast(U32).rearrange("p (a s) -> p a s", a=2)
        e12 = xn[:, 640:896].rearrange("p (a s) -> p a s", a=2)

        def cols(a, n):
            return st[:, a:a + n]
        ssq, ms, sd, rstd = (cols(i * 20, 20) for i in range(4))
        ig = cols(80, 16).rearrange("p (b d h) -> p b d h", b=2, d=2)
        nlf = cols(96, 16).rearrange("p (b d h) -> p b d h", b=2, d=2)
        bt = cols(112, 32).rearrange("p (b n) -> p b n", b=2)
        rcol = cols(144, 16).rearrange("p (b d h) -> p b d h", b=2, d=2)
        mst = cols(160, 8).rearrange("p (d h) -> p d h", d=2)
        rall, rmx, nMp = cols(168, 4), cols(172, 4), cols(176, 4)
        t12, ae = cols(180, 8), cols(188, 8)
        dww, dw = cols(196, 8), cols(204, 8)
        den, rden = cols(212, 4), cols(216, 4)
        mpp = cols(220, 4)
        smx, nsmx, rsum, rrs = cols(224, 4), cols(228, 4), cols(232, 4), cols(236, 4)
        gsum, grec = cols(240, 8), cols(248, 8)
        gtmp = sb("gtmp", [P, 4, 32])
        gates_all = gtmp[:, 0].rearrange("p (b n) -> p b n", b=2)

        acc = ctx.enter_context(nc.psum_tensor("acc", [P, D], F32))
        banks = [ctx.enter_context(nc.psum_tensor(f"bank{i}", [P, 512], F32)) for i in range(BANKS)]

        inputs_in = sem("inputs_in")
        w_in = [sem(f"weights_in{i}") for i in range(WRING)]
        rows_in = [sem(f"rows_in{i}") for i in range(RING * GS)]
        tile_full = sem("tile_full")
        freed = {"A": sem("act_emptied_tile"), "D": sem("dve_emptied_tile")}
        act_step, dve_step = sem("act_step"), sem("dve_step")
        act_chain, dve_chain = sem("act_chain"), sem("dve_chain")
        squares, mean_sq, root, normed = sem("squares"), sem("mean_sq"), sem("root"), sem("normed")
        convolved, abs_gate, soft_gate, log_gate = sem("convolved"), sem("abs_gate"), sem("soft_gate"), sem("log_gate")
        decay_rows, maxima, probs_raw = sem("decay_rows"), sem("maxima"), sem("probs_raw")
        carry_in, carry_exp, state_in, state_out = sem("carry_in"), sem("carry_exp"), sem("state_in"), sem("state_out")
        key_pairs, cache_in, row_max, kv_done = sem("key_pairs"), sem("cache_in"), sem("row_max"), sem("kv_done")
        tops, top_exp, experts_chosen = sem("tops"), sem("top_exp"), sem("experts_chosen")
        dots, gelus, weighted, diags, summed = sem("dots"), sem("gelus"), sem("weighted"), sem("diags"), sem("summed")
        sum_read, y_done, stored = sem("sum_read"), sem("y_done"), sem("stored")

        def places(eng, chain):
            owner, seen = [], {}
            count = {"A": 0, "D": 0}
            place = {"first": 0, "acts": 0, "dves": 0, "step": None, "chain": 0}

            def begin(s, with_tensor=True):
                if place["step"] is not None:
                    place["acts"] += place["step"][0] in ACT_ENDS
                    place["dves"] += dve_ends(place["step"])
                place["first"] = len(owner)
                before = dict(count)
                for e in psum_tiles(s):
                    count[e] += 1
                    owner.append((e, count[e]))
                place["step"] = s
                if with_tensor and place["first"]:
                    eng.wait_ge(tile_full, place["first"])
                if before["A"]:
                    eng.wait_ge(freed["A"], before["A"])
                if place["acts"]:
                    eng.wait_ge(act_step, place["acts"])
                if before["D"]:
                    eng.wait_ge(freed["D"], before["D"])
                if place["dves"]:
                    eng.wait_ge(dve_step, place["dves"])

            def open_tile(j):
                n = place["first"] + j
                if n >= BANKS:
                    e, c = owner[n - BANKS]
                    eng.wait_ge(freed[e], c)
                return banks[n % BANKS]

            def full_tile(j):
                n = place["first"] + j
                eng.wait_ge(tile_full, n + 1)
                return banks[n % BANKS]

            def emptied(j):
                e, c = owner[place["first"] + j]
                eng.wait_ge(freed[e], c)

            def next_of(sem, k=1):
                key = id(sem)
                seen[key] = seen.get(key, 0) + k
                eng.wait_ge(sem, seen[key])

            def note(ins):
                ins.then_inc(chain, 1)
                place["chain"] += 1

            def settle():
                if place["chain"]:
                    eng.wait_ge(chain, place["chain"])

            def link(ins):
                note(ins)
                settle()

            return begin, open_tile, full_tile, emptied, next_of, note, settle, link

        def tok(b):
            return slice(b * P, (b + 1) * P)

        GORDER = [(0, 0), (0, 1), (0, 2), (1, 0), (1, 1), (1, 2)]

        def run_groups(eng, s, body):
            _, l, b, lo, hi = s
            base = GORDER.index((l, b)) * GROUPS
            g = lo
            if g == 0:
                body(base, 0, base % RING, True, (base // RING))
                g = 1
            whole = (hi - g) // RING
            if whole >= 2:
                with eng.Fori(0, whole) as i:
                    for k in range(RING):
                        n = base + g + k
                        body(i * RING + n, i * (RING * GS) + (g + k) * GS, n % RING, False, i + n // RING)
                g += whole * RING
            for k in range(g, hi):
                n = base + k
                body(n, k * GS, n % RING, False, n // RING)

        block = ctx.enter_context(nc.Block())

        @block.sync
        def _(sp):
            sp.dma_start(small[:], A["small"]).then_inc(inputs_in, 16)
            sp.dma_start(x[:, 0, :], A["x_prompt"][0]).then_inc(inputs_in, 16)
            sp.dma_start(x[:, 1:3, :], A["x_sample"][0].rearrange("(b p) n -> p b n", p=P)).then_inc(inputs_in, 16)
            tiles, free_at, n = 0, [], 0
            for s in PLAN:
                for src, last in weight_tiles(s, A):
                    if n >= WRING:
                        sp.wait_ge(tile_full, free_at[n - WRING])
                    sp.dma_start(wt[:, n % WRING, :].rearrange("p (k n) -> p k n", k=KC), src)\
                        .then_inc(w_in[n % WRING], 16)
                    free_at.append(tiles + last + 1)
                    n += 1
                tiles += len(psum_tiles(s))

        @block.gpsimd
        def _(pool):
            for n, (l, b) in enumerate(GORDER):
                pool.wait_ge(experts_chosen, n + 1)
                for g in range(n * GROUPS, (n + 1) * GROUPS):
                    if g >= RING:
                        pool.wait_ge(summed, g - RING + 1)
                    for j in range(GS):
                        r = (g % RING) * GS + j
                        slot = (g - n * GROUPS) * GS + j
                        nc.gpsimd.indirect_dma_start(
                            out=rows[:, r, :], out_offset=None, in_=A["uv"],
                            in_offset=bass.IndirectOffsetOnAxis(ap=eidx[:, b, slot:slot + 1], axis=0))\
                            .then_inc(rows_in[r], 16)

        @block.tensor
        def _(pe):
            begin, open_tile, full_tile, emptied, next_of, note, settle, link = places(pe, None)
            used = [0]

            def mm(out, lhsT, rhs, start, stop):
                return nc.tensor.matmul(out, lhsT, rhs, start=start, stop=stop)

            def weights():
                n = used[0]
                used[0] += 1
                pe.wait_ge(w_in[n % WRING], 16 * (n // WRING + 1))
                return wt[:, n % WRING, :].rearrange("p (k n) -> p k n", k=KC)

            def product(out, lhs, rhs):
                for k in range(KC):
                    last = mm(out, lhs(k), rhs(k), k == 0, k == KC - 1)
                return last

            def transposes(out, ins):
                for i, a in enumerate(ins):
                    last = nc.tensor.transpose(out[:, i * P:(i + 1) * P], a, ident)
                return last

            def by_token(n_tiles, blocks):
                for j in range(n_tiles):
                    w = weights()
                    for b in range(blocks):
                        t = open_tile(j * blocks + b)
                        product(t[:, 0:WC], lambda k: hT[:, k, tok(b)], lambda k: w[:, k, :]).then_inc(tile_full, 1)

            def by_feature(n_tokens):
                for j in range(2):
                    w = weights()
                    for i in range(2):
                        t = open_tile(2 * j + i)
                        product(t[:, 0:n_tokens], lambda k: w[:, k, i * P:(i + 1) * P],
                                lambda k: hT[:, k, 0:n_tokens]).then_inc(tile_full, 1)

            def on_all_partitions(j, column):
                for i in range(2):
                    t = open_tile(j + i)
                    for k in range(4):
                        last = mm(t[:, k * P:(k + 1) * P], column(4 * i + k).to_broadcast([P, P]), ident, True, True)
                    last.then_inc(tile_full, 1)

            def group(n, slot, ring, first, turn):
                if first and isinstance(n, int) and n:
                    pe.wait_ge(sum_read, n // GROUPS)
                pe.wait_ge(diags, n + 1)
                for j in range(GS):
                    r = ring * GS + j
                    for h in range(2):
                        last = nc.tensor.matmul(acc[:, h * 512:(h + 1) * 512], diag[:, r, :],
                                                rows[:, r, D + h * 512:D + (h + 1) * 512],
                                                start=first and j == 0, stop=True, skip_group_check=True)
                last.then_inc(summed, 1)

            pe.wait_ge(inputs_in, 48)
            for s in PLAN:
                k = s[0]
                if k == "GROUPS":
                    run_groups(pe, s, group)
                    continue
                begin(s, False)
                if k == "MOD":
                    for j in range(8):
                        w = weights()
                        t = open_tile(j)
                        for i in range(2):
                            last = product(t[:, 2 * i:2 * i + 2], lambda q: w[:, q, i * P:(i + 1) * P], lambda q: cs[:, q, :])
                        last.then_inc(tile_full, 1)
                elif k == "NORM":
                    next_of(normed)
                    for i in range(2):
                        transposes(open_tile(i), [xn[:, (4 * i + q) * P:(4 * i + q + 1) * P] for q in range(4)])\
                            .then_inc(tile_full, 1)
                elif k == "MLQK":
                    by_feature(P * len(BLOCKS[s[1]]))
                elif k in ("MLV", "MLO", "AQKV"):
                    by_token(2, len(BLOCKS[s[1]]))
                elif k == "OUT":
                    by_token(2, len(BLOCKS[s[2]]))
                elif k == "MLG":
                    nb = len(BLOCKS[s[1]])
                    t = open_tile(0)
                    for b in range(nb):
                        last = product(t[:, b * 16:b * 16 + 16], lambda q: hT[:, q, tok(b)], lambda q: w_gate[:, q, :])
                    last.then_inc(tile_full, 1)
                    next_of(log_gate)
                    t = open_tile(1)
                    for b in range(nb):
                        for d in range(2):
                            mm(t[:, b * 16 + d * 4:b * 16 + d * 4 + 4], tri[:, d, :], nlf[:, b, d, :], True, True)
                        last = mm(t[:, b * 16 + 8:b * 16 + 16], ones, nlf[:, b].rearrange("p d h -> p (d h)"), True, True)
                    last.then_inc(tile_full, 1)
                elif k == "MLA":
                    _, g, d, b = s
                    next_of(decay_rows)
                    t = open_tile(0)
                    mm(t[:], ones, W.rearrange("p h n -> p (h n)"), True, True).then_inc(tile_full, 1)
                    t = open_tile(1)
                    for h in range(MH):
                        last = mm(t[:, h * P:(h + 1) * P], cv[:, h, tok(b)], cv[:, 4 + h, tok(b)], True, True)
                    last.then_inc(tile_full, 1)
                    emptied(1)
                    transposes(open_tile(2), [W[:, h, :] for h in range(MH)]).then_inc(tile_full, 1)
                elif k == "MLB":
                    _, g, d, b = s
                    per = 2 if g == "S" else 1
                    if g == "S" and b == d:
                        next_of(state_in, 32)
                    for h in range(MH):
                        if g == "S":
                            t = open_tile(per * h)
                            mm(t[:, 0:DV + 1], cv[:, h, tok(b)], Cst[:, h, :], True, True).then_inc(tile_full, 1)
                        t = open_tile(per * h + per - 1)
                        mm(t[:, 0:DV + 1], WT[:, h, :], va[:, b, h, :], True, True).then_inc(tile_full, 1)
                elif k == "MLC":
                    _, g, d, b = s
                    transposes(open_tile(0), [cv[:, 4 + h, tok(b)] for h in range(MH)]).then_inc(tile_full, 1)
                    emptied(0)
                    for h in range(MH):
                        t = open_tile(1 + h)
                        mm(t[:, 0:DV + 1], W[:, h, :], va[:, b, h, :], True, True).then_inc(tile_full, 1)
                elif k == "T2":
                    _, l, g = s
                    src = hm if l == 0 else qkv
                    for b in range(len(BLOCKS[g])):
                        for i in range(2):
                            transposes(open_tile(2 * b + i),
                                       [src[:, b, (4 * i + q) * P:(4 * i + q + 1) * P] for q in range(4)])\
                                .then_inc(tile_full, 1)
                    c = COND[BLOCKS[g][0]]
                    on_all_partitions(2 * len(BLOCKS[g]), lambda q: modT[:, l, 16 + q, c:c + 1])
                elif k == "PQ":
                    by_feature(P * len(BLOCKS[s[2]]))
                elif k == "PS":
                    _, l, g, b = s
                    w = weights().rearrange("p k n -> p (k n)")
                    for i in range(4):
                        t = open_tile(i)
                        for q in range(4):
                            e = 4 * i + q
                            last = mm(t[:, q * P:(q + 1) * P], qTp[:, e, tok(b)], w[:, e * NKEYS:(e + 1) * NKEYS], True, True)
                        last.then_inc(tile_full, 1)
                    for i in range(2):
                        transposes(open_tile(4 + i), [hT[:, 4 * i + q, tok(b)] for q in range(4)]).then_inc(tile_full, 1)
                elif k == "AC":
                    next_of(cache_in, 48)
                    transposes(open_tile(0), [kdup[:, v, :, :].rearrange("p a n -> p (a n)") for v in range(AKV)])\
                        .then_inc(tile_full, 1)
                elif k == "AT":
                    _, g, b = s
                    for i in range(2):
                        transposes(open_tile(i), [qkv[:, b, (4 * i + q) * P:(4 * i + q + 1) * P] for q in range(4)])\
                            .then_inc(tile_full, 1)
                    next_of(key_pairs)
                    transposes(open_tile(2), [kdup[:, v, :, :].rearrange("p a n -> p (a n)") for v in range(AKV)])\
                        .then_inc(tile_full, 1)
                elif k == "AS":
                    _, g, b, kv = s
                    nk = 1 if g == "P" else 3
                    for i in range(4):
                        h = kv * 4 + i
                        half = slice((h % 2) * HD, (h % 2 + 1) * HD)
                        t = open_tile(i)
                        mm(t[:, 0:nk * P], qTa[half, h // 2, tok(b)], kTa[half, kv, 0:nk * P], True, True)\
                            .then_inc(tile_full, 1)

                    def values(i):
                        emptied(4 + i)
                        for c in range(nk):
                            v = vc[:, kv, :] if nk == 3 and c == 0 else \
                                qkv[:, c - (nk == 3), (AH + AKV + kv) * HD:(AH + AKV + kv + 1) * HD]
                            last = mm(out[:, i * HD:(i + 1) * HD], pTa[i % 2][:, c * P:(c + 1) * P], v,
                                      c == 0, c == nk - 1)
                        return last

                    out = open_tile(8)
                    for i in range(4):
                        t = open_tile(4 + i)
                        emptied(i)
                        transposes(t, [prA[i][:, c * P:(c + 1) * P] for c in range(nk)]).then_inc(tile_full, 1)
                        if i:
                            values(i - 1)
                    values(3).then_inc(tile_full, 1)
                elif k == "FIN":
                    c = COND[s[2]]
                    on_all_partitions(0, lambda q: modT[:, s[1], 40 + q, c:c + 1])
                elif k == "YOUT":
                    on_all_partitions(0, lambda q: cst("final_g")[:, q:q + 1])


        @block.scalar
        def _(act):
            begin, open_tile, full_tile, emptied, next_of, note, settle, link = places(act, act_chain)
            sent = {"stored": 0, "state_out": 0}

            def f(out, in_, func, **kw):
                return nc.scalar.activation(out, in_, func, **kw)

            def copy_tile(j, out, n=512, view=None):
                t = full_tile(j)[:, 0:n]
                f(out, view(t) if view else t, ACT.Copy).then_inc(freed["A"], 1)

            def rsqrt_parts(src, n=D):
                f(xn, src, ACT.Square, accum_out=ssq[:, 0:1]).then_inc(squares, 1)
                next_of(mean_sq)
                f(sd[:, 0:1], ms[:, 0:1], ACT.Sqrt).then_inc(root, 1)

            def group(n, slot, ring, first, turn):
                act.wait_ge(dots, n + 1)
                f(act_out[:, ring, :], act_in[:, ring, :], ACT.Gelu).then_inc(gelus, 1)
                act.wait_ge(weighted, n + 1)
                for j in range(GS):
                    last = f(diag[:, ring * GS + j, :], ident, ACT.Copy, scale=wv[:, ring, j:j + 1])
                last.then_inc(diags, 1)

            def store(out, in_):
                act.dma_start(out, in_).then_inc(stored, 16)
                sent["stored"] += 1

            act.wait_ge(inputs_in, 48)
            for s in PLAN:
                k = s[0]
                if k == "GROUPS":
                    run_groups(act, s, group)
                    continue
                begin(s)
                settle()
                if k == "INIT":
                    f(cs[:].rearrange("p k c -> p (k c)"), cst("cond"), ACT.Silu).then_inc(act_step, 1)
                elif k == "NORM":
                    _, l, w, b = s
                    c = COND[b]
                    rsqrt_parts(x[:, b, :])
                    t = full_tile(0)
                    place = tok(b - (b > 0))
                    for q in range(4):
                        last = f(hT[:, q, place], t[:, q * P:(q + 1) * P], ACT.Identity,
                                 scale=gain[:, l, w, q, c:c + 1], bias=modT[:, l, 24 * w + q, c:c + 1])
                    last.then_inc(freed["A"], 1)
                elif k == "MLQK":
                    _, g, half = s
                    n = P * len(BLOCKS[g])
                    for i in range(4):
                        copy_tile(i, raw[:, 4 * half + i, 1:n + 1], n)
                    for i in range(4):
                        e = 4 * half + i
                        next_of(convolved)
                        last = f(cv[:, e, 0:n], cv[:, e, 0:n], ACT.Silu, bias=cst("conv_b")[:, e:e + 1])
                    last.then_inc(act_step, 1)
                elif k == "MLV":
                    _, g, half = s
                    nb = len(BLOCKS[g])
                    for j in range(2):
                        for b in range(nb):
                            copy_tile(j * nb + b, va[:, b, 2 * half + j, 0:DV], WC)
                elif k == "MLG":
                    n = 8 * len(BLOCKS[s[1]])
                    next_of(abs_gate)
                    link(f(gtmp[:, 2, 0:n], gtmp[:, 1, 0:n], ACT.Exp, scale=-1.0))
                    f(gtmp[:, 3, 0:n], gtmp[:, 2, 0:n], ACT.Ln, bias=1.0).then_inc(soft_gate, 1)
                elif k == "MLA":
                    _, g, d, b = s
                    if g == "S" and b == d:
                        act.dma_start(Cst[:, :, 0:DV], A["state_mlstm_C"][0, 0, d].rearrange("h p v -> p h v"))\
                            .then_inc(state_in, 16)
                        act.dma_start(Cst[:, :, DV], A["state_mlstm_n"][0, 0, d].rearrange("h p -> p h"), allow_slow_non_contiguous=True)\
                            .then_inc(state_in, 16)
                    next_of(maxima)
                    note(f(ae, t12, ACT.Exp))
                    for h in range(MH):
                        last = f(W[:, h, :], W[:, h, :], ACT.Exp, bias=nMp[:, h:h + 1])
                    last.then_inc(probs_raw, 1)
                    copy_tile(2, WT.rearrange("p h n -> p (h n)"))
                elif k == "MLB":
                    if s[1] == "S":
                        settle()
                        for h in range(MH):
                            t = full_tile(2 * h)
                            f(Nn[:, h, :], t[:, 0:DV + 1], ACT.Copy, scale=ae[:, h:h + 1]).then_inc(freed["A"], 1)
                elif k == "MLC":
                    _, g, d, b = s
                    next_of(carry_in)
                    f(dw, dww, ACT.Exp).then_inc(carry_exp, 1)
                    if g == "P":
                        emptied(MH)
                        act.dma_start(O["new_C"][0, 0, d].rearrange("h p v -> p h v"), Cst[:, :, 0:DV]).then_inc(state_out, 16)
                        act.dma_start(O["new_n"][0, 0, d].rearrange("h p -> p h"), Cst[:, :, DV], allow_slow_non_contiguous=True).then_inc(state_out, 16)
                        act.dma_start(O["new_m"][0, 0, d:d + 1, :], mst[0:1, d, :]).then_inc(state_out, 16)
                        sent["state_out"] += 3
                elif k == "MLN":
                    for b in range(len(BLOCKS[s[1]])):
                        next_of(mean_sq)
                        f(sd[:, 0:MH], ms[:, 0:MH], ACT.Sqrt).then_inc(root, 1)
                elif k == "MLO":
                    nb = len(BLOCKS[s[1]])
                    for i in range(2 * nb):
                        t = full_tile(i)
                        f(Nflat[:, i * WC:(i + 1) * WC], t[:, 0:WC], ACT.Sigmoid).then_inc(freed["A"], 1)
                elif k == "T2":
                    _, l, g = s
                    nb = len(BLOCKS[g])
                    for b in range(nb):
                        for i in range(2):
                            t = full_tile(2 * b + i)
                            if l == 0:
                                for q in range(4):
                                    last = f(hT[:, 4 * i + q, tok(b)], t[:, q * P:(q + 1) * P], ACT.Copy,
                                             scale=cst("head_g")[:, 4 * i + q:4 * i + q + 1])
                            else:
                                last = f(hT[:, 4 * i:4 * i + 4, tok(b)], t[:].rearrange("p (q n) -> p q n", n=P), ACT.Copy)
                            last.then_inc(freed["A"], 1)
                    for i in range(2):
                        copy_tile(2 * nb + i, gbc[:, i * 512:(i + 1) * 512])
                elif k == "PQ":
                    _, l, g, q = s
                    n = P * len(BLOCKS[g])
                    for i in range(4):
                        copy_tile(i, qTp[:, 4 * q + i, 0:n], n)
                elif k == "PS":
                    _, l, g, b = s
                    for i in range(2):
                        copy_tile(4 + i, xb[:, BLOCKS[g][b], i * 512:(i + 1) * 512])
                elif k == "PG":
                    next_of(tops)
                    f(topc.rearrange("p h k -> p (h k)"), topc.rearrange("p h k -> p (h k)"), ACT.Exp).then_inc(top_exp, 1)
                elif k == "AQKV":
                    _, g, third = s
                    nb = len(BLOCKS[g])
                    for j in range(2):
                        for b in range(nb):
                            c = (2 * third + j) * WC
                            copy_tile(j * nb + b, qkv[:, b, c:c + WC], WC)
                elif k == "AN":
                    _, g, b = s
                    next_of(mean_sq)
                    f(sd[:], ms[:], ACT.Sqrt).then_inc(root, 1)
                    if g == "P":
                        next_of(kv_done)
                        store(O["new_k"][0, 0].rearrange("v t n -> t v n"),
                              qkv[:, 0, AH * HD:(AH + AKV) * HD].rearrange("p (v n) -> p v n", n=HD))
                        store(O["new_v"][0, 0].rearrange("v t n -> t v n"),
                              qkv[:, 0, (AH + AKV) * HD:].rearrange("p (v n) -> p v n", n=HD))
                elif k == "AC":
                    for a in range(2):
                        act.dma_start(kdup[:, :, a, :], A["cache_attn_k"][0, 0].rearrange("v t n -> t v n")).then_inc(cache_in, 16)
                    act.dma_start(vc, A["cache_attn_v"][0, 0].rearrange("v t n -> t v n")).then_inc(cache_in, 16)
                    copy_tile(0, kTa[:, :, 0:P], 512, lambda t: t.rearrange("p (v n) -> p v n", n=P))
                elif k == "AT":
                    _, g, b = s
                    for i in range(2):
                        copy_tile(i, qTa[:, 4 * i:4 * i + 4, tok(b)], 512, lambda t: t.rearrange("p (q n) -> p q n", n=P))
                    copy_tile(2, kTa[:, :, tok(b + (g == "S"))], 512, lambda t: t.rearrange("p (v n) -> p v n", n=P))
                elif k == "AS":
                    _, g, b, kv = s
                    n = P if g == "P" else 3 * P
                    for i in range(4):
                        next_of(row_max)
                        t = full_tile(i)
                        f(prA[i][:, 0:n], t[:, 0:n], ACT.Exp, bias=nsmx[:, i:i + 1], scale=ASCALE,
                                   accum_out=rsum[:, i:i + 1]).then_inc(freed["A"], 1)
                elif k in ("FIN", "YOUT"):
                    if k == "YOUT":
                        rsqrt_parts(x[:, s[1], :])
                    for i in range(2):
                        copy_tile(i, gbc[:, i * 512:(i + 1) * 512])
                    if k == "YOUT":
                        next_of(y_done)
                        b = s[1]
                        store(O["y_prompt"][0] if b == 0 else O["y_sample"][0, tok(b - 1), :], x[:, b, :])
            act.wait_ge(stored, 16 * sent["stored"])
            act.wait_ge(state_out, 16 * sent["state_out"])

        @block.vector
        def _(dve):
            begin, open_tile, full_tile, emptied, next_of, note, settle, link = places(dve, dve_chain)
            V = nc.vector

            def bc(ap, n):
                return ap.unsqueeze(len(ap.shape)).to_broadcast([*ap.shape, n])

            def rsqrt(n, width):
                V.tensor_scalar(ms[:, 0:n], ssq[:, 0:n], 1.0 / width, EPS, ALU.mult, ALU.add).then_inc(mean_sq, 1)
                next_of(root)
                link(V.reciprocal(rstd[:, 0:n], sd[:, 0:n]))

            def top16(vals, idx, src):
                link(V.max(vals[:, 0:8], src))
                link(V.max_index(idx[:, 0:8], vals[:, 0:8], src))
                link(V.match_replace(src, vals[:, 0:8], src, NEG))
                link(V.max(vals[:, 8:16], src))
                return V.max_index(idx[:, 8:16], vals[:, 8:16], src)

            def group(b):
                def body(n, slot, ring, first, turn):
                    for j in range(GS):
                        r = ring * GS + j
                        dve.wait_ge(rows_in[r], turn * 16 + 16)
                        last = V.tensor_tensor_reduce(out=rows[:, r, 0:D], in0=rows[:, r, 0:D], in1=xb[:, b, :],
                                                      scale=1.0, scalar=0.0, op0=ALU.mult, op1=ALU.add,
                                                      accum_out=act_in[:, ring, j:j + 1])
                    last.then_inc(dots, 1)
                    dve.wait_ge(gelus, n + 1)
                    g = gate[:, b, slot:slot + GS] if isinstance(slot, int) else gate[:, b, bass.ds(slot, GS)]
                    V.tensor_tensor(wv[:, ring, :], act_out[:, ring, :], g, ALU.mult).then_inc(weighted, 1)
                return body

            dve.wait_ge(inputs_in, 48)
            for s in PLAN:
                k = s[0]
                if k == "GROUPS":
                    if s[3] == 0:
                        dve.wait_ge(experts_chosen, GORDER.index((s[1], s[2])) + 1)
                    run_groups(dve, s, group(s[2]))
                    continue
                begin(s)
                settle()
                if k == "MOD":
                    _, l, q = s
                    for j in range(8):
                        t = full_tile(j)
                        n = slice(16 * q + 2 * j, 16 * q + 2 * j + 2)
                        V.tensor_tensor(modT[:, l, n, :], t[:, 0:4].rearrange("p (n c) -> p n c", c=2),
                                              bc(ada_b[:, l, n], 2), ALU.add).then_inc(freed["D"], 1)
                    emptied(7)
                    if q != 1:
                        w = q // 2
                        at_ = 8 if q == 0 else 32
                        link(V.tensor_scalar(gain[:, l, w], modT[:, l, at_:at_ + 8, :], 1.0, None, ALU.add))
                        V.tensor_tensor(gain[:, l, w], gain[:, l, w], bc(norm_g[:, l, w], 2), ALU.mult).then_inc(dve_step, 1)
                elif k == "NORM":
                    _, l, w, b = s
                    c = COND[b]
                    next_of(squares)
                    rsqrt(1, D)
                    V.tensor_scalar(xn, x[:, b, :], rstd[:, 0:1], None, ALU.mult).then_inc(normed, 1)
                    t = full_tile(1)
                    place = tok(b - (b > 0))
                    for q in range(4):
                        last = V.tensor_scalar(hT[:, 4 + q, place], t[:, q * P:(q + 1) * P], gain[:, l, w, 4 + q, c:c + 1],
                                               modT[:, l, 24 * w + 4 + q, c:c + 1], ALU.mult, ALU.add)
                    last.then_inc(freed["D"], 1)
                elif k == "MLQK":
                    _, g, half = s
                    n = P * len(BLOCKS[g])
                    note(V.memset(raw[:, 4 * half:4 * half + 4, 0:1], 0.0))
                    note(V.memset(raw[:, 4 * half:4 * half + 4, n + 1:n + 2], 0.0))
                    settle()
                    for i in range(4):
                        e = 4 * half + i
                        emptied(i)
                        link(V.tensor_scalar(cv[:, e, 0:n], raw[:, e, 0:n], conv_w[:, e, 0:1], None, ALU.mult))
                        for j in (1, 2):
                            last = V.scalar_tensor_tensor(cv[:, e, 0:n], raw[:, e, j:j + n], conv_w[:, e, j:j + 1],
                                                          cv[:, e, 0:n], ALU.mult, ALU.add)
                            if j == 1:
                                link(last)
                        last.then_inc(convolved, 1)
                elif k == "MLV":
                    _, g, half = s
                    V.memset(va[:, 0:len(BLOCKS[g]), 2 * half:2 * half + 2, DV], 1.0).then_inc(dve_step, 1)
                elif k == "MLG":
                    g = s[1]
                    nb = len(BLOCKS[g])
                    n = 8 * nb
                    t = full_tile(0)
                    gt = gates_all[:, 0:nb, :]
                    V.tensor_tensor(gt, t[:, 0:16 * nb].rearrange("p (b n) -> p b n", n=16),
                                          cst("gate_b").unsqueeze(1).to_broadcast([P, nb, 16]), ALU.add).then_inc(freed["D"], 1)
                    emptied(0)
                    kinds = gtmp[:, 0, 0:16 * nb].rearrange("p (e k h) -> p e k h", k=2, h=MH)
                    fg, inp = kinds[:, :, 1, :], kinds[:, :, 0, :]
                    part = [gtmp[:, i, 0:n].rearrange("p (e h) -> p e h", h=MH) for i in range(4)]
                    flat = [v[:, 0:nb].rearrange("p b d h -> p (b d) h") for v in (ig, nlf)]
                    V.scalar_tensor_tensor(part[1], fg, -1.0, fg, ALU.mult, ALU.max).then_inc(abs_gate, 1)
                    note(V.tensor_copy(flat[0], inp))
                    link(V.tensor_scalar(flat[1], fg, -1.0, 0.0, ALU.mult, ALU.max))
                    next_of(soft_gate)
                    V.tensor_tensor(flat[1], flat[1], part[3], ALU.add).then_inc(log_gate, 1)
                    if g == "P":
                        note(V.memset(mst, 0.0))
                    else:
                        note(V.tensor_copy(mst.rearrange("p d h -> p (d h)"), cst("m0")))
                    t = full_tile(1)
                    V.tensor_copy(bt[:, 0:nb, :], t[:, 0:16 * nb].rearrange("p (b n) -> p b n", n=16)).then_inc(freed["D"], 1)
                    emptied(1)
                    V.tensor_tensor(rcol[:, 0:nb].rearrange("p b d h -> p b (d h)"), ig[:, 0:nb].rearrange("p b d h -> p b (d h)"),
                                        bt[:, 0:nb, 0:8], ALU.add).then_inc(dve_step, 1)
                elif k == "MLA":
                    _, g, d, b = s
                    each = lambda m: m.unsqueeze(1).to_broadcast([P, MH, P])
                    note(V.tensor_tensor(WT, each(tri[:, d, :]), bc(nlf[:, b, d, :], P), ALU.mult))
                    note(V.tensor_tensor(W, each(ident), bc(ig[:, b, d, :], P), ALU.mult))
                    settle()
                    V.tensor_tensor(W, W, WT, ALU.add).then_inc(decay_rows, 1)
                    t = full_tile(0).rearrange("p (h n) -> p h n", n=P)
                    note(V.tensor_reduce(rall, t, AX.X, ALU.max))
                    V.tensor_tensor(W, t, each(mask[:, d, :]), ALU.add).then_inc(freed["D"], 1)
                    emptied(0)
                    link(V.tensor_reduce(rmx, W, AX.X, ALU.max))
                    link(V.tensor_tensor(rmx, rmx, mst[:, d, :], ALU.max))
                    note(V.tensor_tensor(t12[:, 0:4], mst[:, d, :], rmx, ALU.subtract))
                    note(V.tensor_scalar(nMp, rmx, -1.0, None, ALU.mult))
                    settle()
                    V.tensor_tensor(t12[:, 4:8], bt[:, b, 4 * d:4 * d + 4], nMp, ALU.add).then_inc(maxima, 1)
                    t = full_tile(1)
                    next_of(probs_raw)
                    Wf = W.rearrange("p h n -> p (h n)")
                    V.scalar_tensor_tensor(Wf, t[:], KSCALE, Wf, ALU.mult, ALU.mult).then_inc(freed["D"], 1)
                elif k == "MLB":
                    _, g, d, b = s
                    for h in range(MH):
                        if g == "S":
                            emptied(2 * h)
                            t = full_tile(2 * h + 1)
                            V.tensor_tensor(Nn[:, h, :], t[:, 0:DV + 1], Nn[:, h, :], ALU.add).then_inc(freed["D"], 1)
                            emptied(2 * h + 1)
                        else:
                            t = full_tile(h)
                            V.tensor_copy(Nn[:, h, :], t[:, 0:DV + 1]).then_inc(freed["D"], 1)
                            emptied(h)
                    link(V.tensor_scalar(den, Nn[:, :, DV], -1.0, None, ALU.mult))
                    link(V.tensor_tensor(den, den, Nn[:, :, DV], ALU.max))
                    link(V.tensor_tensor(den, den, ae[:, 4:8], ALU.max))
                    link(V.reciprocal(rden, den))
                    out = hm[:, b, :].rearrange("p (h v) -> p h v", v=DV)
                    if d == 0:
                        V.tensor_tensor(out, Nn[:, :, 0:DV], bc(rden, DV), ALU.mult).then_inc(dve_step, 1)
                    else:
                        link(V.tensor_tensor(Nn[:, :, 0:DV], Nn[:, :, 0:DV], bc(rden, DV), ALU.mult))
                        V.tensor_tensor(out, out, Nn[:, :, 0:DV], ALU.add).then_inc(dve_step, 1)
                elif k == "MLC":
                    _, g, d, b = s
                    link(V.tensor_tensor(mpp, mst[:, d, :], rall, ALU.max))
                    note(V.tensor_tensor(dww[:, 0:4], mst[:, d, :], mpp, ALU.subtract))
                    settle()
                    V.tensor_tensor(dww[:, 4:8], rcol[:, b, d, :], mpp, ALU.subtract).then_inc(carry_in, 1)
                    link(V.tensor_tensor(mst[:, d, :], mpp, bt[:, b, 8 + 4 * d:12 + 4 * d], ALU.subtract))
                    next_of(carry_exp)
                    link(V.tensor_scalar(dw[:, 4:8], dw[:, 4:8], KSCALE, None, ALU.mult))
                    t = full_tile(0)
                    V.tensor_tensor(W, t[:].rearrange("p (h n) -> p h n", n=P), bc(dw[:, 4:8], P), ALU.mult).then_inc(freed["D"], 1)
                    if g == "P" and d == 1:
                        dve.wait_ge(state_out, 48)
                    for h in range(MH):
                        t = full_tile(1 + h)
                        if g == "P":
                            last = V.tensor_copy(Cst[:, h, :], t[:, 0:DV + 1])
                        else:
                            last = V.scalar_tensor_tensor(Cst[:, h, :], Cst[:, h, :], dw[:, h:h + 1], t[:, 0:DV + 1],
                                                          ALU.mult, ALU.add)
                        last.then_inc(freed["D"], 1)
                elif k == "MLN":
                    if s[1] == "P":
                        dve.wait_ge(state_out, 96)
                    for b in range(len(BLOCKS[s[1]])):
                        h4 = hm[:, b, :].rearrange("p (h v) -> p h v", v=DV)
                        link(V.tensor_tensor(Nn[:, :, 0:DV], h4, h4, ALU.mult))
                        link(V.tensor_reduce(ssq[:, 0:MH], Nn[:, :, 0:DV], AX.X, ALU.add))
                        rsqrt(MH, DV)
                        last = V.tensor_tensor(h4, h4, bc(rstd[:, 0:MH], DV), ALU.mult)
                        if b < len(BLOCKS[s[1]]) - 1:
                            link(last)
                    last.then_inc(dve_step, 1)
                elif k == "MLO":
                    _, g, half = s
                    nb = len(BLOCKS[g])
                    for j in range(2):
                        for b in range(nb):
                            i = j * nb + b
                            emptied(i)
                            h1 = hm[:, b, (2 * half + j) * DV:(2 * half + j + 1) * DV]
                            last = V.tensor_tensor(h1, h1, Nflat[:, i * WC:(i + 1) * WC], ALU.mult)
                    last.then_inc(dve_step, 1)
                elif k == "OUT":
                    _, l, g, half = s
                    nb = len(BLOCKS[g])
                    if l == 1 and g == "P" and half == 0:
                        dve.wait_ge(stored, 32)
                    for j in range(2):
                        for b in range(nb):
                            i = j * nb + b
                            c = slice((2 * half + j) * WC, (2 * half + j + 1) * WC)
                            t = full_tile(i)
                            tmp = xn[:, i * WC:(i + 1) * WC]
                            V.tensor_tensor(tmp, t[:, 0:WC], gbc[:, c], ALU.mult).then_inc(freed["D"], 1)
                            emptied(i)
                            xc = x[:, BLOCKS[g][b], c]
                            last = V.tensor_tensor(xc, xc, tmp, ALU.add)
                            if i < 2 * nb - 1:
                                note(last)
                    last.then_inc(dve_step, 1)
                elif k == "PS":
                    for i in range(4):
                        t = full_tile(i)
                        V.tensor_copy(sc[:, 4 * i:4 * i + 4, :], t[:].rearrange("p (e n) -> p e n", n=NKEYS)).then_inc(freed["D"], 1)
                elif k == "PT":
                    q = s[4]
                    for e in range(4 * q, 4 * q + 4):
                        last = top16(top1[:, e, :], i1u[:, e, :], sc[:, e, :])
                        if e < 4 * q + 3:
                            note(last)
                    last.then_inc(dve_step, 1)
                elif k == "PC":
                    q = s[4]
                    h0 = 4 * q
                    t2 = top1.rearrange("p (h a) k -> p h a k", a=2)[:, h0:h0 + 4]
                    c4 = cand.rearrange("p h (i j) -> p h i j", j=TOPK)
                    link(V.tensor_tensor(c4, bc(t2[:, :, 0, :], TOPK),
                                           t2[:, :, 1, :].unsqueeze(2).to_broadcast([P, 4, TOPK, TOPK]), ALU.add))
                    for h in range(4):
                        last = top16(topc[:, h0 + h, :], posu[:, h0 + h, :], cand[:, h, :])
                        if h < 3:
                            note(last)
                    last.then_inc(dve_step, 1)
                elif k == "PG":
                    _, l, g, b = s
                    blk = BLOCKS[g][b]
                    pos = posu.rearrange("p h k -> p (h k)")
                    link(V.tensor_copy(gsum, topc[:, :, 0]))
                    V.tensor_tensor(topc, topc, bc(gsum, TOPK), ALU.subtract).then_inc(tops, 1)
                    note(V.tensor_scalar(piju[:, 0, :], pos, 4, None, ALU.logical_shift_right))
                    note(V.tensor_scalar(piju[:, 1, :], pos, 15, None, ALU.bitwise_and))
                    note(V.tensor_copy(i1f, i1u))
                    settle()
                    link(V.tensor_copy(pij, piju))
                    hot = sc.rearrange("p a b -> p (a b)").rearrange("p (s e) -> p s e", e=TOPK)
                    hot4 = sc.rearrange("p a b -> p (a b)").rearrange("p (h s e) -> p h s e", h=PH, e=TOPK)
                    keys = i1f.rearrange("p (h a) k -> p h a k", a=2)
                    for a in range(2):
                        link(V.tensor_tensor(hot, bc(pij[:, a, :], TOPK),
                                               cst("iota").unsqueeze(1).to_broadcast([P, SLOTS, TOPK]), ALU.is_equal))
                        link(V.tensor_tensor(hot4, hot4, keys[:, :, a, :].unsqueeze(2).to_broadcast([P, PH, TOPK, TOPK]), ALU.mult))
                        link(V.tensor_reduce(e12[:, a, :], hot, AX.X, ALU.add))
                    link(V.scalar_tensor_tensor(e12[:, 0, :], e12[:, 0, :], float(NKEYS), e12[:, 1, :], ALU.mult, ALU.add))
                    link(V.tensor_scalar(e12[:, 0, :], e12[:, 0, :], float(l * EXPERTS), None, ALU.add))
                    next_of(top_exp)
                    link(V.tensor_reduce(gsum, topc, AX.X, ALU.add))
                    link(V.reciprocal(grec, gsum))
                    link(V.tensor_tensor(gate[:, blk, :].rearrange("p (h k) -> p h k", k=TOPK), topc, bc(grec, TOPK), ALU.mult))
                    V.tensor_copy(eidx[:, blk, :], e12[:, 0, :]).then_inc(experts_chosen, 1)
                    next_of(experts_chosen)
                    V.tensor_copy(gsum, grec).then_inc(dve_step, 1)
                elif k == "AN":
                    _, g, b = s
                    heads = AH + AKV
                    w = qkv[:, b, 0:heads * HD]
                    w3 = w.rearrange("p (h n) -> p h n", n=HD)
                    link(V.tensor_tensor(sq20, w, w, ALU.mult))
                    link(V.tensor_reduce(ssq, sq20.rearrange("p (h n) -> p h n", n=HD), AX.X, ALU.add))
                    rsqrt(heads, HD)
                    link(V.tensor_tensor(w3, w3, bc(rstd, HD), ALU.mult))
                    note(V.tensor_tensor(w3[:, 0:AH], w3[:, 0:AH], cst("q_g").unsqueeze(1).to_broadcast([P, AH, HD]), ALU.mult))
                    settle()
                    last = V.tensor_tensor(w3[:, AH:], w3[:, AH:], cst("k_g").unsqueeze(1).to_broadcast([P, AKV, HD]), ALU.mult)
                    if g == "P":
                        last.then_inc(kv_done, 1)
                        next_of(kv_done)
                        V.tensor_copy(ssq, rstd).then_inc(dve_step, 1)
                    else:
                        link(last)
                        wr = w.rearrange("p (h a r n) -> p h a r n", a=2, r=2, n=16)
                        t = sq20.rearrange("p (r h a n) -> p r h a n", r=2, a=2, n=16)
                        for a in range(2):
                            x1, x2 = wr[:, :, a, 0, :], wr[:, :, a, 1, :]
                            t1, t2 = t[:, 0, :, a, :], t[:, 1, :, a, :]
                            o = b * 32 + a * 16
                            cc = cst("cos")[:, o:o + 16].unsqueeze(1).to_broadcast([P, heads, 16])
                            ss = cst("sin")[:, o:o + 16].unsqueeze(1).to_broadcast([P, heads, 16])
                            note(V.tensor_tensor(t1, x1, ss, ALU.mult))
                            note(V.tensor_tensor(t2, x2, ss, ALU.mult))
                            settle()
                            note(V.tensor_tensor(x1, x1, cc, ALU.mult))
                            note(V.tensor_tensor(x2, x2, cc, ALU.mult))
                            settle()
                            note(V.tensor_tensor(x1, x1, t2, ALU.subtract))
                            last = V.tensor_tensor(x2, x2, t1, ALU.add)
                            if a == 0:
                                link(last)
                        last.then_inc(dve_step, 1)
                elif k == "AT":
                    _, g, b = s
                    keys = qkv[:, b, AH * HD:(AH + AKV) * HD].rearrange("p (v n) -> p v n", n=HD)
                    link(V.tensor_copy(kdup[:, :, 0, :], keys))
                    V.tensor_copy(kdup[:, :, 1, :], keys).then_inc(key_pairs, 1)
                elif k == "AS":
                    _, g, b, kv = s
                    n = P if g == "P" else 3 * P
                    for i in range(4):
                        t = full_tile(i)
                        link(V.tensor_reduce(smx[:, i:i + 1], t[:, 0:n], AX.X, ALU.max))
                        V.tensor_scalar(nsmx[:, i:i + 1], smx[:, i:i + 1], -ASCALE, None, ALU.mult).then_inc(row_max, 1)
                    for i in range(4):
                        t = full_tile(4 + i)
                        V.tensor_copy(pTa[i % 2][:, 0:n], t[:, 0:n]).then_inc(freed["D"], 1)
                    link(V.reciprocal(rrs, rsum))
                    t = full_tile(8)
                    o = qkv[:, b, kv * 4 * HD:(kv * 4 + 4) * HD].rearrange("p (h n) -> p h n", n=HD)
                    V.tensor_tensor(o, t[:, 0:4 * HD].rearrange("p (h n) -> p h n", n=HD), bc(rrs, HD), ALU.mult).then_inc(freed["D"], 1)
                elif k == "FIN":
                    _, l, b = s
                    dve.wait_ge(summed, (GORDER.index((l, b)) + 1) * GROUPS)
                    emptied(1)
                    V.tensor_tensor(xn, acc[:], gbc, ALU.mult).then_inc(sum_read, 1)
                    next_of(sum_read)
                    V.tensor_tensor(x[:, b, :], x[:, b, :], xn, ALU.add).then_inc(dve_step, 1)
                elif k == "YOUT":
                    b = s[1]
                    next_of(squares)
                    rsqrt(1, D)
                    link(V.tensor_scalar(x[:, b, :], x[:, b, :], rstd[:, 0:1], None, ALU.mult))
                    emptied(1)
                    V.tensor_tensor(x[:, b, :], x[:, b, :], gbc, ALU.mult).then_inc(y_done, 1)
                    next_of(y_done)
                    V.tensor_copy(ssq[:, 0:1], rstd[:, 0:1]).then_inc(dve_step, 1)


_OUTS = [("y_prompt", (1, 128, 1024)), ("y_sample", (1, 256, 1024)), ("new_C", (1, 1, 2, 4, 128, 256)),
         ("new_n", (1, 1, 2, 4, 128)), ("new_m", (1, 1, 2, 4)), ("new_k", (1, 1, 4, 128, 64)), ("new_v", (1, 1, 4, 128, 64))]


def small_inputs(v):
    f = np.float32
    s = np.arange(P)

    def by_feature(a):
        return np.ascontiguousarray(a).reshape(-1, P).T

    def everywhere(a):
        return np.broadcast_to(np.ascontiguousarray(a).reshape(1, -1), (P, a.size))

    half = HD // 4
    inv = 10000.0 ** (-np.arange(half, dtype=f) / half)
    t = np.arange(2 * P)
    ang = np.concatenate([(t // 64).astype(f)[:, None] * inv, (t % 64).astype(f)[:, None] * inv], -1).astype(f)
    rope = lambda a: a.astype(f).reshape(2, P, 32).transpose(1, 0, 2).reshape(P, 64)
    upto, since = s[:, None] <= s[None, :], s[:, None] >= s[None, :]
    parts = {
        "ident": np.eye(P, dtype=f), "ones": np.ones((P, P), f),
        "tri": np.concatenate([upto, since], 1).astype(f),
        "mask": np.where(np.concatenate([since, upto], 1), 0.0, NEG).astype(f),
        "iota": everywhere(np.arange(TOPK, dtype=f)), "cos": rope(np.cos(ang)), "sin": rope(np.sin(ang)),
        "cond": np.stack([v["c_ctx"].reshape(P, KC), v["c"].reshape(P, KC)], -1).reshape(P, 2 * KC),
        "ada_b": by_feature(v["ada_b"]), "norm_g": by_feature(v["norm_g"]), "final_g": by_feature(v["final_g"]),
        "head_g": by_feature(v["mlstm_head_g"]),
        "conv_w": v["mlstm_conv_w"][0].reshape(3, KC, P).transpose(2, 1, 0).reshape(P, 3 * KC),
        "conv_b": by_feature(v["mlstm_conv_b"]), "gate_b": everywhere(v["mlstm_gate_b"]),
        "q_g": everywhere(v["attn_q_g"]), "k_g": everywhere(v["attn_k_g"]), "m0": everywhere(v["state_mlstm_m"]),
        "w_gate": v["mlstm_w_in"][0, :, 3072:].reshape(KC, P, 16).transpose(1, 0, 2).reshape(P, KC * 16),
    }
    return np.ascontiguousarray(np.concatenate([parts[n] for n in SMALL], 1))


def kernel(**inputs):
    import concourse.bacc as _bacc
    from concourse.bass_utils import run_bass_kernel_spmd as _run

    v = {k: np.asarray(a) for k, a in inputs.items()}
    arrays = {n: np.ascontiguousarray(v[n]) for n in (
        "x_prompt", "x_sample", "state_mlstm_C", "state_mlstm_n", "cache_attn_k", "cache_attn_v", "ada_w",
        "mlstm_w_in", "mlstm_w_out", "attn_w_qkv", "attn_w_out", "peer_w_q")}
    arrays["uv"] = np.concatenate([v["peer_u"], v["peer_v"]], -1).reshape(DEPTH * EXPERTS, 2 * D)
    arrays["subkeys"] = np.ascontiguousarray(v["peer_subkeys"].transpose(0, 4, 1, 2, 3)).reshape(DEPTH, P, NSETS * NKEYS)
    arrays["small"] = small_inputs(v)
    nc = _bacc.Bacc("TRN2", target_bir_lowering=False, num_devices=1)
    A = {n: nc.dram_tensor(f"in_{n}", a.shape, mybir.dt.from_np(a.dtype), kind="ExternalInput").ap() for n, a in arrays.items()}
    O = {n: nc.dram_tensor(f"out_{n}", shape, F32, kind="ExternalOutput").ap() for n, shape in _OUTS}
    trunk(nc, A, O)
    r = _run(nc, [{f"in_{n}": a for n, a in arrays.items()}], core_ids=[0])
    return tuple(r.results[0][f"out_{n}"] for n, _ in _OUTS)
```

```python
import concourse.bass as bass
from concourse import mybir
from contextlib import ExitStack
import numpy as np

F32 = mybir.dt.float32
U32 = mybir.dt.uint32
ALU = mybir.AluOpType
ACT = mybir.ActivationFunctionType
AX = mybir.AxisListType

P = 128
D = 1024
KC = D // P
EPS = 1e-6
DEPTH = 2
MH, DQK, DV = 4, 128, 256
KSCALE = DQK ** -0.5
AH, AKV, HD = 16, 4, 64
ASCALE = HD ** -0.5
QKV = (AH + 2 * AKV) * HD
PH, NKEYS, TOPK = 8, 128, 16
NSETS = 2 * PH
EXPERTS = NKEYS * NKEYS
SLOTS = PH * TOPK
GS = 2
GROUPS = SLOTS // GS
SIDE_EVERY, SIDE = 2, 1
RING = 6
WC = 256
WRING = 3
BANKS = 6
NEG = -1.0e30

BLOCKS = {"P": [0], "S": [1, 2]}
COND = [0, 1, 1]

SMALL, _at = {}, 0
for _name, _n in [("ident", P), ("ones", P), ("tri", 2 * P), ("mask", 2 * P), ("iota", TOPK), ("pick", 2),
                  ("cos", 2 * 32), ("sin", 2 * 32), ("cond", 2 * KC), ("ada_b", DEPTH * 48),
                  ("norm_g", DEPTH * 2 * KC), ("final_g", KC), ("head_g", KC), ("conv_w", 3 * KC),
                  ("conv_b", KC), ("gate_b", 16), ("q_g", HD), ("k_g", HD), ("m0", 8), ("w_gate", KC * 16)]:
    SMALL[_name] = (_at, _n)
    _at += _n
NSMALL = _at


def plan():
    def mlstm(g):
        nb = len(BLOCKS[g])
        yield from (("NORM", 0, 0, b) for b in BLOCKS[g])
        yield from (("MLQK", g, h) for h in range(2))
        yield from (("MLV", g, h) for h in range(2))
        yield ("MLG", g)
        for d in range(2):
            order = list(range(nb))[::1 - 2 * d]
            for n, b in enumerate(order):
                yield ("MLA", g, d, b)
                yield ("MLB", g, d, b)
                if g == "P" or n < nb - 1:
                    yield ("MLC", g, d, b)
        yield ("MLN", g)
        yield from (("MLO", g, h) for h in range(2))
        yield ("T2", 0, g)
        yield from (("OUT", 0, g, h) for h in range(2))

    def attention(g):
        nb = len(BLOCKS[g])
        yield from (("NORM", 1, 0, b) for b in BLOCKS[g])
        yield from (("AQKV", g, h) for h in range(3))
        if g == "S":
            yield ("AC", g)
        yield from (("AN", g, b) for b in range(nb))
        yield from (("AT", g, b) for b in range(nb))
        yield from (("AS", g, b, kv) for b in range(nb) for kv in range(AKV))
        yield ("T2", 1, g)
        yield from (("OUT", 1, g, h) for h in range(2))

    def queries(l, g):
        yield from (("NORM", l, 1, b) for b in BLOCKS[g])
        yield from (("PQ", l, g, q) for q in range(4))

    def choice(l, g, b, half):
        if half == 0:
            yield ("PS", l, g, b)
        yield from (("PT", l, g, b, q) for q in (2 * half, 2 * half + 1))
        yield ("PC", l, g, b, half)
        yield ("PG", l, g, b, half)

    def cost(s):
        both = "S" in s
        return {"MLQK": 13, "MLV": 13, "MLO": 13, "OUT": 13, "PQ": 13, "AQKV": 13, "AS": 11, "MOD": 10}.get(s[0], 0) / (2 - both) \
            or {"MLA": 8, "MLG": 8, "MLN": 10, "PS": 5, "PC": 8, "PG": 9, "PT": 5, "AN": 12}.get(s[0], 6)

    def spread(l, b, steps):
        steps = list(steps)
        total = sum(cost(s) for s in steps)
        done = spent = 0
        for s in steps:
            upto = int((GROUPS - 4) * spent / total)
            if upto > done:
                yield ("GROUPS", l, b, done, upto)
                done = upto
            yield s
            spent += cost(s)
        yield ("GROUPS", l, b, done, GROUPS)
        yield ("FIN", l, b)

    yield ("INIT",)
    yield from (("MOD", 0, q) for q in range(2))
    context = list(mlstm("P"))
    for s in context:
        if s == ("MLB", "P", 0, 0):
            yield ("MOD", 0, 2)
        if s == ("MLC", "P", 0, 0):
            yield ("MOD", 0, 3)
        if s == ("MLB", "P", 1, 0):
            yield ("MOD", 0, 4)
        if s == ("MLC", "P", 1, 0):
            yield ("MOD", 0, 5)
        yield s
    yield from queries(0, "P")
    yield from choice(0, "P", 0, 0)
    yield from spread(0, 0, [*choice(0, "P", 0, 1), *mlstm("S"), *queries(0, "S"), *choice(0, "S", 0, 0)])
    yield from spread(0, 1, [*choice(0, "S", 0, 1), *choice(0, "S", 1, 0), *choice(0, "S", 1, 1),
                             *(("MOD", 1, q) for q in range(6))])
    yield from spread(0, 2, [*attention("P"), *queries(1, "P"), *choice(1, "P", 0, 0)])
    yield from spread(1, 0, [*choice(1, "P", 0, 1), *attention("S"), *queries(1, "S"), *choice(1, "S", 0, 0)])
    yield from spread(1, 1, [*choice(1, "S", 0, 1), *choice(1, "S", 1, 0), *choice(1, "S", 1, 1), ("YOUT", 0)])
    yield from spread(1, 2, [("YOUT", 1)])
    yield ("YOUT", 2)


PLAN = list(plan())


def psum_tiles(s):
    k = s[0]
    nb = len(BLOCKS[s[1]]) if len(s) > 1 and s[1] in ("P", "S") else 0
    if k == "MOD":
        return "AADADADD"
    if k == "NORM":
        return "AD"
    if k == "MLQK":
        return "AAAA"
    if k in ("MLV", "MLO", "AQKV"):
        return "A" * (2 * nb)
    if k == "MLG":
        return "DD"
    if k == "MLA":
        return "DDA"
    if k == "MLB":
        return "AD" * MH if s[1] == "S" else "D" * MH
    if k == "MLC":
        return "D" * (1 + MH)
    if k == "T2":
        return "A" * (2 * len(BLOCKS[s[2]]) + 2)
    if k == "OUT":
        return "D" * (2 * len(BLOCKS[s[2]]))
    if k == "PQ":
        return "AAAA"
    if k == "PS":
        return "DDDDAA"
    if k == "AC":
        return "A"
    if k == "AT":
        return "AAA"
    if k == "AS":
        return "AAAADDDDD"
    if k in ("FIN", "YOUT"):
        return "AA"
    return ""


MOD_ROWS, MOD_COLUMNS = (0, 1, 3, 5), (2, 4, 6, 7)


def weight_tiles(s, A):
    k = s[0]

    def cols(w, first, n, per):
        w = w.rearrange("(k p) n -> p k n", p=P)
        return [(w[:, :, (first + j) * WC:(first + j + 1) * WC], per * (j + 1) - 1) for j in range(n)]

    if k == "MOD":
        w = A["ada_w"][s[1]].rearrange("(p k) n -> p k n", p=P)
        return [(w[:, :, (4 * s[2] + j) * WC:(4 * s[2] + j + 1) * WC], MOD_ROWS[j]) for j in range(4)]
    if k == "MLQK":
        return cols(A["mlstm_w_in"][0], 2 * s[2], 2, 2)
    if k == "MLV":
        return cols(A["mlstm_w_in"][0], 4 + 2 * s[2], 2, len(BLOCKS[s[1]]))
    if k == "MLO":
        return cols(A["mlstm_w_in"][0], 8 + 2 * s[2], 2, len(BLOCKS[s[1]]))
    if k == "AQKV":
        return cols(A["attn_w_qkv"][0], 2 * s[2], 2, len(BLOCKS[s[1]]))
    if k == "OUT":
        w = A["mlstm_w_out"] if s[1] == 0 else A["attn_w_out"]
        return cols(w[0], 2 * s[3], 2, len(BLOCKS[s[2]]))
    if k == "PQ":
        return cols(A["peer_w_q"][s[1]], 2 * s[3], 2, 2)
    if k == "PS":
        return [(A["subkeys"][s[1]].rearrange("p (k n) -> p k n", k=KC), 3)]
    return []


ACT_ENDS = ("INIT", "MLQK")
IDLE = {"P": ("INIT", "MLN", "PT", "PC", "PG", "AN"), "A": ("PT", "PC", "OUT"), "D": ("INIT", "PQ", "AQKV", "T2", "AC")}


def dve_ends(s):
    return s[0] in ("MLV", "MLG", "MLB", "MLN", "MLO", "OUT", "PT", "PC", "PG", "AN", "FIN", "YOUT") \
        or (s[0] == "MOD" and s[2] in (1, 4))


def needed(i, who):
    s = PLAN[i]

    def after(*kinds):
        return max(j for j in range(i) if PLAN[j][0] in kinds) + 1

    if s[0] in ("MLQK", "MLV", "MLG", "PQ", "AQKV"):
        return after("NORM")
    if s[0] == "MOD":
        return after("INIT")
    if s[0] == "MLO" and who == "P":
        return after("NORM")
    if s[0] == "OUT" and who == "P":
        return after("T2")
    if s[0] == "PS" and who != "D":
        return after("PQ")
    if s[0] == "AS" and who == "P":
        return after("AT")
    return i


def trunk(nc, A, O):
    ctx = ExitStack()
    with ctx:
        def sb(name, shape, dt=F32):
            return ctx.enter_context(nc.sbuf_tensor(name, shape, dt))

        def sem(name):
            return ctx.enter_context(nc.semaphore(name))

        rows = sb("rows", [P, RING * GS, 2 * D])
        wt = sb("wt", [P, WRING, KC * WC])
        x = sb("x", [P, 3, D])
        xb = sb("xb", [P, 2, D])
        hT = sb("hT", [P, KC, 2 * P])
        small = sb("small", [P, NSMALL])
        diag = sb("diag", [P, RING * GS, P])
        eidx = sb("eidx", [P, 3, SLOTS], U32)
        gate = sb("gate", [P, 3, SLOTS])
        act_in = sb("act_in", [P, RING, GS])
        act_out = sb("act_out", [P, RING, GS])
        wv = sb("wv", [P, RING, GS])
        cs = sb("cs", [P, KC, 32])
        side = sb("side", [P, D])
        modT = sb("modT", [P, DEPTH, 48, 2])
        gain = sb("gain", [P, DEPTH, 2, KC, 2])
        mod_rows = sb("mod_rows", [P, 2, WC])
        st = sb("st", [P, 256])
        ARENA = 8220
        arena = sb("arena", [P, ARENA])

        def cst(name):
            a, n = SMALL[name]
            return small[:, a:a + n]

        ident, ones = cst("ident"), cst("ones")
        tri = cst("tri").rearrange("p (d n) -> p d n", d=2)
        mask = cst("mask").rearrange("p (d n) -> p d n", d=2)
        norm_g = cst("norm_g").rearrange("p (l w k) -> p l w k", l=DEPTH, w=2)
        ada_b = cst("ada_b").rearrange("p (l n) -> p l n", l=DEPTH)
        conv_w = cst("conv_w").rearrange("p (f j) -> p f j", j=3)
        w_gate = cst("w_gate").rearrange("p (k n) -> p k n", k=KC)

        def area(at, *shape):
            n = 1
            for v in shape:
                n *= v
            assert at + n <= ARENA, (at, shape)
            a = arena[:, at:at + n]
            if len(shape) == 2:
                a = a.rearrange("p (a b) -> p a b", b=shape[1])
            if len(shape) == 3:
                a = a.rearrange("p (a b c) -> p a b c", b=shape[1], c=shape[2])
            return a, at + n

        xn, at = area(0, D)
        raw, _ = area(at, KC, 2 * P + 2)
        hm, _ = area(at, 2, D)
        at += KC * (2 * P + 2)
        cv, at = area(at, KC, 2 * P)
        va, at = area(at, 2, MH, DV + 1)
        Cst, at = area(at, MH, DV + 1)
        W = xn[:, 0:512].rearrange("p (h n) -> p h n", n=P)
        WT = xn[:, 512:1024].rearrange("p (h n) -> p h n", n=P)
        Nn = sb("Nn", [P, MH, DV + 1])
        Nflat = Nn[:].rearrange("p a b -> p (a b)")
        gbc = Nflat[:, 0:D]
        qkv, at = area(D, 2, QKV)
        qTa, at = area(at, AH // 2, 2 * P)
        kTa, at = area(at, AKV, 3 * P)
        kdup, at = area(at, AKV, 2, HD)
        vc = xn[:, 3 * 2 * P:D].rearrange("p (v n) -> p v n", n=HD)
        sq20 = area(D + 2 * QKV, 20 * HD)[0]
        prA = [hT[:].rearrange("p a b -> p (a b)")[:, i * 3 * P:(i + 1) * 3 * P] for i in range(4)]
        pTa = [xn[:, i * 3 * P:(i + 1) * 3 * P] for i in range(2)]
        qTp, at = area(D, NSETS, 2 * P)
        sc, at = area(at, NSETS, NKEYS)
        cand, at = area(at, PH // 2, TOPK * TOPK)
        top1 = Nflat[:, 0:256].rearrange("p (s k) -> p s k", k=TOPK)
        i1f = Nflat[:, 256:512].rearrange("p (s k) -> p s k", k=TOPK)
        topc = Nflat[:, 512:640].rearrange("p (s k) -> p s k", k=TOPK)
        pij = Nflat[:, 640:896].rearrange("p (a s) -> p a s", a=2)
        i1u = xn[:, 0:256].bitcast(U32).rearrange("p (s k) -> p s k", k=TOPK)
        posu = xn[:, 256:384].bitcast(U32).rearrange("p (s k) -> p s k", k=TOPK)
        piju = xn[:, 384:640].bitcast(U32).rearrange("p (a s) -> p a s", a=2)
        e12 = xn[:, 640:896].rearrange("p (a s) -> p a s", a=2)

        def cols(a, n):
            return st[:, a:a + n]
        ssq, ms, sd, rstd = (cols(i * 20, 20) for i in range(4))
        ig = cols(80, 16).rearrange("p (b d h) -> p b d h", b=2, d=2)
        nlf = cols(96, 16).rearrange("p (b d h) -> p b d h", b=2, d=2)
        bt = cols(112, 32).rearrange("p (b n) -> p b n", b=2)
        rcol = cols(144, 16).rearrange("p (b d h) -> p b d h", b=2, d=2)
        mst = cols(160, 8).rearrange("p (d h) -> p d h", d=2)
        rall, rmx, nMp = cols(168, 4), cols(172, 4), cols(176, 4)
        t12, ae = cols(180, 8), cols(188, 8)
        dww, dw = cols(196, 8), cols(204, 8)
        den, rden = cols(212, 4), cols(216, 4)
        mpp = cols(220, 4)
        smx, nsmx, rsum, rrs = cols(224, 4), cols(228, 4), cols(232, 4), cols(236, 4)
        gsum, grec = cols(240, 8), cols(248, 8)
        gtmp = xn[:, 0:128].rearrange("p (a n) -> p a n", a=4)
        gates_all = gtmp[:, 0].rearrange("p (b n) -> p b n", b=2)

        acc = ctx.enter_context(nc.psum_tensor("acc", [P, D], F32))
        banks = [ctx.enter_context(nc.psum_tensor(f"bank{i}", [P, 512], F32)) for i in range(BANKS)]

        inputs_in = sem("inputs_in")
        w_in = [sem(f"weights_in{i}") for i in range(WRING)]
        rows_in = [sem(f"rows_in{i}") for i in range(RING * GS)]
        tile_full = sem("tile_full")
        act_freed, dve_freed = sem("act_emptied_tile"), sem("dve_emptied_tile")
        freed = {"A": act_freed, "D": dve_freed}
        act_step, dve_step = sem("act_step"), sem("dve_step")
        act_chain, dve_chain = sem("act_chain"), sem("dve_chain")
        zeroed = sem("zeroed")
        squares, mean_sq, root, normed = sem("squares"), sem("mean_sq"), sem("root"), sem("normed")
        convolved, abs_gate, soft_gate, log_gate = sem("convolved"), sem("abs_gate"), sem("soft_gate"), sem("log_gate")
        decay_rows, maxima, probs_raw = sem("decay_rows"), sem("maxima"), sem("probs_raw")
        carry_in, carry_exp, state_in, state_out = sem("carry_in"), sem("carry_exp"), sem("state_in"), sem("state_out")
        key_pairs, cache_in, row_max, kv_done = sem("key_pairs"), sem("cache_in"), sem("row_max"), sem("kv_done")
        tops, top_exp, experts_chosen = sem("tops"), sem("top_exp"), sem("experts_chosen")
        dots, gelus, weighted, diags, summed = sem("dots"), sem("gelus"), sem("weighted"), sem("diags"), sem("summed")
        side_summed, side_zero = sem("side_summed"), sem("side_zero")
        sum_read, y_done, stored = sem("sum_read"), sem("y_done"), sem("stored")

        def places(who):
            owner, seen = [], {}
            count = {"A": 0, "D": 0}
            place = {"first": 0, "acts": 0, "dves": 0, "chain": 0}
            before = []

            def begin(i):
                s = PLAN[i]
                place["first"] = len(owner)
                before.append((len(owner), count["A"], count["D"], place["acts"], place["dves"]))
                if s[0] == "GROUPS":
                    return 0, 0, 0, 0, 0
                for e in psum_tiles(s):
                    count[e] += 1
                    owner.append((e, count[e]))
                place["acts"] += s[0] in ACT_ENDS
                place["dves"] += dve_ends(s)
                return (0, 0, 0, 0, 0) if s[0] in IDLE[who] else before[needed(i, who)]

            def tile(j):
                return banks[(place["first"] + j) % BANKS]

            def full(j):
                return place["first"] + j + 1

            def by(j):
                return freed[owner[place["first"] + j][0]]

            def emptied(j):
                return owner[place["first"] + j][1]

            def next_of(sem, k=1):
                key = id(sem)
                seen[key] = seen.get(key, 0) + k
                return seen[key]

            def one():
                place["chain"] += 1
                return 1

            def noted():
                return place["chain"]

            return begin, tile, full, by, emptied, next_of, one, noted

        def tok(b):
            return slice(b * P, (b + 1) * P)

        GORDER = [(0, 0), (0, 1), (0, 2), (1, 0), (1, 1), (1, 2)]

        def run_groups(eng, s, body, last_ones):
            _, l, b, lo, hi = s
            base = GORDER.index((l, b)) * GROUPS

            def straight(g0, g1):
                for g in range(g0, g1):
                    n = base + g
                    body(n, g * GS, n % RING, n // RING, g)

            g = lo
            if g < 3:
                straight(g, min(3, hi))
                g = min(3, hi)
            whole = (hi - g) // RING
            if whole >= 2:
                with eng.Fori(0, whole) as i:
                    for k in range(RING):
                        n = base + g + k
                        body(i * RING + n, i * (RING * GS) + (g + k) * GS, n % RING, i + n // RING, None)
                g += whole * RING
            straight(g, hi)
            if hi == GROUPS:
                last_ones(base + GROUPS)

        block = ctx.enter_context(nc.Block())

        @block.sync
        def _(sp):
            sp.dma_start(small[:], A["small"]).then_inc(inputs_in, 16)
            sp.dma_start(x[:, 0, :], A["x_prompt"][0]).then_inc(inputs_in, 16)
            sp.dma_start(x[:, 1:3, :], A["x_sample"][0].rearrange("(b p) n -> p b n", p=P)).then_inc(inputs_in, 16)
            tiles, free_at, n = 0, [], 0
            for s in PLAN:
                for src, last in weight_tiles(s, A):
                    if n >= WRING:
                        sp.wait_ge(tile_full, free_at[n - WRING])
                    sp.dma_start(wt[:, n % WRING, :].rearrange("p (k n) -> p k n", k=KC), src)\
                        .then_inc(w_in[n % WRING], 16)
                    free_at.append(tiles + last + 1)
                    n += 1
                tiles += len(psum_tiles(s))

        @block.gpsimd
        def _(pool):
            for n, (l, b) in enumerate(GORDER):
                for g in range(n * GROUPS, (n + 1) * GROUPS):
                    if g % (GROUPS // 2) == 0:
                        pool.wait_ge(experts_chosen, g // (GROUPS // 2) + 1)
                    if g >= RING:
                        pool.wait_ge(summed, g - RING + 1)
                        if g - RING >= SIDE:
                            pool.wait_ge(side_summed, (g - RING - SIDE) // SIDE_EVERY + 1)
                    for j in range(GS):
                        r = (g % RING) * GS + j
                        slot = (g - n * GROUPS) * GS + j
                        nc.gpsimd.indirect_dma_start(
                            out=rows[:, r, :], out_offset=None, in_=A["uv"],
                            in_offset=bass.IndirectOffsetOnAxis(ap=eidx[:, b, slot:slot + 1], axis=0))\
                            .then_inc(rows_in[r], 16)

        @block.tensor
        def _(pe):
            begin, tile, full, by, emptied, next_of, one, noted = places("P")
            used = [0]

            def open_tile(j):
                if full(j) > BANKS:
                    pe.wait_ge(by(j - BANKS), emptied(j - BANKS))
                return tile(j)

            def mm(out, lhsT, rhs, start, stop):
                return nc.tensor.matmul(out, lhsT, rhs, start=start, stop=stop)

            def weights():
                n = used[0]
                used[0] += 1
                pe.wait_ge(w_in[n % WRING], 16 * (n // WRING + 1))
                return wt[:, n % WRING, :].rearrange("p (k n) -> p k n", k=KC)

            def product(out, lhs, rhs):
                for k in range(KC):
                    last = mm(out, lhs(k), rhs(k), k == 0, k == KC - 1)
                return last

            def transposes(out, ins):
                for i, a in enumerate(ins):
                    last = nc.tensor.transpose(out[:, i * P:(i + 1) * P], a, ident)
                return last

            def by_token(n_tiles, blocks):
                for j in range(n_tiles):
                    w = weights()
                    for b in range(blocks):
                        t = open_tile(j * blocks + b)
                        product(t[:, 0:WC], lambda k: hT[:, k, tok(b)], lambda k: w[:, k, :]).then_inc(tile_full, 1)

            def by_feature(n_tokens):
                for j in range(2):
                    w = weights()
                    for i in range(2):
                        t = open_tile(2 * j + i)
                        product(t[:, 0:n_tokens], lambda k: w[:, k, i * P:(i + 1) * P],
                                lambda k: hT[:, k, 0:n_tokens]).then_inc(tile_full, 1)

            def on_all_partitions(j, column):
                for i in range(2):
                    t = open_tile(j + i)
                    for k in range(4):
                        last = mm(t[:, k * P:(k + 1) * P], column(4 * i + k).to_broadcast([P, P]), ident, True, True)
                    last.then_inc(tile_full, 1)

            def add_up(n, ring, first):
                pe.wait_ge(diags, n + 1)
                for j in range(GS - (ring % SIDE_EVERY == SIDE)):
                    r = ring * GS + j
                    for h in range(2):
                        last = nc.tensor.matmul(acc[:, h * 512:(h + 1) * 512], diag[:, r, :],
                                                rows[:, r, D + h * 512:D + (h + 1) * 512],
                                                start=first and j == 0, stop=True, skip_group_check=True)
                last.then_inc(summed, 1)

            def group(n, slot, ring, turn, g):
                if g == 2 and n >= GROUPS:
                    pe.wait_ge(sum_read, n // GROUPS)
                if g is None or g >= 2:
                    add_up(n - 2, (ring - 2) % RING, g == 2)

            def last_groups(n):
                add_up(n - 2, (n - 2) % RING, False)
                add_up(n - 1, (n - 1) % RING, False)

            pe.wait_ge(inputs_in, 48)
            for n_entry, s in enumerate(PLAN):
                k = s[0]
                tiles, by_act, by_dve, acts, dves = begin(n_entry)
                if by_act:
                    pe.wait_ge(act_freed, by_act)
                if by_dve:
                    pe.wait_ge(dve_freed, by_dve)
                if acts:
                    pe.wait_ge(act_step, acts)
                if dves:
                    pe.wait_ge(dve_step, dves)
                if k == "GROUPS":
                    run_groups(pe, s, group, last_groups)
                    continue
                if k == "MOD":
                    for j in range(5):
                        if j < 4:
                            w = weights()
                            t = open_tile(MOD_ROWS[j])
                            for q in range(KC):
                                c = slice(32 * (q % 4), 32 * (q % 4) + 32)
                                last = mm(t[c, 0:WC], cs[:, q, :], w[:, q, :], q < 4, q >= 4)
                            last.then_inc(tile_full, 1)
                        if j:
                            t = open_tile(MOD_COLUMNS[j - 1])
                            pe.wait_ge(by(MOD_ROWS[j - 1]), emptied(MOD_ROWS[j - 1]))
                            for i in range(2):
                                last = mm(t[:, 2 * i:2 * i + 2], mod_rows[:, (j - 1) % 2, i * P:(i + 1) * P], cst("pick"), True, True)
                            last.then_inc(tile_full, 1)
                elif k == "NORM":
                    pe.wait_ge(normed, next_of(normed))
                    for i in range(2):
                        transposes(open_tile(i), [xn[:, (4 * i + q) * P:(4 * i + q + 1) * P] for q in range(4)])\
                            .then_inc(tile_full, 1)
                elif k == "MLQK":
                    by_feature(P * len(BLOCKS[s[1]]))
                elif k in ("MLV", "MLO", "AQKV"):
                    by_token(2, len(BLOCKS[s[1]]))
                elif k == "OUT":
                    by_token(2, len(BLOCKS[s[2]]))
                elif k == "MLG":
                    nb = len(BLOCKS[s[1]])
                    t = open_tile(0)
                    for b in range(nb):
                        last = product(t[:, b * 16:b * 16 + 16], lambda q: hT[:, q, tok(b)], lambda q: w_gate[:, q, :])
                    last.then_inc(tile_full, 1)
                    pe.wait_ge(log_gate, next_of(log_gate))
                    t = open_tile(1)
                    for b in range(nb):
                        for d in range(2):
                            mm(t[:, b * 16 + d * 4:b * 16 + d * 4 + 4], tri[:, d, :], nlf[:, b, d, :], True, True)
                        last = mm(t[:, b * 16 + 8:b * 16 + 16], ones, nlf[:, b].rearrange("p d h -> p (d h)"), True, True)
                    last.then_inc(tile_full, 1)
                elif k == "MLA":
                    _, g, d, b = s
                    pe.wait_ge(decay_rows, next_of(decay_rows))
                    t = open_tile(0)
                    mm(t[:], ones, W.rearrange("p h n -> p (h n)"), True, True).then_inc(tile_full, 1)
                    t = open_tile(1)
                    for h in range(MH):
                        last = mm(t[:, h * P:(h + 1) * P], cv[:, h, tok(b)], cv[:, 4 + h, tok(b)], True, True)
                    last.then_inc(tile_full, 1)
                    pe.wait_ge(by(1), emptied(1))
                    transposes(open_tile(2), [W[:, h, :] for h in range(MH)]).then_inc(tile_full, 1)
                elif k == "MLB":
                    _, g, d, b = s
                    per = 2 if g == "S" else 1
                    if g == "S" and b == d:
                        pe.wait_ge(state_in, next_of(state_in, 32))
                    for h in range(MH):
                        if g == "S":
                            t = open_tile(per * h)
                            mm(t[:, 0:DV + 1], cv[:, h, tok(b)], Cst[:, h, :], True, True).then_inc(tile_full, 1)
                        t = open_tile(per * h + per - 1)
                        mm(t[:, 0:DV + 1], WT[:, h, :], va[:, b, h, :], True, True).then_inc(tile_full, 1)
                elif k == "MLC":
                    _, g, d, b = s
                    transposes(open_tile(0), [cv[:, 4 + h, tok(b)] for h in range(MH)]).then_inc(tile_full, 1)
                    pe.wait_ge(by(0), emptied(0))
                    for h in range(MH):
                        t = open_tile(1 + h)
                        mm(t[:, 0:DV + 1], W[:, h, :], va[:, b, h, :], True, True).then_inc(tile_full, 1)
                elif k == "T2":
                    _, l, g = s
                    src = hm if l == 0 else qkv
                    for b in range(len(BLOCKS[g])):
                        for i in range(2):
                            transposes(open_tile(2 * b + i),
                                       [src[:, b, (4 * i + q) * P:(4 * i + q + 1) * P] for q in range(4)])\
                                .then_inc(tile_full, 1)
                    c = COND[BLOCKS[g][0]]
                    on_all_partitions(2 * len(BLOCKS[g]), lambda q: modT[:, l, 16 + q, c:c + 1])
                elif k == "PQ":
                    by_feature(P * len(BLOCKS[s[2]]))
                elif k == "PS":
                    _, l, g, b = s
                    w = weights().rearrange("p k n -> p (k n)")
                    for i in range(4):
                        t = open_tile(i)
                        for q in range(4):
                            e = 4 * i + q
                            last = mm(t[:, q * P:(q + 1) * P], qTp[:, e, tok(b)], w[:, e * NKEYS:(e + 1) * NKEYS], True, True)
                        last.then_inc(tile_full, 1)
                    for i in range(2):
                        transposes(open_tile(4 + i), [hT[:, 4 * i + q, tok(b)] for q in range(4)]).then_inc(tile_full, 1)
                elif k == "AC":
                    pe.wait_ge(cache_in, next_of(cache_in, 48))
                    transposes(open_tile(0), [kdup[:, v, :, :].rearrange("p a n -> p (a n)") for v in range(AKV)])\
                        .then_inc(tile_full, 1)
                elif k == "AT":
                    _, g, b = s
                    for i in range(2):
                        transposes(open_tile(i), [qkv[:, b, (4 * i + q) * P:(4 * i + q + 1) * P] for q in range(4)])\
                            .then_inc(tile_full, 1)
                    pe.wait_ge(key_pairs, next_of(key_pairs))
                    transposes(open_tile(2), [kdup[:, v, :, :].rearrange("p a n -> p (a n)") for v in range(AKV)])\
                        .then_inc(tile_full, 1)
                elif k == "AS":
                    _, g, b, kv = s
                    nk = 1 if g == "P" else 3
                    for i in range(4):
                        h = kv * 4 + i
                        half = slice((h % 2) * HD, (h % 2 + 1) * HD)
                        t = open_tile(i)
                        mm(t[:, 0:nk * P], qTa[half, h // 2, tok(b)], kTa[half, kv, 0:nk * P], True, True)\
                            .then_inc(tile_full, 1)

                    def values(i):
                        pe.wait_ge(by(4 + i), emptied(4 + i))
                        for c in range(nk):
                            v = vc[:, kv, :] if nk == 3 and c == 0 else \
                                qkv[:, c - (nk == 3), (AH + AKV + kv) * HD:(AH + AKV + kv + 1) * HD]
                            last = mm(out[:, i * HD:(i + 1) * HD], pTa[i % 2][:, c * P:(c + 1) * P], v,
                                      c == 0, c == nk - 1)
                        return last

                    out = open_tile(8)
                    for i in range(4):
                        t = open_tile(4 + i)
                        pe.wait_ge(by(i), emptied(i))
                        transposes(t, [prA[i][:, c * P:(c + 1) * P] for c in range(nk)]).then_inc(tile_full, 1)
                        if i:
                            values(i - 1)
                    values(3).then_inc(tile_full, 1)
                elif k == "FIN":
                    c = COND[s[2]]
                    on_all_partitions(0, lambda q: modT[:, s[1], 40 + q, c:c + 1])
                elif k == "YOUT":
                    on_all_partitions(0, lambda q: cst("final_g")[:, q:q + 1])

        @block.scalar
        def _(act):
            begin, tile, full, by, emptied, next_of, one, noted = places("A")
            sent = {"stored": 0, "state_out": 0}

            def f(out, in_, func, **kw):
                return nc.scalar.activation(out, in_, func, **kw)

            def copy_tile(j, out, n=512, view=None):
                act.wait_ge(tile_full, full(j))
                t = tile(j)[:, 0:n]
                f(out, view(t) if view else t, ACT.Copy).then_inc(act_freed, 1)

            def rsqrt_parts(src, n=D):
                f(xn, src, ACT.Square, accum_out=ssq[:, 0:1]).then_inc(squares, 1)
                act.wait_ge(mean_sq, next_of(mean_sq))
                f(sd[:, 0:1], ms[:, 0:1], ACT.Sqrt).then_inc(root, 1)

            def diagonals(n, ring):
                act.wait_ge(weighted, n + 1)
                for j in range(GS - (ring % SIDE_EVERY == SIDE)):
                    last = f(diag[:, ring * GS + j, :], ident, ACT.Copy, scale=wv[:, ring, j:j + 1])
                last.then_inc(diags, 1)

            def group(n, slot, ring, turn, g):
                act.wait_ge(dots, n + 1)
                f(act_out[:, ring, :], act_in[:, ring, :], ACT.Gelu).then_inc(gelus, 1)
                if g != 0:
                    diagonals(n - 1, (ring - 1) % RING)

            def last_groups(n):
                diagonals(n - 1, (n - 1) % RING)

            def store(out, in_):
                act.dma_start(out, in_).then_inc(stored, 16)
                sent["stored"] += 1

            act.wait_ge(inputs_in, 48)
            for n_entry, s in enumerate(PLAN):
                k = s[0]
                tiles, by_act, by_dve, acts, dves = begin(n_entry)
                if tiles:
                    act.wait_ge(tile_full, tiles)
                if by_act:
                    act.wait_ge(act_freed, by_act)
                if by_dve:
                    act.wait_ge(dve_freed, by_dve)
                if acts:
                    act.wait_ge(act_step, acts)
                if dves:
                    act.wait_ge(dve_step, dves)
                if k == "GROUPS":
                    run_groups(act, s, group, last_groups)
                    continue
                if noted():
                    act.wait_ge(act_chain, noted())
                if k == "INIT":
                    act.wait_ge(zeroed, 1)
                    f(cs[:, :, 0:2], cst("cond").rearrange("p (k c) -> p k c", c=2), ACT.Silu).then_inc(act_step, 1)
                elif k == "MOD":
                    for j in range(4):
                        act.wait_ge(tile_full, full(MOD_ROWS[j]))
                        t = tile(MOD_ROWS[j])
                        f(mod_rows[:, j % 2, :], t[:, 0:WC], ACT.Copy).then_inc(act_freed, 1)
                elif k == "NORM":
                    _, l, w, b = s
                    c = COND[b]
                    rsqrt_parts(x[:, b, :])
                    act.wait_ge(tile_full, full(0))
                    t = tile(0)
                    place = tok(b - (b > 0))
                    for q in range(4):
                        last = f(hT[:, q, place], t[:, q * P:(q + 1) * P], ACT.Identity,
                                 scale=gain[:, l, w, q, c:c + 1], bias=modT[:, l, 24 * w + q, c:c + 1])
                    last.then_inc(act_freed, 1)
                elif k == "MLQK":
                    _, g, half = s
                    n = P * len(BLOCKS[g])
                    for i in range(4):
                        copy_tile(i, raw[:, 4 * half + i, 1:n + 1], n)
                    for i in range(4):
                        e = 4 * half + i
                        act.wait_ge(convolved, next_of(convolved))
                        last = f(cv[:, e, 0:n], cv[:, e, 0:n], ACT.Silu, bias=cst("conv_b")[:, e:e + 1])
                    last.then_inc(act_step, 1)
                elif k == "MLV":
                    _, g, half = s
                    nb = len(BLOCKS[g])
                    for j in range(2):
                        for b in range(nb):
                            copy_tile(j * nb + b, va[:, b, 2 * half + j, 0:DV], WC)
                elif k == "MLG":
                    n = 8 * len(BLOCKS[s[1]])
                    act.wait_ge(abs_gate, next_of(abs_gate))
                    f(gtmp[:, 2, 0:n], gtmp[:, 1, 0:n], ACT.Exp, scale=-1.0).then_inc(act_chain, one())
                    act.wait_ge(act_chain, noted())
                    f(gtmp[:, 3, 0:n], gtmp[:, 2, 0:n], ACT.Ln, bias=1.0).then_inc(soft_gate, 1)
                elif k == "MLA":
                    _, g, d, b = s
                    if g == "S" and b == d:
                        act.dma_start(Cst[:, :, 0:DV], A["state_mlstm_C"][0, 0, d].rearrange("h p v -> p h v"))\
                            .then_inc(state_in, 16)
                        act.dma_start(Cst[:, :, DV], A["state_mlstm_n"][0, 0, d].rearrange("h p -> p h"), allow_slow_non_contiguous=True)\
                            .then_inc(state_in, 16)
                    act.wait_ge(maxima, next_of(maxima))
                    f(ae, t12, ACT.Exp).then_inc(act_chain, one())
                    for h in range(MH):
                        last = f(W[:, h, :], W[:, h, :], ACT.Exp, bias=nMp[:, h:h + 1])
                    last.then_inc(probs_raw, 1)
                    copy_tile(2, WT.rearrange("p h n -> p (h n)"))
                elif k == "MLB":
                    if s[1] == "S":
                        act.wait_ge(act_chain, noted())
                        for h in range(MH):
                            act.wait_ge(tile_full, full(2 * h))
                            t = tile(2 * h)
                            f(Nn[:, h, :], t[:, 0:DV + 1], ACT.Copy, scale=ae[:, h:h + 1]).then_inc(act_freed, 1)
                elif k == "MLC":
                    _, g, d, b = s
                    act.wait_ge(carry_in, next_of(carry_in))
                    f(dw, dww, ACT.Exp).then_inc(carry_exp, 1)
                    if g == "P":
                        act.wait_ge(by(MH), emptied(MH))
                        act.dma_start(O["new_C"][0, 0, d].rearrange("h p v -> p h v"), Cst[:, :, 0:DV]).then_inc(state_out, 16)
                        act.dma_start(O["new_n"][0, 0, d].rearrange("h p -> p h"), Cst[:, :, DV], allow_slow_non_contiguous=True).then_inc(state_out, 16)
                        act.dma_start(O["new_m"][0, 0, d:d + 1, :], mst[0:1, d, :]).then_inc(state_out, 16)
                        sent["state_out"] += 3
                elif k == "MLN":
                    for b in range(len(BLOCKS[s[1]])):
                        act.wait_ge(mean_sq, next_of(mean_sq))
                        f(sd[:, 0:MH], ms[:, 0:MH], ACT.Sqrt).then_inc(root, 1)
                elif k == "MLO":
                    nb = len(BLOCKS[s[1]])
                    for i in range(2 * nb):
                        act.wait_ge(tile_full, full(i))
                        t = tile(i)
                        f(Nflat[:, i * WC:(i + 1) * WC], t[:, 0:WC], ACT.Sigmoid).then_inc(act_freed, 1)
                elif k == "T2":
                    _, l, g = s
                    nb = len(BLOCKS[g])
                    for b in range(nb):
                        for i in range(2):
                            act.wait_ge(tile_full, full(2 * b + i))
                            t = tile(2 * b + i)
                            if l == 0:
                                for q in range(4):
                                    last = f(hT[:, 4 * i + q, tok(b)], t[:, q * P:(q + 1) * P], ACT.Copy,
                                             scale=cst("head_g")[:, 4 * i + q:4 * i + q + 1])
                            else:
                                last = f(hT[:, 4 * i:4 * i + 4, tok(b)], t[:].rearrange("p (q n) -> p q n", n=P), ACT.Copy)
                            last.then_inc(act_freed, 1)
                    for i in range(2):
                        copy_tile(2 * nb + i, gbc[:, i * 512:(i + 1) * 512])
                elif k == "PQ":
                    _, l, g, q = s
                    n = P * len(BLOCKS[g])
                    for i in range(4):
                        copy_tile(i, qTp[:, 4 * q + i, 0:n], n)
                elif k == "PS":
                    _, l, g, b = s
                    for i in range(2):
                        copy_tile(4 + i, xb[:, GORDER.index((l, BLOCKS[g][b])) % 2, i * 512:(i + 1) * 512])
                elif k == "PG":
                    half = s[4] * (PH // 2)
                    act.wait_ge(tops, next_of(tops))
                    f(topc[:, half:half + PH // 2, :], topc[:, half:half + PH // 2, :], ACT.Exp).then_inc(top_exp, 1)
                elif k == "AQKV":
                    _, g, third = s
                    nb = len(BLOCKS[g])
                    for j in range(2):
                        for b in range(nb):
                            c = (2 * third + j) * WC
                            copy_tile(j * nb + b, qkv[:, b, c:c + WC], WC)
                elif k == "AN":
                    _, g, b = s
                    act.wait_ge(mean_sq, next_of(mean_sq))
                    f(sd[:], ms[:], ACT.Sqrt).then_inc(root, 1)
                    if g == "P":
                        act.wait_ge(kv_done, next_of(kv_done))
                        store(O["new_k"][0, 0].rearrange("v t n -> t v n"),
                              qkv[:, 0, AH * HD:(AH + AKV) * HD].rearrange("p (v n) -> p v n", n=HD))
                        store(O["new_v"][0, 0].rearrange("v t n -> t v n"),
                              qkv[:, 0, (AH + AKV) * HD:].rearrange("p (v n) -> p v n", n=HD))
                elif k == "AC":
                    for a in range(2):
                        act.dma_start(kdup[:, :, a, :], A["cache_attn_k"][0, 0].rearrange("v t n -> t v n")).then_inc(cache_in, 16)
                    act.dma_start(vc, A["cache_attn_v"][0, 0].rearrange("v t n -> t v n")).then_inc(cache_in, 16)
                    copy_tile(0, kTa[:, :, 0:P], 512, lambda t: t.rearrange("p (v n) -> p v n", n=P))
                elif k == "AT":
                    _, g, b = s
                    for i in range(2):
                        copy_tile(i, qTa[:, 4 * i:4 * i + 4, tok(b)], 512, lambda t: t.rearrange("p (q n) -> p q n", n=P))
                    copy_tile(2, kTa[:, :, tok(b + (g == "S"))], 512, lambda t: t.rearrange("p (v n) -> p v n", n=P))
                elif k == "AS":
                    _, g, b, kv = s
                    n = P if g == "P" else 3 * P
                    for i in range(4):
                        act.wait_ge(row_max, next_of(row_max))
                        act.wait_ge(tile_full, full(i))
                        t = tile(i)
                        f(prA[i][:, 0:n], t[:, 0:n], ACT.Exp, bias=nsmx[:, i:i + 1], scale=ASCALE,
                                   accum_out=rsum[:, i:i + 1]).then_inc(act_freed, 1)
                elif k in ("FIN", "YOUT"):
                    if k == "YOUT":
                        rsqrt_parts(x[:, s[1], :])
                    for i in range(2):
                        copy_tile(i, gbc[:, i * 512:(i + 1) * 512])
                    if k == "YOUT":
                        act.wait_ge(y_done, next_of(y_done))
                        b = s[1]
                        store(O["y_prompt"][0] if b == 0 else O["y_sample"][0, tok(b - 1), :], x[:, b, :])
            act.wait_ge(stored, 16 * sent["stored"])
            act.wait_ge(state_out, 16 * sent["state_out"])

        @block.vector
        def _(dve):
            begin, tile, full, by, emptied, next_of, one, noted = places("D")
            V = nc.vector

            def bc(ap, n):
                return ap.unsqueeze(len(ap.shape)).to_broadcast([*ap.shape, n])

            def rsqrt(n, width):
                V.tensor_scalar(ms[:, 0:n], ssq[:, 0:n], 1.0 / width, EPS, ALU.mult, ALU.add).then_inc(mean_sq, 1)
                dve.wait_ge(root, next_of(root))
                V.reciprocal(rstd[:, 0:n], sd[:, 0:n]).then_inc(dve_chain, one())
                dve.wait_ge(dve_chain, noted())

            def top16(vals, idx, srcs):
                sets = range(len(srcs))
                for e in sets:
                    V.max(vals[:, e, 0:8], srcs[e]).then_inc(dve_chain, one())
                dve.wait_ge(dve_chain, noted())
                for e in sets:
                    V.max_index(idx[:, e, 0:8], vals[:, e, 0:8], srcs[e]).then_inc(dve_chain, one())
                dve.wait_ge(dve_chain, noted())
                for e in sets:
                    V.match_replace(srcs[e], vals[:, e, 0:8], srcs[e], NEG).then_inc(dve_chain, one())
                dve.wait_ge(dve_chain, noted())
                for e in sets:
                    V.max(vals[:, e, 8:16], srcs[e]).then_inc(dve_chain, one())
                dve.wait_ge(dve_chain, noted())
                for e in sets:
                    last = V.max_index(idx[:, e, 8:16], vals[:, e, 8:16], srcs[e])
                    if e < len(srcs) - 1:
                        last.then_inc(dve_chain, one())
                last.then_inc(dve_step, 1)

            def weigh(b, n, slot, ring):
                dve.wait_ge(gelus, n + 1)
                g = gate[:, b, slot:slot + GS] if isinstance(slot, int) else gate[:, b, bass.ds(slot, GS)]
                V.tensor_tensor(wv[:, ring, :], act_out[:, ring, :], g, ALU.mult).then_inc(weighted, 1)

            def add_up(n, ring):
                dve.wait_ge(weighted, n + 1)
                V.scalar_tensor_tensor(side[:], rows[:, ring * GS + GS - 1, D:2 * D], wv[:, ring, GS - 1:GS], side[:],
                                       ALU.mult, ALU.add).then_inc(side_summed, 1)

            def group(b, place):
                def body(n, slot, ring, turn, g):
                    if g == 0:
                        V.memset(side[:], 0.0).then_inc(side_zero, 1)
                        dve.wait_ge(side_zero, n // GROUPS + 1)
                    for j in range(GS):
                        r = ring * GS + j
                        dve.wait_ge(rows_in[r], turn * 16 + 16)
                        last = V.tensor_tensor_reduce(out=rows[:, r, 0:D], in0=rows[:, r, 0:D], in1=xb[:, place, :],
                                                      scale=1.0, scalar=0.0, op0=ALU.mult, op1=ALU.add,
                                                      accum_out=act_in[:, ring, j:j + 1])
                    last.then_inc(dots, 1)
                    if g != 0:
                        weigh(b, n - 1, slot - GS, (ring - 1) % RING)
                        if (ring - 1) % SIDE_EVERY == SIDE:
                            add_up(n - 1, (ring - 1) % RING)
                return body

            def last_groups(b):
                def body(n):
                    weigh(b, n - 1, SLOTS - GS, (n - 1) % RING)
                    if (n - 1) % SIDE_EVERY == SIDE:
                        add_up(n - 1, (n - 1) % RING)
                return body

            V.memset(cs[:], 0.0).then_inc(zeroed, 1)
            dve.wait_ge(inputs_in, 48)
            for n_entry, s in enumerate(PLAN):
                k = s[0]
                tiles, by_act, by_dve, acts, dves = begin(n_entry)
                if tiles:
                    dve.wait_ge(tile_full, tiles)
                if by_act:
                    dve.wait_ge(act_freed, by_act)
                if by_dve:
                    dve.wait_ge(dve_freed, by_dve)
                if acts:
                    dve.wait_ge(act_step, acts)
                if dves:
                    dve.wait_ge(dve_step, dves)
                if k == "GROUPS":
                    if s[3] == 0:
                        dve.wait_ge(experts_chosen, 2 * GORDER.index((s[1], s[2])) + 1)
                    run_groups(dve, s, group(s[2], GORDER.index((s[1], s[2])) % 2), last_groups(s[2]))
                    continue
                if noted():
                    dve.wait_ge(dve_chain, noted())
                if k == "MOD":
                    _, l, q = s
                    for j in range(4):
                        dve.wait_ge(tile_full, full(MOD_COLUMNS[j]))
                        t = tile(MOD_COLUMNS[j])
                        n = slice(8 * q + 2 * j, 8 * q + 2 * j + 2)
                        V.tensor_tensor(modT[:, l, n, :], t[:, 0:4].rearrange("p (n c) -> p n c", c=2),
                                        bc(ada_b[:, l, n], 2), ALU.add).then_inc(dve_freed, 1)
                    dve.wait_ge(by(MOD_COLUMNS[3]), emptied(MOD_COLUMNS[3]))
                    if q in (1, 4):
                        w = q // 4
                        V.tensor_scalar(gain[:, l, w], modT[:, l, 8 * q:8 * q + 8, :], 1.0, None, ALU.add).then_inc(dve_chain, one())
                        dve.wait_ge(dve_chain, noted())
                        V.tensor_tensor(gain[:, l, w], gain[:, l, w], bc(norm_g[:, l, w], 2), ALU.mult).then_inc(dve_step, 1)
                elif k == "NORM":
                    _, l, w, b = s
                    c = COND[b]
                    dve.wait_ge(squares, next_of(squares))
                    rsqrt(1, D)
                    V.tensor_scalar(xn, x[:, b, :], rstd[:, 0:1], None, ALU.mult).then_inc(normed, 1)
                    dve.wait_ge(tile_full, full(1))
                    t = tile(1)
                    place = tok(b - (b > 0))
                    for q in range(4):
                        last = V.tensor_scalar(hT[:, 4 + q, place], t[:, q * P:(q + 1) * P], gain[:, l, w, 4 + q, c:c + 1],
                                               modT[:, l, 24 * w + 4 + q, c:c + 1], ALU.mult, ALU.add)
                    last.then_inc(dve_freed, 1)
                elif k == "MLQK":
                    _, g, half = s
                    n = P * len(BLOCKS[g])
                    V.memset(raw[:, 4 * half:4 * half + 4, 0:1], 0.0).then_inc(dve_chain, one())
                    V.memset(raw[:, 4 * half:4 * half + 4, n + 1:n + 2], 0.0).then_inc(dve_chain, one())
                    dve.wait_ge(dve_chain, noted())
                    for i in range(4):
                        e = 4 * half + i
                        dve.wait_ge(by(i), emptied(i))
                        V.tensor_scalar(cv[:, e, 0:n], raw[:, e, 0:n], conv_w[:, e, 0:1], None, ALU.mult).then_inc(dve_chain, one())
                        dve.wait_ge(dve_chain, noted())
                        for j in (1, 2):
                            last = V.scalar_tensor_tensor(cv[:, e, 0:n], raw[:, e, j:j + n], conv_w[:, e, j:j + 1],
                                                          cv[:, e, 0:n], ALU.mult, ALU.add)
                            if j == 1:
                                last.then_inc(dve_chain, one())
                                dve.wait_ge(dve_chain, noted())
                        last.then_inc(convolved, 1)
                elif k == "MLV":
                    _, g, half = s
                    V.memset(va[:, 0:len(BLOCKS[g]), 2 * half:2 * half + 2, DV], 1.0).then_inc(dve_step, 1)
                elif k == "MLG":
                    g = s[1]
                    nb = len(BLOCKS[g])
                    n = 8 * nb
                    dve.wait_ge(tile_full, full(0))
                    t = tile(0)
                    gt = gates_all[:, 0:nb, :]
                    V.tensor_tensor(gt, t[:, 0:16 * nb].rearrange("p (b n) -> p b n", n=16),
                                          cst("gate_b").unsqueeze(1).to_broadcast([P, nb, 16]), ALU.add).then_inc(dve_freed, 1)
                    dve.wait_ge(by(0), emptied(0))
                    kinds = gtmp[:, 0, 0:16 * nb].rearrange("p (e k h) -> p e k h", k=2, h=MH)
                    fg, inp = kinds[:, :, 1, :], kinds[:, :, 0, :]
                    part = [gtmp[:, i, 0:n].rearrange("p (e h) -> p e h", h=MH) for i in range(4)]
                    flat = [v[:, 0:nb].rearrange("p b d h -> p (b d) h") for v in (ig, nlf)]
                    V.scalar_tensor_tensor(part[1], fg, -1.0, fg, ALU.mult, ALU.max).then_inc(abs_gate, 1)
                    V.tensor_copy(flat[0], inp).then_inc(dve_chain, one())
                    V.tensor_scalar(flat[1], fg, -1.0, 0.0, ALU.mult, ALU.max).then_inc(dve_chain, one())
                    dve.wait_ge(dve_chain, noted())
                    dve.wait_ge(soft_gate, next_of(soft_gate))
                    V.tensor_tensor(flat[1], flat[1], part[3], ALU.add).then_inc(log_gate, 1)
                    if g == "P":
                        V.memset(mst, 0.0).then_inc(dve_chain, one())
                    else:
                        V.tensor_copy(mst.rearrange("p d h -> p (d h)"), cst("m0")).then_inc(dve_chain, one())
                    dve.wait_ge(tile_full, full(1))
                    t = tile(1)
                    V.tensor_copy(bt[:, 0:nb, :], t[:, 0:16 * nb].rearrange("p (b n) -> p b n", n=16)).then_inc(dve_freed, 1)
                    dve.wait_ge(by(1), emptied(1))
                    V.tensor_tensor(rcol[:, 0:nb].rearrange("p b d h -> p b (d h)"), ig[:, 0:nb].rearrange("p b d h -> p b (d h)"),
                                        bt[:, 0:nb, 0:8], ALU.add).then_inc(dve_step, 1)
                elif k == "MLA":
                    _, g, d, b = s
                    each = lambda m: m.unsqueeze(1).to_broadcast([P, MH, P])
                    V.tensor_tensor(WT, each(tri[:, d, :]), bc(nlf[:, b, d, :], P), ALU.mult).then_inc(dve_chain, one())
                    V.tensor_tensor(W, each(ident), bc(ig[:, b, d, :], P), ALU.mult).then_inc(dve_chain, one())
                    dve.wait_ge(dve_chain, noted())
                    V.tensor_tensor(W, W, WT, ALU.add).then_inc(decay_rows, 1)
                    dve.wait_ge(tile_full, full(0))
                    t = tile(0).rearrange("p (h n) -> p h n", n=P)
                    V.tensor_reduce(rall, t, AX.X, ALU.max).then_inc(dve_chain, one())
                    V.tensor_tensor(W, t, each(mask[:, d, :]), ALU.add).then_inc(dve_freed, 1)
                    dve.wait_ge(by(0), emptied(0))
                    V.tensor_reduce(rmx, W, AX.X, ALU.max).then_inc(dve_chain, one())
                    dve.wait_ge(dve_chain, noted())
                    V.tensor_tensor(rmx, rmx, mst[:, d, :], ALU.max).then_inc(dve_chain, one())
                    dve.wait_ge(dve_chain, noted())
                    V.tensor_tensor(t12[:, 0:4], mst[:, d, :], rmx, ALU.subtract).then_inc(dve_chain, one())
                    V.tensor_scalar(nMp, rmx, -1.0, None, ALU.mult).then_inc(dve_chain, one())
                    dve.wait_ge(dve_chain, noted())
                    V.tensor_tensor(t12[:, 4:8], bt[:, b, 4 * d:4 * d + 4], nMp, ALU.add).then_inc(maxima, 1)
                    dve.wait_ge(tile_full, full(1))
                    t = tile(1)
                    dve.wait_ge(probs_raw, next_of(probs_raw))
                    Wf = W.rearrange("p h n -> p (h n)")
                    V.scalar_tensor_tensor(Wf, t[:], KSCALE, Wf, ALU.mult, ALU.mult).then_inc(dve_freed, 1)
                elif k == "MLB":
                    _, g, d, b = s
                    for h in range(MH):
                        if g == "S":
                            dve.wait_ge(by(2 * h), emptied(2 * h))
                            dve.wait_ge(tile_full, full(2 * h + 1))
                            t = tile(2 * h + 1)
                            V.tensor_tensor(Nn[:, h, :], t[:, 0:DV + 1], Nn[:, h, :], ALU.add).then_inc(dve_freed, 1)
                            dve.wait_ge(by(2 * h + 1), emptied(2 * h + 1))
                        else:
                            dve.wait_ge(tile_full, full(h))
                            t = tile(h)
                            V.tensor_copy(Nn[:, h, :], t[:, 0:DV + 1]).then_inc(dve_freed, 1)
                            dve.wait_ge(by(h), emptied(h))
                    V.tensor_scalar(den, Nn[:, :, DV], -1.0, None, ALU.mult).then_inc(dve_chain, one())
                    dve.wait_ge(dve_chain, noted())
                    V.tensor_tensor(den, den, Nn[:, :, DV], ALU.max).then_inc(dve_chain, one())
                    dve.wait_ge(dve_chain, noted())
                    V.tensor_tensor(den, den, ae[:, 4:8], ALU.max).then_inc(dve_chain, one())
                    dve.wait_ge(dve_chain, noted())
                    V.reciprocal(rden, den).then_inc(dve_chain, one())
                    dve.wait_ge(dve_chain, noted())
                    out = hm[:, b, :].rearrange("p (h v) -> p h v", v=DV)
                    if d == 0:
                        V.tensor_tensor(out, Nn[:, :, 0:DV], bc(rden, DV), ALU.mult).then_inc(dve_step, 1)
                    else:
                        V.tensor_tensor(Nn[:, :, 0:DV], Nn[:, :, 0:DV], bc(rden, DV), ALU.mult).then_inc(dve_chain, one())
                        dve.wait_ge(dve_chain, noted())
                        V.tensor_tensor(out, out, Nn[:, :, 0:DV], ALU.add).then_inc(dve_step, 1)
                elif k == "MLC":
                    _, g, d, b = s
                    V.tensor_tensor(mpp, mst[:, d, :], rall, ALU.max).then_inc(dve_chain, one())
                    dve.wait_ge(dve_chain, noted())
                    V.tensor_tensor(dww[:, 0:4], mst[:, d, :], mpp, ALU.subtract).then_inc(dve_chain, one())
                    dve.wait_ge(dve_chain, noted())
                    V.tensor_tensor(dww[:, 4:8], rcol[:, b, d, :], mpp, ALU.subtract).then_inc(carry_in, 1)
                    V.tensor_tensor(mst[:, d, :], mpp, bt[:, b, 8 + 4 * d:12 + 4 * d], ALU.subtract).then_inc(dve_chain, one())
                    dve.wait_ge(dve_chain, noted())
                    dve.wait_ge(carry_exp, next_of(carry_exp))
                    V.tensor_scalar(dw[:, 4:8], dw[:, 4:8], KSCALE, None, ALU.mult).then_inc(dve_chain, one())
                    dve.wait_ge(dve_chain, noted())
                    dve.wait_ge(tile_full, full(0))
                    t = tile(0)
                    V.tensor_tensor(W, t[:].rearrange("p (h n) -> p h n", n=P), bc(dw[:, 4:8], P), ALU.mult).then_inc(dve_freed, 1)
                    if g == "P" and d == 1:
                        dve.wait_ge(state_out, 48)
                    for h in range(MH):
                        dve.wait_ge(tile_full, full(1 + h))
                        t = tile(1 + h)
                        if g == "P":
                            last = V.tensor_copy(Cst[:, h, :], t[:, 0:DV + 1])
                        else:
                            last = V.scalar_tensor_tensor(Cst[:, h, :], Cst[:, h, :], dw[:, h:h + 1], t[:, 0:DV + 1],
                                                          ALU.mult, ALU.add)
                        last.then_inc(dve_freed, 1)
                elif k == "MLN":
                    if s[1] == "P":
                        dve.wait_ge(state_out, 96)
                    for b in range(len(BLOCKS[s[1]])):
                        h4 = hm[:, b, :].rearrange("p (h v) -> p h v", v=DV)
                        V.tensor_tensor(Nn[:, :, 0:DV], h4, h4, ALU.mult).then_inc(dve_chain, one())
                        dve.wait_ge(dve_chain, noted())
                        V.tensor_reduce(ssq[:, 0:MH], Nn[:, :, 0:DV], AX.X, ALU.add).then_inc(dve_chain, one())
                        dve.wait_ge(dve_chain, noted())
                        rsqrt(MH, DV)
                        last = V.tensor_tensor(h4, h4, bc(rstd[:, 0:MH], DV), ALU.mult)
                        if b < len(BLOCKS[s[1]]) - 1:
                            last.then_inc(dve_chain, one())
                            dve.wait_ge(dve_chain, noted())
                    last.then_inc(dve_step, 1)
                elif k == "MLO":
                    _, g, half = s
                    nb = len(BLOCKS[g])
                    for j in range(2):
                        for b in range(nb):
                            i = j * nb + b
                            dve.wait_ge(by(i), emptied(i))
                            h1 = hm[:, b, (2 * half + j) * DV:(2 * half + j + 1) * DV]
                            last = V.tensor_tensor(h1, h1, Nflat[:, i * WC:(i + 1) * WC], ALU.mult)
                    last.then_inc(dve_step, 1)
                elif k == "OUT":
                    _, l, g, half = s
                    nb = len(BLOCKS[g])
                    if l == 1 and g == "P" and half == 0:
                        dve.wait_ge(stored, 32)
                    for j in range(2):
                        for b in range(nb):
                            i = j * nb + b
                            c = slice((2 * half + j) * WC, (2 * half + j + 1) * WC)
                            dve.wait_ge(tile_full, full(i))
                            t = tile(i)
                            tmp = xn[:, i * WC:(i + 1) * WC]
                            V.tensor_tensor(tmp, t[:, 0:WC], gbc[:, c], ALU.mult).then_inc(dve_freed, 1)
                            dve.wait_ge(by(i), emptied(i))
                            xc = x[:, BLOCKS[g][b], c]
                            last = V.tensor_tensor(xc, xc, tmp, ALU.add)
                            if i < 2 * nb - 1:
                                last.then_inc(dve_chain, one())
                    last.then_inc(dve_step, 1)
                elif k == "PS":
                    for i in range(4):
                        dve.wait_ge(tile_full, full(i))
                        t = tile(i)
                        V.tensor_copy(sc[:, 4 * i:4 * i + 4, :], t[:].rearrange("p (e n) -> p e n", n=NKEYS)).then_inc(dve_freed, 1)
                elif k == "PT":
                    q = s[4]
                    n = slice(4 * q, 4 * q + 4)
                    top16(top1[:, n, :], i1u[:, n, :], [sc[:, e, :] for e in range(4 * q, 4 * q + 4)])
                elif k == "PC":
                    q = s[4]
                    h0 = 4 * q
                    t2 = top1.rearrange("p (h a) k -> p h a k", a=2)[:, h0:h0 + 4]
                    c4 = cand.rearrange("p h (i j) -> p h i j", j=TOPK)
                    V.tensor_tensor(c4, bc(t2[:, :, 0, :], TOPK),
                                           t2[:, :, 1, :].unsqueeze(2).to_broadcast([P, 4, TOPK, TOPK]), ALU.add).then_inc(dve_chain, one())
                    dve.wait_ge(dve_chain, noted())
                    n = slice(h0, h0 + 4)
                    top16(topc[:, n, :], posu[:, n, :], [cand[:, h, :] for h in range(4)])
                elif k == "PG":
                    _, l, g, b, half = s
                    blk = BLOCKS[g][b]
                    nh = PH // 2
                    heads = slice(half * nh, (half + 1) * nh)
                    n = slice(half * nh * TOPK, (half + 1) * nh * TOPK)
                    tc = topc[:, heads, :]
                    V.tensor_copy(gsum[:, 0:nh], tc[:, :, 0]).then_inc(dve_chain, one())
                    dve.wait_ge(dve_chain, noted())
                    V.tensor_tensor(tc, tc, bc(gsum[:, 0:nh], TOPK), ALU.subtract).then_inc(tops, 1)
                    pos = posu.rearrange("p h k -> p (h k)")[:, n]
                    V.tensor_scalar(piju[:, 0, n], pos, 4, None, ALU.logical_shift_right).then_inc(dve_chain, one())
                    V.tensor_scalar(piju[:, 1, n], pos, 15, None, ALU.bitwise_and).then_inc(dve_chain, one())
                    keys = i1f[:, 2 * half * nh:2 * (half + 1) * nh, :]
                    V.tensor_copy(keys, i1u[:, 2 * half * nh:2 * (half + 1) * nh, :]).then_inc(dve_chain, one())
                    dve.wait_ge(dve_chain, noted())
                    V.tensor_copy(pij[:, :, n], piju[:, :, n]).then_inc(dve_chain, one())
                    dve.wait_ge(dve_chain, noted())
                    place_of = [cand.rearrange("p a b -> p (a b)"), sc[:, 2 * half * nh:2 * (half + 1) * nh, :].rearrange("p a b -> p (a b)")]
                    keys = keys.rearrange("p (h a) k -> p h a k", a=2)
                    slots = nh * TOPK
                    for a in range(2):
                        V.tensor_tensor(place_of[a].rearrange("p (s e) -> p s e", e=TOPK), bc(pij[:, a, n], TOPK),
                                             cst("iota").unsqueeze(1).to_broadcast([P, slots, TOPK]), ALU.is_equal).then_inc(dve_chain, one())
                    dve.wait_ge(dve_chain, noted())
                    for a in range(2):
                        hot4 = place_of[a].rearrange("p (h s e) -> p h s e", h=nh, e=TOPK)
                        V.tensor_tensor(hot4, hot4, keys[:, :, a, :].unsqueeze(2).to_broadcast([P, nh, TOPK, TOPK]), ALU.mult).then_inc(dve_chain, one())
                    dve.wait_ge(dve_chain, noted())
                    for a in range(2):
                        V.tensor_reduce(e12[:, a, n], place_of[a].rearrange("p (s e) -> p s e", e=TOPK), AX.X, ALU.add).then_inc(dve_chain, one())
                    dve.wait_ge(dve_chain, noted())
                    V.scalar_tensor_tensor(e12[:, 0, n], e12[:, 0, n], float(NKEYS), e12[:, 1, n], ALU.mult, ALU.add).then_inc(dve_chain, one())
                    dve.wait_ge(dve_chain, noted())
                    V.tensor_scalar(eidx[:, blk, n], e12[:, 0, n], float(l * EXPERTS), None, ALU.add).then_inc(experts_chosen, 1)
                    dve.wait_ge(top_exp, next_of(top_exp))
                    V.tensor_reduce(gsum[:, 0:nh], tc, AX.X, ALU.add).then_inc(dve_chain, one())
                    dve.wait_ge(dve_chain, noted())
                    V.reciprocal(grec[:, 0:nh], gsum[:, 0:nh]).then_inc(dve_chain, one())
                    dve.wait_ge(dve_chain, noted())
                    V.tensor_tensor(gate[:, blk, n].rearrange("p (h k) -> p h k", k=TOPK), tc, bc(grec[:, 0:nh], TOPK), ALU.mult)\
                        .then_inc(dve_step, 1)
                elif k == "AN":
                    _, g, b = s
                    heads = AH + AKV
                    w = qkv[:, b, 0:heads * HD]
                    w3 = w.rearrange("p (h n) -> p h n", n=HD)
                    V.tensor_tensor(sq20, w, w, ALU.mult).then_inc(dve_chain, one())
                    dve.wait_ge(dve_chain, noted())
                    V.tensor_reduce(ssq, sq20.rearrange("p (h n) -> p h n", n=HD), AX.X, ALU.add).then_inc(dve_chain, one())
                    dve.wait_ge(dve_chain, noted())
                    rsqrt(heads, HD)
                    V.tensor_tensor(w3, w3, bc(rstd, HD), ALU.mult).then_inc(dve_chain, one())
                    dve.wait_ge(dve_chain, noted())
                    V.tensor_tensor(w3[:, 0:AH], w3[:, 0:AH], cst("q_g").unsqueeze(1).to_broadcast([P, AH, HD]), ALU.mult).then_inc(dve_chain, one())
                    dve.wait_ge(dve_chain, noted())
                    last = V.tensor_tensor(w3[:, AH:], w3[:, AH:], cst("k_g").unsqueeze(1).to_broadcast([P, AKV, HD]), ALU.mult)
                    if g == "P":
                        last.then_inc(kv_done, 1)
                        dve.wait_ge(kv_done, next_of(kv_done))
                        V.tensor_copy(ssq, rstd).then_inc(dve_step, 1)
                    else:
                        last.then_inc(dve_chain, one())
                        dve.wait_ge(dve_chain, noted())
                        wr = w.rearrange("p (h a r n) -> p h a r n", a=2, r=2, n=16)
                        t = sq20.rearrange("p (r h a n) -> p r h a n", r=2, a=2, n=16)
                        for a in range(2):
                            x1, x2 = wr[:, :, a, 0, :], wr[:, :, a, 1, :]
                            t1, t2 = t[:, 0, :, a, :], t[:, 1, :, a, :]
                            o = b * 32 + a * 16
                            cc = cst("cos")[:, o:o + 16].unsqueeze(1).to_broadcast([P, heads, 16])
                            ss = cst("sin")[:, o:o + 16].unsqueeze(1).to_broadcast([P, heads, 16])
                            V.tensor_tensor(t1, x1, ss, ALU.mult).then_inc(dve_chain, one())
                            V.tensor_tensor(t2, x2, ss, ALU.mult).then_inc(dve_chain, one())
                            dve.wait_ge(dve_chain, noted())
                            V.tensor_tensor(x1, x1, cc, ALU.mult).then_inc(dve_chain, one())
                            V.tensor_tensor(x2, x2, cc, ALU.mult).then_inc(dve_chain, one())
                            dve.wait_ge(dve_chain, noted())
                            V.tensor_tensor(x1, x1, t2, ALU.subtract).then_inc(dve_chain, one())
                            last = V.tensor_tensor(x2, x2, t1, ALU.add)
                            if a == 0:
                                last.then_inc(dve_chain, one())
                                dve.wait_ge(dve_chain, noted())
                        last.then_inc(dve_step, 1)
                elif k == "AT":
                    _, g, b = s
                    keys = qkv[:, b, AH * HD:(AH + AKV) * HD].rearrange("p (v n) -> p v n", n=HD)
                    V.tensor_copy(kdup[:, :, 0, :], keys).then_inc(dve_chain, one())
                    dve.wait_ge(dve_chain, noted())
                    V.tensor_copy(kdup[:, :, 1, :], keys).then_inc(key_pairs, 1)
                elif k == "AS":
                    _, g, b, kv = s
                    n = P if g == "P" else 3 * P
                    for i in range(4):
                        dve.wait_ge(tile_full, full(i))
                        t = tile(i)
                        V.tensor_reduce(smx[:, i:i + 1], t[:, 0:n], AX.X, ALU.max).then_inc(dve_chain, one())
                        dve.wait_ge(dve_chain, noted())
                        V.tensor_scalar(nsmx[:, i:i + 1], smx[:, i:i + 1], -ASCALE, None, ALU.mult).then_inc(row_max, 1)
                    for i in range(4):
                        dve.wait_ge(tile_full, full(4 + i))
                        t = tile(4 + i)
                        V.tensor_copy(pTa[i % 2][:, 0:n], t[:, 0:n]).then_inc(dve_freed, 1)
                    V.reciprocal(rrs, rsum).then_inc(dve_chain, one())
                    dve.wait_ge(dve_chain, noted())
                    dve.wait_ge(tile_full, full(8))
                    t = tile(8)
                    o = qkv[:, b, kv * 4 * HD:(kv * 4 + 4) * HD].rearrange("p (h n) -> p h n", n=HD)
                    V.tensor_tensor(o, t[:, 0:4 * HD].rearrange("p (h n) -> p h n", n=HD), bc(rrs, HD), ALU.mult).then_inc(dve_freed, 1)
                elif k == "FIN":
                    _, l, b = s
                    dve.wait_ge(summed, (GORDER.index((l, b)) + 1) * GROUPS)
                    dve.wait_ge(by(1), emptied(1))
                    dve.wait_ge(side_summed, (GORDER.index((l, b)) + 1) * (GROUPS // SIDE_EVERY))
                    V.tensor_tensor(xn, acc[:], side[:], ALU.add).then_inc(sum_read, 1)
                    dve.wait_ge(sum_read, next_of(sum_read))
                    V.tensor_tensor(xn, xn, gbc, ALU.mult).then_inc(dve_chain, one())
                    dve.wait_ge(dve_chain, noted())
                    V.tensor_tensor(x[:, b, :], x[:, b, :], xn, ALU.add).then_inc(dve_step, 1)
                elif k == "YOUT":
                    b = s[1]
                    dve.wait_ge(squares, next_of(squares))
                    rsqrt(1, D)
                    V.tensor_scalar(x[:, b, :], x[:, b, :], rstd[:, 0:1], None, ALU.mult).then_inc(dve_chain, one())
                    dve.wait_ge(dve_chain, noted())
                    dve.wait_ge(by(1), emptied(1))
                    V.tensor_tensor(x[:, b, :], x[:, b, :], gbc, ALU.mult).then_inc(y_done, 1)
                    dve.wait_ge(y_done, next_of(y_done))
                    V.tensor_copy(ssq[:, 0:1], rstd[:, 0:1]).then_inc(dve_step, 1)


_OUTS = [("y_prompt", (1, 128, 1024)), ("y_sample", (1, 256, 1024)), ("new_C", (1, 1, 2, 4, 128, 256)),
         ("new_n", (1, 1, 2, 4, 128)), ("new_m", (1, 1, 2, 4)), ("new_k", (1, 1, 4, 128, 64)), ("new_v", (1, 1, 4, 128, 64))]


def small_inputs(v):
    f = np.float32
    s = np.arange(P)

    def by_feature(a):
        return np.ascontiguousarray(a).reshape(-1, P).T

    def everywhere(a):
        return np.broadcast_to(np.ascontiguousarray(a).reshape(1, -1), (P, a.size))

    half = HD // 4
    inv = 10000.0 ** (-np.arange(half, dtype=f) / half)
    t = np.arange(2 * P)
    ang = np.concatenate([(t // 64).astype(f)[:, None] * inv, (t % 64).astype(f)[:, None] * inv], -1).astype(f)
    rope = lambda a: a.astype(f).reshape(2, P, 32).transpose(1, 0, 2).reshape(P, 64)
    upto, since = s[:, None] <= s[None, :], s[:, None] >= s[None, :]
    parts = {
        "ident": np.eye(P, dtype=f), "ones": np.ones((P, P), f),
        "tri": np.concatenate([upto, since], 1).astype(f),
        "mask": np.where(np.concatenate([since, upto], 1), 0.0, NEG).astype(f),
        "pick": (s[:, None] % 32 == np.arange(2)).astype(f), "iota": everywhere(np.arange(TOPK, dtype=f)), "cos": rope(np.cos(ang)), "sin": rope(np.sin(ang)),
        "cond": np.stack([v["c_ctx"].reshape(P, KC), v["c"].reshape(P, KC)], -1).reshape(P, 2 * KC),
        "ada_b": by_feature(v["ada_b"]), "norm_g": by_feature(v["norm_g"]), "final_g": by_feature(v["final_g"]),
        "head_g": by_feature(v["mlstm_head_g"]),
        "conv_w": v["mlstm_conv_w"][0].reshape(3, KC, P).transpose(2, 1, 0).reshape(P, 3 * KC),
        "conv_b": by_feature(v["mlstm_conv_b"]), "gate_b": everywhere(v["mlstm_gate_b"]),
        "q_g": everywhere(v["attn_q_g"]), "k_g": everywhere(v["attn_k_g"]), "m0": everywhere(v["state_mlstm_m"]),
        "w_gate": v["mlstm_w_in"][0, :, 3072:].reshape(KC, P, 16).transpose(1, 0, 2).reshape(P, KC * 16),
    }
    return np.ascontiguousarray(np.concatenate([parts[n] for n in SMALL], 1))


def kernel(**inputs):
    import concourse.bacc as _bacc
    from concourse.bass_utils import run_bass_kernel_spmd as _run

    v = {k: np.asarray(a) for k, a in inputs.items()}
    arrays = {n: np.ascontiguousarray(v[n]) for n in (
        "x_prompt", "x_sample", "state_mlstm_C", "state_mlstm_n", "cache_attn_k", "cache_attn_v", "ada_w",
        "mlstm_w_in", "mlstm_w_out", "attn_w_qkv", "attn_w_out", "peer_w_q")}
    arrays["uv"] = np.concatenate([v["peer_u"], v["peer_v"]], -1).reshape(DEPTH * EXPERTS, 2 * D)
    arrays["subkeys"] = np.ascontiguousarray(v["peer_subkeys"].transpose(0, 4, 1, 2, 3)).reshape(DEPTH, P, NSETS * NKEYS)
    arrays["small"] = small_inputs(v)
    nc = _bacc.Bacc("TRN2", target_bir_lowering=False, num_devices=1)
    A = {n: nc.dram_tensor(f"in_{n}", a.shape, mybir.dt.from_np(a.dtype), kind="ExternalInput").ap() for n, a in arrays.items()}
    O = {n: nc.dram_tensor(f"out_{n}", shape, F32, kind="ExternalOutput").ap() for n, shape in _OUTS}
    trunk(nc, A, O)
    r = _run(nc, [{f"in_{n}": a for n, a in arrays.items()}], core_ids=[0])
    return tuple(r.results[0][f"out_{n}"] for n, _ in _OUTS)
```

```python
import concourse.bass as bass
from concourse import mybir
from contextlib import ExitStack
import numpy as np

F32 = mybir.dt.float32
U32 = mybir.dt.uint32
ALU = mybir.AluOpType
ACT = mybir.ActivationFunctionType
AX = mybir.AxisListType

P = 128
D = 1024
KC = D // P
EPS = 1e-6
DEPTH = 2
MH, DQK, DV = 4, 128, 256
KSCALE = DQK ** -0.5
AH, AKV, HD = 16, 4, 64
ASCALE = HD ** -0.5
QKV = (AH + 2 * AKV) * HD
PH, NKEYS, TOPK = 8, 128, 16
NSETS = 2 * PH
EXPERTS = NKEYS * NKEYS
SLOTS = PH * TOPK
GS = 2
GROUPS = SLOTS // GS
QUARTERS = 4
QH = PH // QUARTERS
RING = 6
WC = 256
WRING = 3
BANKS = 6
NEG = -1.0e30
SIDE_PLACES = [(0, 1, 3, 4, 5), (1, 3, 5), (1, 3, 5), (0, 1, 3, 4, 5), (1, 3, 5), (1, 3, 5)]

BLOCKS = {"P": [0], "S": [1, 2]}
COND = [0, 1, 1]

SMALL, _at = {}, 0
for _name, _n in [("ident", P), ("ones", P), ("tri", 2 * P), ("mask", 2 * P), ("iota", TOPK), ("pick", 2),
                  ("cos", 2 * 32), ("sin", 2 * 32), ("cond", 2 * KC), ("ada_b", DEPTH * 48),
                  ("norm_g", DEPTH * 2 * KC), ("final_g", KC), ("head_g", KC), ("conv_w", 3 * KC),
                  ("conv_b", KC), ("gate_b", 16), ("q_g", HD), ("k_g", HD), ("m0", 8), ("w_gate", KC * 16)]:
    SMALL[_name] = (_at, _n)
    _at += _n
NSMALL = _at


def plan():
    def norm(l, w, g):
        for b in BLOCKS[g]:
            yield ("NORM", l, w, b)
            yield ("NT", l, w, b)

    def mlstm(g):
        nb = len(BLOCKS[g])
        yield from norm(0, 0, g)
        yield from (("MLQK", g, h) for h in range(2))
        for h in range(2):
            yield ("CONV", g, h)
            yield ("MLV", g, h)
        yield ("MLG", g)
        for d in range(2):
            order = list(range(nb))[::1 - 2 * d]
            for n, b in enumerate(order):
                yield ("MLA", g, d, b)
                yield ("MLB", g, d, b)
                if g == "P" or n < nb - 1:
                    yield ("MLC", g, d, b)
        yield ("MLN", g)
        yield from (("MLO", g, h) for h in range(2))
        yield ("T2", 0, g)
        yield from (("OUT", 0, g, h) for h in range(2))

    def attention(g):
        nb = len(BLOCKS[g])
        yield from norm(1, 0, g)
        yield from (("AQKV", g, h) for h in range(3))
        if g == "S":
            yield ("AC", g)
        yield from (("AN", g, b) for b in range(nb))
        yield from (("AT", g, b) for b in range(nb))
        yield from (("AS", g, b, kv) for b in range(nb) for kv in range(AKV))
        yield ("T2", 1, g)
        yield from (("OUT", 1, g, h) for h in range(2))

    def choice(l, g, b, quarters, queries):
        for q in quarters:
            if queries:
                yield ("PQ", l, g, q)
            yield from ((k, l, g, b, q) for k in ("PS", "PT", "PC", "PG"))

    def cost(s):
        both = "S" in s
        return {"MLQK": 13, "MLV": 13, "MLO": 13, "OUT": 13, "PQ": 13, "AQKV": 13, "AS": 11, "MOD": 10}.get(s[0], 0) / (2 - both) \
            or {"MLA": 8, "MLG": 8, "MLN": 10, "PS": 4, "PC": 5, "PG": 7, "PT": 5, "AN": 15, "CONV": 6, "NT": 4}.get(s[0], 6)

    def spread(l, b, steps):
        steps = list(steps)
        total = sum(cost(s) for s in steps)
        done = spent = 0
        chosen = QUARTERS - sum(s[0] == "PG" and (s[1], BLOCKS[s[2]][s[3]]) == (l, b) for s in steps)
        for s in steps:
            upto = min(int((GROUPS - 4) * spent / total), chosen * GROUPS // QUARTERS)
            if upto > done:
                yield ("GROUPS", l, b, done, upto)
                done = upto
            yield s
            spent += cost(s)
            chosen += s[0] == "PG" and (s[1], BLOCKS[s[2]][s[3]]) == (l, b)
        yield ("GATE", l, b)
        yield ("GROUPS", l, b, done, GROUPS)
        yield ("FIN", l, b)

    def between(steps, extra):
        for s in steps:
            if s in extra:
                yield extra[s]
            yield s

    yield ("INIT",)
    yield from (("MOD", 0, q) for q in range(2))
    yield from between(mlstm("P"), {("MLB", "P", 0, 0): ("MOD", 0, 2), ("MLC", "P", 0, 0): ("MOD", 0, 3),
                                    ("MLB", "P", 1, 0): ("MOD", 0, 4), ("MLC", "P", 1, 0): ("MOD", 0, 5)})
    yield from between(norm(0, 1, "P"), {("NT", 0, 1, 0): ("MOD", 1, 0)})
    for q in range(QUARTERS):
        yield ("PQ", 0, "P", q)
        yield ("PS", 0, "P", 0, q)
        if q == 2:
            yield from ((k, 0, "P", 0, 0) for k in ("PT", "PC", "PG"))
    first, others, every = range(1), range(1, QUARTERS), range(QUARTERS)
    later = list(mlstm("S"))
    quarter = {q: [(k, 0, "P", 0, q) for k in ("PT", "PC", "PG")] for q in others}
    start = [*quarter[1], *later[0:4], *quarter[2], later[4], *quarter[3], later[5], later[6]]
    later = [s for s in later if s not in start]
    yield from spread(0, 0, [*start, *later, *norm(0, 1, "S"), *choice(0, "S", 0, first, True)])
    yield from spread(0, 1, [*choice(0, "S", 0, others, True), *choice(0, "S", 1, every, False),
                             *(("MOD", 1, q) for q in range(1, 6))])
    yield from spread(0, 2, [*attention("P"), *norm(1, 1, "P"), *choice(1, "P", 0, every, True)])
    yield from spread(1, 0, [*attention("S"), *norm(1, 1, "S"), *choice(1, "S", 0, first, True)])
    yield from spread(1, 1, [*choice(1, "S", 0, others, True), *choice(1, "S", 1, every, False), ("FG",), ("YOUT", 0)])
    yield from spread(1, 2, [("YOUT", 1)])
    yield ("YOUT", 2)


PLAN = list(plan())


FIRST_SCORES = ("PS", 0, "P", 0, 0)


def in_order(who):
    late = {"P": (), "A": ("NT", "MLQK", "MLV", "MLO", "AQKV", "PQ", "OUT", "T2", "PS"),
            "D": ("NT", "MLQK", "MLV", "MLO", "AQKV", "PQ", "OUT", "T2", "PS", "MOD")}[who]
    order, i = [], 0
    while i < len(PLAN):
        if PLAN[i][0] in late and PLAN[i + 1][0] == "GROUPS":
            order += [i + 1, i]
            i += 2
        else:
            order.append(i)
            i += 1
    if who == "D":
        for k in ("PG", "PC", "PT"):
            i = PLAN.index((k, 0, "P", 0, 0))
            order.remove(i)
            order.insert(order.index(PLAN.index(FIRST_SCORES)) + 1, i)
    return order


def psum_tiles(s):
    k = s[0]
    nb = len(BLOCKS[s[1]]) if len(s) > 1 and s[1] in ("P", "S") else 0
    if k == "MOD":
        return "AADADADD"
    if k == "NT":
        return "AD"
    if k == "MLQK":
        return "AAAA"
    if k in ("MLV", "MLO", "AQKV"):
        return "A" * (2 * nb)
    if k == "MLG":
        return "DD"
    if k == "MLA":
        return "DDA"
    if k == "MLB":
        return "AD" * MH if s[1] == "S" else "D" * MH
    if k == "MLC":
        return "D" * (1 + MH)
    if k == "T2":
        return "A" * (2 * len(BLOCKS[s[2]]) + 2)
    if k == "OUT":
        return "D" * (2 * len(BLOCKS[s[2]]))
    if k == "PQ":
        return "AAAA"
    if k == "PS":
        return "D" if s[4] else "DAA"
    if k == "AC":
        return "A"
    if k == "AT":
        return "AAA"
    if k == "AS":
        return "AAAADDDDD"
    if k in ("GATE", "FG"):
        return "AA"
    return ""


MOD_ROWS, MOD_COLUMNS = (0, 1, 3, 5), (2, 4, 6, 7)


def weight_tiles(s, A):
    k = s[0]

    def cols(w, first, n, per):
        w = w.rearrange("(k p) n -> p k n", p=P)
        return [(w[:, :, (first + j) * WC:(first + j + 1) * WC], per * (j + 1) - 1) for j in range(n)]

    if k == "MOD":
        w = A["ada_w"][s[1]].rearrange("(p k) n -> p k n", p=P)
        return [(w[:, :, (4 * s[2] + j) * WC:(4 * s[2] + j + 1) * WC], MOD_ROWS[j]) for j in range(4)]
    if k == "MLQK":
        return cols(A["mlstm_w_in"][0], 2 * s[2], 2, 2)
    if k == "MLV":
        return cols(A["mlstm_w_in"][0], 4 + 2 * s[2], 2, len(BLOCKS[s[1]]))
    if k == "MLO":
        return cols(A["mlstm_w_in"][0], 8 + 2 * s[2], 2, len(BLOCKS[s[1]]))
    if k == "AQKV":
        return cols(A["attn_w_qkv"][0], 2 * s[2], 2, len(BLOCKS[s[1]]))
    if k == "OUT":
        w = A["mlstm_w_out"] if s[1] == 0 else A["attn_w_out"]
        return cols(w[0], 2 * s[3], 2, len(BLOCKS[s[2]]))
    if k == "PQ":
        return cols(A["peer_w_q"][s[1]], 2 * s[3], 2, 2)
    if k == "PS":
        n = 2 * QH * NKEYS
        return [(A["subkeys"][s[1], :, s[4] * n:(s[4] + 1) * n], 0)]
    return []


def weight_loads(A):
    loads, turns, free_at, tiles = [], {}, {}, 0
    last_early = PLAN.index(("PS", 0, "P", 0, QUARTERS - 1))
    for i, s in enumerate(PLAN):
        for src, last in weight_tiles(s, A):
            n = len(loads)
            place = n % (WRING + RING * GS) if i <= last_early else n % WRING
            turns[place] = turns.get(place, 0) + 1
            loads.append((src, place, turns[place], free_at.get(place, 0)))
            free_at[place] = tiles + last + 1
        tiles += len(psum_tiles(s))
    return loads, free_at


ACT_ENDS = ("INIT", "CONV")
IDLE = {"P": ("INIT", "NORM", "CONV", "MLN", "PT", "PC", "PG", "AN", "FIN", "YOUT"), "A": ("PT", "PC", "OUT", "FIN"),
        "D": ("INIT", "MLQK", "PQ", "AQKV", "T2", "AC", "GATE", "FG")}


def dve_ends(s):
    return s[0] in ("MLV", "MLG", "MLB", "MLN", "MLO", "OUT", "PT", "PC", "PG", "AN", "FIN", "YOUT", "NORM") \
        or (s[0] == "MOD" and s[2] in (1, 4))


def needed(i, who):
    s = PLAN[i]

    def after(*kinds):
        return max(j for j in range(i) if PLAN[j][0] in kinds) + 1

    if s in [(k, *FIRST_SCORES[1:]) for k in ("PT", "PC", "PG")]:
        return PLAN.index(FIRST_SCORES) + 1
    if s[0] in ("MLQK", "MLV", "MLG", "PQ", "AQKV"):
        return after("NT")
    if s[0] == "MOD":
        return after("INIT")
    if s[0] == "MLO" and who == "P":
        return after("NT")
    if s[0] == "OUT" and who == "P":
        return after("T2")
    if s[0] == "PS" and who != "D":
        return after("PQ")
    if s[0] == "AS" and who == "P":
        return after("AT")
    return i


def has_side(order, ring):
    return ring in SIDE_PLACES[order]


def side_sums(n):
    return sum(has_side(g // GROUPS, g % RING) for g in range(n))


def trunk(nc, A, O):
    ctx = ExitStack()
    with ctx:
        def sb(name, shape, dt=F32):
            return ctx.enter_context(nc.sbuf_tensor(name, shape, dt))

        def sem(name):
            return ctx.enter_context(nc.semaphore(name))

        rows = sb("rows", [P, RING * GS, 2 * D])
        wt = sb("wt", [P, WRING, KC * WC])
        x = sb("x", [P, 3, D])
        xb = sb("xb", [P, 2, D])
        hT = sb("hT", [P, KC, 2 * P])
        small = sb("small", [P, NSMALL])
        diag = sb("diag", [P, RING * GS, P])
        eidx = sb("eidx", [P, 3, SLOTS], U32)
        gate = sb("gate", [P, 3, SLOTS])
        act_in = sb("act_in", [P, RING, GS])
        act_out = sb("act_out", [P, RING, GS])
        wv = sb("wv", [P, RING, GS])
        cs = sb("cs", [P, KC, 32])
        side = sb("side", [P, D])
        modT = sb("modT", [P, DEPTH, 48, 2])
        gain = sb("gain", [P, DEPTH, 2, KC, 2])
        mod_rows = sb("mod_rows", [P, 2, WC])
        st = sb("st", [P, 256])
        ARENA = 8220
        arena = sb("arena", [P, ARENA])

        def cst(name):
            a, n = SMALL[name]
            return small[:, a:a + n]

        ident, ones = cst("ident"), cst("ones")
        tri = cst("tri").rearrange("p (d n) -> p d n", d=2)
        mask = cst("mask").rearrange("p (d n) -> p d n", d=2)
        norm_g = cst("norm_g").rearrange("p (l w k) -> p l w k", l=DEPTH, w=2)
        ada_b = cst("ada_b").rearrange("p (l n) -> p l n", l=DEPTH)
        conv_w = cst("conv_w").rearrange("p (f j) -> p f j", j=3)
        w_gate = cst("w_gate").rearrange("p (k n) -> p k n", k=KC)

        def area(at, *shape):
            n = 1
            for v in shape:
                n *= v
            assert at + n <= ARENA, (at, shape)
            a = arena[:, at:at + n]
            if len(shape) == 2:
                a = a.rearrange("p (a b) -> p a b", b=shape[1])
            if len(shape) == 3:
                a = a.rearrange("p (a b c) -> p a b c", b=shape[1], c=shape[2])
            return a, at + n

        xn, at = area(0, D)
        raw, _ = area(at, KC, 2 * P + 2)
        hm, _ = area(at, 2, D)
        at += KC * (2 * P + 2)
        cv, at = area(at, KC, 2 * P)
        va, at = area(at, 2, MH, DV + 1)
        Cst, at = area(at, MH, DV + 1)
        W = xn[:, 0:512].rearrange("p (h n) -> p h n", n=P)
        WT = xn[:, 512:1024].rearrange("p (h n) -> p h n", n=P)
        Nn = sb("Nn", [P, MH, DV + 1])
        Nflat = Nn[:].rearrange("p a b -> p (a b)")
        gbc = Nflat[:, 0:D]
        final_gain = hT[:].rearrange("p a b -> p (a b)")[:, 0:D]
        def normed(s):
            return xb[:, 1, :] if s[1:3] == (0, 0) and s[3] > 0 else xn

        qkv, at = area(D, 2, QKV)
        qTa, at = area(at, AH // 2, 2 * P)
        kTa, at = area(at, AKV, 3 * P)
        kdup, at = area(at, AKV, 2, HD)
        vc = xn[:, 3 * 2 * P:D].rearrange("p (v n) -> p v n", n=HD)
        sq20 = area(D + 2 * QKV, 20 * HD)[0]
        prA = [hT[:].rearrange("p a b -> p (a b)")[:, i * 3 * P:(i + 1) * 3 * P] for i in range(4)]
        pTa = [xn[:, i * 3 * P:(i + 1) * 3 * P] for i in range(2)]
        qTp, at = area(D, NSETS, 2 * P)
        sc, at = area(at, NSETS, NKEYS)
        cand, at = area(at, PH // 2, TOPK * TOPK)
        top1 = Nflat[:, 0:256].rearrange("p (s k) -> p s k", k=TOPK)
        i1f = Nflat[:, 256:512].rearrange("p (s k) -> p s k", k=TOPK)
        topc = Nflat[:, 512:640].rearrange("p (s k) -> p s k", k=TOPK)
        pij = Nflat[:, 640:896].rearrange("p (a s) -> p a s", a=2)
        i1u = xn[:, 0:256].bitcast(U32).rearrange("p (s k) -> p s k", k=TOPK)
        posu = xn[:, 256:384].bitcast(U32).rearrange("p (s k) -> p s k", k=TOPK)
        piju = xn[:, 384:640].bitcast(U32).rearrange("p (a s) -> p a s", a=2)
        e12 = xn[:, 640:896].rearrange("p (a s) -> p a s", a=2)

        def cols(a, n):
            return st[:, a:a + n]
        ssq, ms, sd, rstd = (cols(i * 20, 20) for i in range(4))
        ig = cols(80, 16).rearrange("p (b d h) -> p b d h", b=2, d=2)
        nlf = cols(96, 16).rearrange("p (b d h) -> p b d h", b=2, d=2)
        bt = cols(112, 32).rearrange("p (b n) -> p b n", b=2)
        rcol = cols(144, 16).rearrange("p (b d h) -> p b d h", b=2, d=2)
        mst = cols(160, 8).rearrange("p (d h) -> p d h", d=2)
        rall, rmx, nMp = cols(168, 4), cols(172, 4), cols(176, 4)
        t12, ae = cols(180, 8), cols(188, 8)
        dww, dw = cols(196, 8), cols(204, 8)
        den, rden = cols(212, 4), cols(216, 4)
        mpp = cols(220, 4)
        smx, nsmx, rsum, rrs = cols(224, 4), cols(228, 4), cols(232, 4), cols(236, 4)
        gsum, grec = cols(240, 8), cols(248, 8)
        gtmp = xn[:, 0:128].rearrange("p (a n) -> p a n", a=4)
        gates_all = gtmp[:, 0].rearrange("p (b n) -> p b n", b=2)

        acc = ctx.enter_context(nc.psum_tensor("acc", [P, D], F32))
        banks = [ctx.enter_context(nc.psum_tensor(f"bank{i}", [P, 512], F32)) for i in range(BANKS)]

        inputs_in = sem("inputs_in")
        w_in = [sem(f"weights_in{i}") for i in range(WRING + RING * GS)]
        loads, last_use = weight_loads(A)
        rows_in = [sem(f"rows_in{i}") for i in range(RING * GS)]
        tile_full = sem("tile_full")
        act_freed, dve_freed = sem("act_emptied_tile"), sem("dve_emptied_tile")
        freed = {"A": act_freed, "D": dve_freed}
        act_step, dve_step = sem("act_step"), sem("dve_step")
        act_chain, dve_chain = sem("act_chain"), sem("dve_chain")
        zeroed = sem("zeroed")
        squares, mean_sq, root = sem("squares"), sem("mean_sq"), sem("root")
        convolved, abs_gate, soft_gate, log_gate = sem("convolved"), sem("abs_gate"), sem("soft_gate"), sem("log_gate")
        decay_rows, maxima, probs_raw = sem("decay_rows"), sem("maxima"), sem("probs_raw")
        carry_in, carry_exp, state_in, state_out = sem("carry_in"), sem("carry_exp"), sem("state_in"), sem("state_out")
        key_pairs, cache_in, row_max, kv_done = sem("key_pairs"), sem("cache_in"), sem("row_max"), sem("kv_done")
        tops, top_exp, experts_chosen = sem("tops"), sem("top_exp"), sem("experts_chosen")
        dots, gelus, weighted, diags, summed = sem("dots"), sem("gelus"), sem("weighted"), sem("diags"), sem("summed")
        side_summed, side_zero = sem("side_summed"), sem("side_zero")
        sum_read, y_done, stored = sem("sum_read"), sem("y_done"), sem("stored")

        def places(who):
            owner, seen = [], {}
            place = {"first": 0, "chain": 0}
            before = []
            total = {"A": 0, "D": 0, "acts": 0, "dves": 0}
            for s in PLAN:
                before.append((len(owner), total["A"], total["D"], total["acts"], total["dves"]))
                for e in psum_tiles(s):
                    total[e] += 1
                    owner.append((e, total[e]))
                total["acts"] += s[0] in ACT_ENDS
                total["dves"] += dve_ends(s)

            def begin(i):
                place["first"] = before[i][0]
                s = PLAN[i]
                if s[0] in (*IDLE[who], "GROUPS") or (s[0] == "PS" and who == "A" and s[4]):
                    return 0, 0, 0, 0, 0
                counts = before[needed(i, who)]
                return (0, counts[1], 0, 0, 0) if s[0] == "PS" and who == "P" else counts

            def tile(j):
                return banks[(place["first"] + j) % BANKS]

            def full(j):
                return place["first"] + j + 1

            def by(j):
                return freed[owner[place["first"] + j][0]]

            def emptied(j):
                return owner[place["first"] + j][1]

            def next_of(sem, k=1):
                key = id(sem)
                seen[key] = seen.get(key, 0) + k
                return seen[key]

            def one():
                place["chain"] += 1
                return 1

            def noted():
                return place["chain"]

            return begin, tile, full, by, emptied, next_of, one, noted

        def weight_place(i):
            a = wt[:, i, :] if i < WRING else rows[:, i - WRING, :]
            return a.rearrange("p (k n) -> p k n", k=KC)

        def tok(b):
            return slice(b * P, (b + 1) * P)

        GORDER = [(0, 0), (0, 1), (0, 2), (1, 0), (1, 1), (1, 2)]

        def run_groups(eng, s, body, last_ones):
            _, l, b, lo, hi = s
            order = GORDER.index((l, b))
            base = order * GROUPS

            def straight(g0, g1):
                for g in range(g0, g1):
                    n = base + g
                    body(order, n, g * GS, n % RING, n // RING, g)

            g = lo
            if g < 3:
                straight(g, min(3, hi))
                g = min(3, hi)
            whole = (hi - g) // RING
            if whole >= 2:
                with eng.Fori(0, whole) as i:
                    for k in range(RING):
                        n = base + g + k
                        body(order, i * RING + n, i * (RING * GS) + (g + k) * GS, n % RING, i + n // RING, None)
                g += whole * RING
            straight(g, hi)
            if hi == GROUPS:
                last_ones(order, base + GROUPS)

        block = ctx.enter_context(nc.Block())

        @block.sync
        def _(sp):
            sp.dma_start(small[:], A["small"]).then_inc(inputs_in, 16)
            sp.dma_start(x[:, 0, :], A["x_prompt"][0]).then_inc(inputs_in, 16)
            sp.dma_start(x[:, 1:3, :], A["x_sample"][0].rearrange("(b p) n -> p b n", p=P)).then_inc(inputs_in, 16)
            for src, place, turn, free in loads:
                if free:
                    sp.wait_ge(tile_full, free)
                to = weight_place(place)
                if len(src.shape) == 2:
                    to = to.rearrange("p k n -> p (k n)")[:, 0:src.shape[1]]
                sp.dma_start(to, src).then_inc(w_in[place], 16)

        @block.gpsimd
        def _(pool):
            for n, (l, b) in enumerate(GORDER):
                for g in range(n * GROUPS, (n + 1) * GROUPS):
                    if g % (GROUPS // QUARTERS) == 0:
                        pool.wait_ge(experts_chosen, g // (GROUPS // QUARTERS) + 1)
                    if g >= RING:
                        pool.wait_ge(summed, g - RING + 1)
                        if side_sums(g - RING + 1):
                            pool.wait_ge(side_summed, side_sums(g - RING + 1))
                    for j in range(GS):
                        r = (g % RING) * GS + j
                        slot = (g - n * GROUPS) * GS + j
                        if g < RING:
                            pool.wait_ge(tile_full, last_use[WRING + r])
                        nc.gpsimd.indirect_dma_start(
                            out=rows[:, r, :], out_offset=None, in_=A["uv"],
                            in_offset=bass.IndirectOffsetOnAxis(ap=eidx[:, b, slot:slot + 1], axis=0))\
                            .then_inc(rows_in[r], 16)

        @block.tensor
        def _(pe):
            begin, tile, full, by, emptied, next_of, one, noted = places("P")
            used = [0]

            def open_tile(j):
                if full(j) > BANKS:
                    pe.wait_ge(by(j - BANKS), emptied(j - BANKS))
                return tile(j)

            def mm(out, lhsT, rhs, start, stop):
                return nc.tensor.matmul(out, lhsT, rhs, start=start, stop=stop)

            def weights():
                _, place, turn, _ = loads[used[0]]
                used[0] += 1
                pe.wait_ge(w_in[place], 16 * turn)
                return weight_place(place)

            def product(out, lhs, rhs):
                for k in range(KC):
                    last = mm(out, lhs(k), rhs(k), k == 0, k == KC - 1)
                return last

            def transposes(out, ins):
                for i, a in enumerate(ins):
                    last = nc.tensor.transpose(out[:, i * P:(i + 1) * P], a, ident)
                return last

            def by_token(n_tiles, blocks):
                for j in range(n_tiles):
                    w = weights()
                    for b in range(blocks):
                        t = open_tile(j * blocks + b)
                        product(t[:, 0:WC], lambda k: hT[:, k, tok(b)], lambda k: w[:, k, :]).then_inc(tile_full, 1)

            def by_feature(n_tokens):
                for j in range(2):
                    w = weights()
                    for i in range(2):
                        t = open_tile(2 * j + i)
                        product(t[:, 0:n_tokens], lambda k: w[:, k, i * P:(i + 1) * P],
                                lambda k: hT[:, k, 0:n_tokens]).then_inc(tile_full, 1)

            def on_all_partitions(j, column):
                for i in range(2):
                    t = open_tile(j + i)
                    for k in range(4):
                        last = mm(t[:, k * P:(k + 1) * P], column(4 * i + k).to_broadcast([P, P]), ident, True, True)
                    last.then_inc(tile_full, 1)

            def add_up(order, n, ring, first):
                pe.wait_ge(diags, n + 1)
                for j in range(GS - has_side(order, ring)):
                    r = ring * GS + j
                    for h in range(2):
                        last = nc.tensor.matmul(acc[:, h * 512:(h + 1) * 512], diag[:, r, :],
                                                rows[:, r, D + h * 512:D + (h + 1) * 512],
                                                start=first and j == 0, stop=True, skip_group_check=True)
                last.then_inc(summed, 1)

            def group(order, n, slot, ring, turn, g):
                if g == 2 and n >= GROUPS:
                    pe.wait_ge(sum_read, n // GROUPS)
                if g is None or g >= 2:
                    add_up(order, n - 2, (ring - 2) % RING, g == 2)

            def last_groups(order, n):
                add_up(order, n - 2, (n - 2) % RING, False)
                add_up(order, n - 1, (n - 1) % RING, False)

            pe.wait_ge(inputs_in, 48)
            for n_entry in in_order("P"):
                s = PLAN[n_entry]
                k = s[0]
                tiles, by_act, by_dve, acts, dves = begin(n_entry)
                if by_act:
                    pe.wait_ge(act_freed, by_act)
                if by_dve:
                    pe.wait_ge(dve_freed, by_dve)
                if acts:
                    pe.wait_ge(act_step, acts)
                if dves:
                    pe.wait_ge(dve_step, dves)
                if k == "GROUPS":
                    run_groups(pe, s, group, last_groups)
                    continue
                if k == "MOD":
                    for j in range(5):
                        if j < 4:
                            w = weights()
                            t = open_tile(MOD_ROWS[j])
                            for q in range(KC):
                                c = slice(32 * (q % 4), 32 * (q % 4) + 32)
                                last = mm(t[c, 0:WC], cs[:, q, :], w[:, q, :], q < 4, q >= 4)
                            last.then_inc(tile_full, 1)
                        if j:
                            t = open_tile(MOD_COLUMNS[j - 1])
                            pe.wait_ge(by(MOD_ROWS[j - 1]), emptied(MOD_ROWS[j - 1]))
                            for i in range(2):
                                last = mm(t[:, 2 * i:2 * i + 2], mod_rows[:, (j - 1) % 2, i * P:(i + 1) * P], cst("pick"), True, True)
                            last.then_inc(tile_full, 1)
                elif k == "NT":
                    for i in range(2):
                        transposes(open_tile(i), [normed(s)[:, (4 * i + q) * P:(4 * i + q + 1) * P] for q in range(4)])\
                            .then_inc(tile_full, 1)
                elif k == "MLQK":
                    by_feature(P * len(BLOCKS[s[1]]))
                elif k in ("MLV", "MLO", "AQKV"):
                    by_token(2, len(BLOCKS[s[1]]))
                elif k == "OUT":
                    by_token(2, len(BLOCKS[s[2]]))
                elif k == "MLG":
                    nb = len(BLOCKS[s[1]])
                    t = open_tile(0)
                    for b in range(nb):
                        last = product(t[:, b * 16:b * 16 + 16], lambda q: hT[:, q, tok(b)], lambda q: w_gate[:, q, :])
                    last.then_inc(tile_full, 1)
                    pe.wait_ge(log_gate, next_of(log_gate))
                    t = open_tile(1)
                    for b in range(nb):
                        for d in range(2):
                            mm(t[:, b * 16 + d * 4:b * 16 + d * 4 + 4], tri[:, d, :], nlf[:, b, d, :], True, True)
                        last = mm(t[:, b * 16 + 8:b * 16 + 16], ones, nlf[:, b].rearrange("p d h -> p (d h)"), True, True)
                    last.then_inc(tile_full, 1)
                elif k == "MLA":
                    _, g, d, b = s
                    pe.wait_ge(decay_rows, next_of(decay_rows))
                    t = open_tile(0)
                    mm(t[:], ones, W.rearrange("p h n -> p (h n)"), True, True).then_inc(tile_full, 1)
                    t = open_tile(1)
                    for h in range(MH):
                        last = mm(t[:, h * P:(h + 1) * P], cv[:, h, tok(b)], cv[:, 4 + h, tok(b)], True, True)
                    last.then_inc(tile_full, 1)
                    pe.wait_ge(by(1), emptied(1))
                    transposes(open_tile(2), [W[:, h, :] for h in range(MH)]).then_inc(tile_full, 1)
                elif k == "MLB":
                    _, g, d, b = s
                    per = 2 if g == "S" else 1
                    if g == "S" and b == d:
                        pe.wait_ge(state_in, next_of(state_in, 32))
                    for h in range(MH):
                        if g == "S":
                            t = open_tile(per * h)
                            mm(t[:, 0:DV + 1], cv[:, h, tok(b)], Cst[:, h, :], True, True).then_inc(tile_full, 1)
                        t = open_tile(per * h + per - 1)
                        mm(t[:, 0:DV + 1], WT[:, h, :], va[:, b, h, :], True, True).then_inc(tile_full, 1)
                elif k == "MLC":
                    _, g, d, b = s
                    transposes(open_tile(0), [cv[:, 4 + h, tok(b)] for h in range(MH)]).then_inc(tile_full, 1)
                    pe.wait_ge(by(0), emptied(0))
                    for h in range(MH):
                        t = open_tile(1 + h)
                        mm(t[:, 0:DV + 1], W[:, h, :], va[:, b, h, :], True, True).then_inc(tile_full, 1)
                elif k == "T2":
                    _, l, g = s
                    src = hm if l == 0 else qkv
                    for b in range(len(BLOCKS[g])):
                        for i in range(2):
                            transposes(open_tile(2 * b + i),
                                       [src[:, b, (4 * i + q) * P:(4 * i + q + 1) * P] for q in range(4)])\
                                .then_inc(tile_full, 1)
                    c = COND[BLOCKS[g][0]]
                    on_all_partitions(2 * len(BLOCKS[g]), lambda q: modT[:, l, 16 + q, c:c + 1])
                elif k == "PQ":
                    by_feature(P * len(BLOCKS[s[2]]))
                elif k == "PS":
                    _, l, g, b, part = s
                    w = weights().rearrange("p k n -> p (k n)")
                    t = open_tile(0)
                    for q in range(2 * QH):
                        last = mm(t[:, q * P:(q + 1) * P], qTp[:, 2 * QH * part + q, tok(b)], w[:, q * NKEYS:(q + 1) * NKEYS], True, True)
                    last.then_inc(tile_full, 1)
                    if part == 0:
                        for i in range(2):
                            transposes(open_tile(1 + i), [hT[:, 4 * i + q, tok(b)] for q in range(4)]).then_inc(tile_full, 1)
                elif k == "AC":
                    pe.wait_ge(cache_in, next_of(cache_in, 48))
                    transposes(open_tile(0), [kdup[:, v, :, :].rearrange("p a n -> p (a n)") for v in range(AKV)])\
                        .then_inc(tile_full, 1)
                elif k == "AT":
                    _, g, b = s
                    for i in range(2):
                        transposes(open_tile(i), [qkv[:, b, (4 * i + q) * P:(4 * i + q + 1) * P] for q in range(4)])\
                            .then_inc(tile_full, 1)
                    pe.wait_ge(key_pairs, next_of(key_pairs))
                    transposes(open_tile(2), [kdup[:, v, :, :].rearrange("p a n -> p (a n)") for v in range(AKV)])\
                        .then_inc(tile_full, 1)
                elif k == "AS":
                    _, g, b, kv = s
                    nk = 1 if g == "P" else 3
                    for i in range(4):
                        h = kv * 4 + i
                        half = slice((h % 2) * HD, (h % 2 + 1) * HD)
                        t = open_tile(i)
                        mm(t[:, 0:nk * P], qTa[half, h // 2, tok(b)], kTa[half, kv, 0:nk * P], True, True)\
                            .then_inc(tile_full, 1)

                    def values(i):
                        pe.wait_ge(by(4 + i), emptied(4 + i))
                        for c in range(nk):
                            v = vc[:, kv, :] if nk == 3 and c == 0 else \
                                qkv[:, c - (nk == 3), (AH + AKV + kv) * HD:(AH + AKV + kv + 1) * HD]
                            last = mm(out[:, i * HD:(i + 1) * HD], pTa[i % 2][:, c * P:(c + 1) * P], v,
                                      c == 0, c == nk - 1)
                        return last

                    out = open_tile(8)
                    for i in range(4):
                        t = open_tile(4 + i)
                        pe.wait_ge(by(i), emptied(i))
                        transposes(t, [prA[i][:, c * P:(c + 1) * P] for c in range(nk)]).then_inc(tile_full, 1)
                        if i:
                            values(i - 1)
                    values(3).then_inc(tile_full, 1)
                elif k == "GATE":
                    c = COND[s[2]]
                    on_all_partitions(0, lambda q: modT[:, s[1], 40 + q, c:c + 1])
                elif k == "FG":
                    on_all_partitions(0, lambda q: cst("final_g")[:, q:q + 1])

        @block.scalar
        def _(act):
            begin, tile, full, by, emptied, next_of, one, noted = places("A")
            sent = {"stored": 0, "state_out": 0}

            def f(out, in_, func, **kw):
                return nc.scalar.activation(out, in_, func, **kw)

            def copy_tile(j, out, n=512, view=None):
                act.wait_ge(tile_full, full(j))
                t = tile(j)[:, 0:n]
                f(out, view(t) if view else t, ACT.Copy).then_inc(act_freed, 1)

            def rsqrt_parts(src, out=xn):
                f(out, src, ACT.Square, accum_out=ssq[:, 0:1]).then_inc(squares, 1)
                act.wait_ge(mean_sq, next_of(mean_sq))
                f(sd[:, 0:1], ms[:, 0:1], ACT.Sqrt).then_inc(root, 1)

            def diagonals(order, n, ring):
                act.wait_ge(weighted, n + 1)
                for j in range(GS - has_side(order, ring)):
                    last = f(diag[:, ring * GS + j, :], ident, ACT.Copy, scale=wv[:, ring, j:j + 1])
                last.then_inc(diags, 1)

            def group(order, n, slot, ring, turn, g):
                act.wait_ge(dots, n + 1)
                f(act_out[:, ring, :], act_in[:, ring, :], ACT.Gelu).then_inc(gelus, 1)
                if g != 0:
                    diagonals(order, n - 1, (ring - 1) % RING)

            def last_groups(order, n):
                diagonals(order, n - 1, (n - 1) % RING)

            def store(out, in_):
                act.dma_start(out, in_).then_inc(stored, 16)
                sent["stored"] += 1

            act.wait_ge(inputs_in, 48)
            for n_entry in in_order("A"):
                s = PLAN[n_entry]
                k = s[0]
                tiles, by_act, by_dve, acts, dves = begin(n_entry)
                if tiles:
                    act.wait_ge(tile_full, tiles)
                if by_act:
                    act.wait_ge(act_freed, by_act)
                if by_dve:
                    act.wait_ge(dve_freed, by_dve)
                if acts:
                    act.wait_ge(act_step, acts)
                if dves:
                    act.wait_ge(dve_step, dves)
                if k == "GROUPS":
                    run_groups(act, s, group, last_groups)
                    continue
                if noted():
                    act.wait_ge(act_chain, noted())
                if k == "INIT":
                    act.wait_ge(zeroed, 1)
                    f(cs[:, :, 0:2], cst("cond").rearrange("p (k c) -> p k c", c=2), ACT.Silu).then_inc(act_step, 1)
                elif k == "MOD":
                    for j in range(4):
                        act.wait_ge(tile_full, full(MOD_ROWS[j]))
                        t = tile(MOD_ROWS[j])
                        f(mod_rows[:, j % 2, :], t[:, 0:WC], ACT.Copy).then_inc(act_freed, 1)
                elif k == "NORM":
                    rsqrt_parts(x[:, s[3], :], normed(s))
                elif k == "NT":
                    _, l, w, b = s
                    c = COND[b]
                    act.wait_ge(tile_full, full(0))
                    t = tile(0)
                    place = tok(b - (b > 0))
                    for q in range(4):
                        last = f(hT[:, q, place], t[:, q * P:(q + 1) * P], ACT.Identity,
                                 scale=gain[:, l, w, q, c:c + 1], bias=modT[:, l, 24 * w + q, c:c + 1])
                    last.then_inc(act_freed, 1)
                elif k == "MLQK":
                    _, g, half = s
                    n = P * len(BLOCKS[g])
                    for i in range(4):
                        copy_tile(i, raw[:, 4 * half + i, 1:n + 1], n)
                elif k == "CONV":
                    _, g, half = s
                    n = P * len(BLOCKS[g])
                    for i in range(4):
                        e = 4 * half + i
                        act.wait_ge(convolved, next_of(convolved))
                        last = f(cv[:, e, 0:n], cv[:, e, 0:n], ACT.Silu, bias=cst("conv_b")[:, e:e + 1])
                    last.then_inc(act_step, 1)
                elif k == "MLV":
                    _, g, half = s
                    nb = len(BLOCKS[g])
                    for j in range(2):
                        for b in range(nb):
                            copy_tile(j * nb + b, va[:, b, 2 * half + j, 0:DV], WC)
                elif k == "MLG":
                    n = 8 * len(BLOCKS[s[1]])
                    act.wait_ge(abs_gate, next_of(abs_gate))
                    f(gtmp[:, 2, 0:n], gtmp[:, 1, 0:n], ACT.Exp, scale=-1.0).then_inc(act_chain, one())
                    act.wait_ge(act_chain, noted())
                    f(gtmp[:, 3, 0:n], gtmp[:, 2, 0:n], ACT.Ln, bias=1.0).then_inc(soft_gate, 1)
                elif k == "MLA":
                    _, g, d, b = s
                    if g == "S" and b == d:
                        act.dma_start(Cst[:, :, 0:DV], A["state_mlstm_C"][0, 0, d].rearrange("h p v -> p h v"))\
                            .then_inc(state_in, 16)
                        act.dma_start(Cst[:, :, DV], A["state_mlstm_n"][0, 0, d].rearrange("h p -> p h"), allow_slow_non_contiguous=True)\
                            .then_inc(state_in, 16)
                    act.wait_ge(maxima, next_of(maxima))
                    f(ae, t12, ACT.Exp).then_inc(act_chain, one())
                    for h in range(MH):
                        last = f(W[:, h, :], W[:, h, :], ACT.Exp, bias=nMp[:, h:h + 1])
                    last.then_inc(probs_raw, 1)
                    copy_tile(2, WT.rearrange("p h n -> p (h n)"))
                elif k == "MLB":
                    if s[1] == "S":
                        act.wait_ge(act_chain, noted())
                        for h in range(MH):
                            act.wait_ge(tile_full, full(2 * h))
                            t = tile(2 * h)
                            f(Nn[:, h, :], t[:, 0:DV + 1], ACT.Copy, scale=ae[:, h:h + 1]).then_inc(act_freed, 1)
                elif k == "MLC":
                    _, g, d, b = s
                    act.wait_ge(carry_in, next_of(carry_in))
                    f(dw, dww, ACT.Exp).then_inc(carry_exp, 1)
                    if g == "P":
                        act.wait_ge(by(MH), emptied(MH))
                        act.dma_start(O["new_C"][0, 0, d].rearrange("h p v -> p h v"), Cst[:, :, 0:DV]).then_inc(state_out, 16)
                        act.dma_start(O["new_n"][0, 0, d].rearrange("h p -> p h"), Cst[:, :, DV], allow_slow_non_contiguous=True).then_inc(state_out, 16)
                        act.dma_start(O["new_m"][0, 0, d:d + 1, :], mst[0:1, d, :]).then_inc(state_out, 16)
                        sent["state_out"] += 3
                elif k == "MLN":
                    for b in range(len(BLOCKS[s[1]])):
                        act.wait_ge(mean_sq, next_of(mean_sq))
                        f(sd[:, 0:MH], ms[:, 0:MH], ACT.Sqrt).then_inc(root, 1)
                elif k == "MLO":
                    nb = len(BLOCKS[s[1]])
                    for i in range(2 * nb):
                        act.wait_ge(tile_full, full(i))
                        t = tile(i)
                        f(Nflat[:, i * WC:(i + 1) * WC], t[:, 0:WC], ACT.Sigmoid).then_inc(act_freed, 1)
                elif k == "T2":
                    _, l, g = s
                    nb = len(BLOCKS[g])
                    for b in range(nb):
                        for i in range(2):
                            act.wait_ge(tile_full, full(2 * b + i))
                            t = tile(2 * b + i)
                            if l == 0:
                                for q in range(4):
                                    last = f(hT[:, 4 * i + q, tok(b)], t[:, q * P:(q + 1) * P], ACT.Copy,
                                             scale=cst("head_g")[:, 4 * i + q:4 * i + q + 1])
                            else:
                                last = f(hT[:, 4 * i:4 * i + 4, tok(b)], t[:].rearrange("p (q n) -> p q n", n=P), ACT.Copy)
                            last.then_inc(act_freed, 1)
                    for i in range(2):
                        copy_tile(2 * nb + i, gbc[:, i * 512:(i + 1) * 512])
                elif k == "PQ":
                    _, l, g, q = s
                    n = P * len(BLOCKS[g])
                    for i in range(4):
                        copy_tile(i, qTp[:, 4 * q + i, 0:n], n)
                elif k == "PS":
                    _, l, g, b, part = s
                    for i in range(2 * (part == 0)):
                        copy_tile(1 + i, xb[:, GORDER.index((l, BLOCKS[g][b])) % 2, i * 512:(i + 1) * 512])
                elif k == "PG":
                    tc = topc[:, s[4] * QH:(s[4] + 1) * QH, :]
                    act.wait_ge(tops, next_of(tops))
                    f(tc, tc, ACT.Exp).then_inc(top_exp, 1)
                elif k == "AQKV":
                    _, g, third = s
                    nb = len(BLOCKS[g])
                    for j in range(2):
                        for b in range(nb):
                            c = (2 * third + j) * WC
                            copy_tile(j * nb + b, qkv[:, b, c:c + WC], WC)
                elif k == "AN":
                    _, g, b = s
                    act.wait_ge(mean_sq, next_of(mean_sq))
                    f(sd[:], ms[:], ACT.Sqrt).then_inc(root, 1)
                    if g == "P":
                        act.wait_ge(kv_done, next_of(kv_done))
                        store(O["new_k"][0, 0].rearrange("v t n -> t v n"),
                              qkv[:, 0, AH * HD:(AH + AKV) * HD].rearrange("p (v n) -> p v n", n=HD))
                        store(O["new_v"][0, 0].rearrange("v t n -> t v n"),
                              qkv[:, 0, (AH + AKV) * HD:].rearrange("p (v n) -> p v n", n=HD))
                elif k == "AC":
                    for a in range(2):
                        act.dma_start(kdup[:, :, a, :], A["cache_attn_k"][0, 0].rearrange("v t n -> t v n")).then_inc(cache_in, 16)
                    act.dma_start(vc, A["cache_attn_v"][0, 0].rearrange("v t n -> t v n")).then_inc(cache_in, 16)
                    copy_tile(0, kTa[:, :, 0:P], 512, lambda t: t.rearrange("p (v n) -> p v n", n=P))
                elif k == "AT":
                    _, g, b = s
                    for i in range(2):
                        copy_tile(i, qTa[:, 4 * i:4 * i + 4, tok(b)], 512, lambda t: t.rearrange("p (q n) -> p q n", n=P))
                    copy_tile(2, kTa[:, :, tok(b + (g == "S"))], 512, lambda t: t.rearrange("p (v n) -> p v n", n=P))
                elif k == "AS":
                    _, g, b, kv = s
                    n = P if g == "P" else 3 * P
                    for i in range(4):
                        act.wait_ge(row_max, next_of(row_max))
                        act.wait_ge(tile_full, full(i))
                        t = tile(i)
                        f(prA[i][:, 0:n], t[:, 0:n], ACT.Exp, bias=nsmx[:, i:i + 1], scale=ASCALE,
                                   accum_out=rsum[:, i:i + 1]).then_inc(act_freed, 1)
                elif k == "GATE":
                    for i in range(2):
                        copy_tile(i, gbc[:, i * 512:(i + 1) * 512])
                elif k == "FG":
                    for i in range(2):
                        copy_tile(i, final_gain[:, i * 512:(i + 1) * 512])
                elif k == "YOUT":
                    b = s[1]
                    rsqrt_parts(x[:, b, :])
                    act.wait_ge(y_done, next_of(y_done))
                    store(O["y_prompt"][0] if b == 0 else O["y_sample"][0, tok(b - 1), :], x[:, b, :])
            act.wait_ge(stored, 16 * sent["stored"])
            act.wait_ge(state_out, 16 * sent["state_out"])

        @block.vector
        def _(dve):
            begin, tile, full, by, emptied, next_of, one, noted = places("D")
            V = nc.vector

            def bc(ap, n):
                return ap.unsqueeze(len(ap.shape)).to_broadcast([*ap.shape, n])

            def rsqrt(n, width):
                V.tensor_scalar(ms[:, 0:n], ssq[:, 0:n], 1.0 / width, EPS, ALU.mult, ALU.add).then_inc(mean_sq, 1)
                dve.wait_ge(root, next_of(root))
                V.reciprocal(rstd[:, 0:n], sd[:, 0:n]).then_inc(dve_chain, one())
                dve.wait_ge(dve_chain, noted())

            def top16(vals, idx, srcs):
                sets = range(len(srcs))
                for e in sets:
                    V.max(vals[:, e, 0:8], srcs[e]).then_inc(dve_chain, one())
                dve.wait_ge(dve_chain, noted())
                for e in sets:
                    V.max_index(idx[:, e, 0:8], vals[:, e, 0:8], srcs[e]).then_inc(dve_chain, one())
                dve.wait_ge(dve_chain, noted())
                for e in sets:
                    V.match_replace(srcs[e], vals[:, e, 0:8], srcs[e], NEG).then_inc(dve_chain, one())
                dve.wait_ge(dve_chain, noted())
                for e in sets:
                    V.max(vals[:, e, 8:16], srcs[e]).then_inc(dve_chain, one())
                dve.wait_ge(dve_chain, noted())
                for e in sets:
                    last = V.max_index(idx[:, e, 8:16], vals[:, e, 8:16], srcs[e])
                    if e < len(srcs) - 1:
                        last.then_inc(dve_chain, one())
                last.then_inc(dve_step, 1)

            def weigh(b, n, slot, ring):
                dve.wait_ge(gelus, n + 1)
                g = gate[:, b, slot:slot + GS] if isinstance(slot, int) else gate[:, b, bass.ds(slot, GS)]
                V.tensor_tensor(wv[:, ring, :], act_out[:, ring, :], g, ALU.mult).then_inc(weighted, 1)

            def add_up(n, ring):
                dve.wait_ge(weighted, n + 1)
                V.scalar_tensor_tensor(side[:], rows[:, ring * GS + GS - 1, D:2 * D], wv[:, ring, GS - 1:GS], side[:],
                                       ALU.mult, ALU.add).then_inc(side_summed, 1)

            def group(b, place):
                def body(order, n, slot, ring, turn, g):
                    if g == 0:
                        V.memset(side[:], 0.0).then_inc(side_zero, 1)
                        dve.wait_ge(side_zero, n // GROUPS + 1)
                    for j in range(GS):
                        r = ring * GS + j
                        dve.wait_ge(rows_in[r], turn * 16 + 16)
                        last = V.tensor_tensor_reduce(out=rows[:, r, 0:D], in0=rows[:, r, 0:D], in1=xb[:, place, :],
                                                      scale=1.0, scalar=0.0, op0=ALU.mult, op1=ALU.add,
                                                      accum_out=act_in[:, ring, j:j + 1])
                    last.then_inc(dots, 1)
                    if g != 0:
                        weigh(b, n - 1, slot - GS, (ring - 1) % RING)
                        if has_side(order, (ring - 1) % RING):
                            add_up(n - 1, (ring - 1) % RING)
                return body

            def last_groups(b):
                def body(order, n):
                    weigh(b, n - 1, SLOTS - GS, (n - 1) % RING)
                    if has_side(order, (n - 1) % RING):
                        add_up(n - 1, (n - 1) % RING)
                return body

            V.memset(cs[:], 0.0).then_inc(zeroed, 1)
            dve.wait_ge(inputs_in, 48)
            for n_entry in in_order("D"):
                s = PLAN[n_entry]
                k = s[0]
                tiles, by_act, by_dve, acts, dves = begin(n_entry)
                if tiles:
                    dve.wait_ge(tile_full, tiles)
                if by_act:
                    dve.wait_ge(act_freed, by_act)
                if by_dve:
                    dve.wait_ge(dve_freed, by_dve)
                if acts:
                    dve.wait_ge(act_step, acts)
                if dves:
                    dve.wait_ge(dve_step, dves)
                if k == "GROUPS":
                    if s[3] == 0:
                        dve.wait_ge(experts_chosen, QUARTERS * GORDER.index((s[1], s[2])) + 1)
                    run_groups(dve, s, group(s[2], GORDER.index((s[1], s[2])) % 2), last_groups(s[2]))
                    continue
                if noted():
                    dve.wait_ge(dve_chain, noted())
                if k == "MOD":
                    _, l, q = s
                    for j in range(4):
                        dve.wait_ge(tile_full, full(MOD_COLUMNS[j]))
                        t = tile(MOD_COLUMNS[j])
                        n = slice(8 * q + 2 * j, 8 * q + 2 * j + 2)
                        V.tensor_tensor(modT[:, l, n, :], t[:, 0:4].rearrange("p (n c) -> p n c", c=2),
                                        bc(ada_b[:, l, n], 2), ALU.add).then_inc(dve_freed, 1)
                    dve.wait_ge(by(MOD_COLUMNS[3]), emptied(MOD_COLUMNS[3]))
                    if q in (1, 4):
                        w = q // 4
                        V.tensor_scalar(gain[:, l, w], modT[:, l, 8 * q:8 * q + 8, :], 1.0, None, ALU.add).then_inc(dve_chain, one())
                        dve.wait_ge(dve_chain, noted())
                        V.tensor_tensor(gain[:, l, w], gain[:, l, w], bc(norm_g[:, l, w], 2), ALU.mult).then_inc(dve_step, 1)
                elif k == "NORM":
                    dve.wait_ge(squares, next_of(squares))
                    rsqrt(1, D)
                    V.tensor_scalar(normed(s), x[:, s[3], :], rstd[:, 0:1], None, ALU.mult).then_inc(dve_step, 1)
                elif k == "NT":
                    _, l, w, b = s
                    c = COND[b]
                    dve.wait_ge(tile_full, full(1))
                    t = tile(1)
                    place = tok(b - (b > 0))
                    for q in range(4):
                        last = V.tensor_scalar(hT[:, 4 + q, place], t[:, q * P:(q + 1) * P], gain[:, l, w, 4 + q, c:c + 1],
                                               modT[:, l, 24 * w + 4 + q, c:c + 1], ALU.mult, ALU.add)
                    last.then_inc(dve_freed, 1)
                elif k == "CONV":
                    _, g, half = s
                    n = P * len(BLOCKS[g])
                    V.memset(raw[:, 4 * half:4 * half + 4, 0:1], 0.0).then_inc(dve_chain, one())
                    V.memset(raw[:, 4 * half:4 * half + 4, n + 1:n + 2], 0.0).then_inc(dve_chain, one())
                    dve.wait_ge(dve_chain, noted())
                    for i in range(4):
                        e = 4 * half + i
                        V.tensor_scalar(cv[:, e, 0:n], raw[:, e, 0:n], conv_w[:, e, 0:1], None, ALU.mult).then_inc(dve_chain, one())
                        dve.wait_ge(dve_chain, noted())
                        for j in (1, 2):
                            last = V.scalar_tensor_tensor(cv[:, e, 0:n], raw[:, e, j:j + n], conv_w[:, e, j:j + 1],
                                                          cv[:, e, 0:n], ALU.mult, ALU.add)
                            if j == 1:
                                last.then_inc(dve_chain, one())
                                dve.wait_ge(dve_chain, noted())
                        last.then_inc(convolved, 1)
                elif k == "MLV":
                    _, g, half = s
                    V.memset(va[:, 0:len(BLOCKS[g]), 2 * half:2 * half + 2, DV], 1.0).then_inc(dve_step, 1)
                elif k == "MLG":
                    g = s[1]
                    nb = len(BLOCKS[g])
                    n = 8 * nb
                    dve.wait_ge(tile_full, full(0))
                    t = tile(0)
                    gt = gates_all[:, 0:nb, :]
                    V.tensor_tensor(gt, t[:, 0:16 * nb].rearrange("p (b n) -> p b n", n=16),
                                          cst("gate_b").unsqueeze(1).to_broadcast([P, nb, 16]), ALU.add).then_inc(dve_freed, 1)
                    dve.wait_ge(by(0), emptied(0))
                    kinds = gtmp[:, 0, 0:16 * nb].rearrange("p (e k h) -> p e k h", k=2, h=MH)
                    fg, inp = kinds[:, :, 1, :], kinds[:, :, 0, :]
                    part = [gtmp[:, i, 0:n].rearrange("p (e h) -> p e h", h=MH) for i in range(4)]
                    flat = [v[:, 0:nb].rearrange("p b d h -> p (b d) h") for v in (ig, nlf)]
                    V.scalar_tensor_tensor(part[1], fg, -1.0, fg, ALU.mult, ALU.max).then_inc(abs_gate, 1)
                    V.tensor_copy(flat[0], inp).then_inc(dve_chain, one())
                    V.tensor_scalar(flat[1], fg, -1.0, 0.0, ALU.mult, ALU.max).then_inc(dve_chain, one())
                    dve.wait_ge(dve_chain, noted())
                    dve.wait_ge(soft_gate, next_of(soft_gate))
                    V.tensor_tensor(flat[1], flat[1], part[3], ALU.add).then_inc(log_gate, 1)
                    if g == "P":
                        V.memset(mst, 0.0).then_inc(dve_chain, one())
                    else:
                        V.tensor_copy(mst.rearrange("p d h -> p (d h)"), cst("m0")).then_inc(dve_chain, one())
                    dve.wait_ge(tile_full, full(1))
                    t = tile(1)
                    V.tensor_copy(bt[:, 0:nb, :], t[:, 0:16 * nb].rearrange("p (b n) -> p b n", n=16)).then_inc(dve_freed, 1)
                    dve.wait_ge(by(1), emptied(1))
                    V.tensor_tensor(rcol[:, 0:nb].rearrange("p b d h -> p b (d h)"), ig[:, 0:nb].rearrange("p b d h -> p b (d h)"),
                                        bt[:, 0:nb, 0:8], ALU.add).then_inc(dve_step, 1)
                elif k == "MLA":
                    _, g, d, b = s
                    each = lambda m: m.unsqueeze(1).to_broadcast([P, MH, P])
                    V.tensor_tensor(WT, each(tri[:, d, :]), bc(nlf[:, b, d, :], P), ALU.mult).then_inc(dve_chain, one())
                    V.tensor_tensor(W, each(ident), bc(ig[:, b, d, :], P), ALU.mult).then_inc(dve_chain, one())
                    dve.wait_ge(dve_chain, noted())
                    V.tensor_tensor(W, W, WT, ALU.add).then_inc(decay_rows, 1)
                    dve.wait_ge(tile_full, full(0))
                    t = tile(0).rearrange("p (h n) -> p h n", n=P)
                    V.tensor_reduce(rall, t, AX.X, ALU.max).then_inc(dve_chain, one())
                    V.tensor_tensor(W, t, each(mask[:, d, :]), ALU.add).then_inc(dve_freed, 1)
                    dve.wait_ge(by(0), emptied(0))
                    V.tensor_reduce(rmx, W, AX.X, ALU.max).then_inc(dve_chain, one())
                    dve.wait_ge(dve_chain, noted())
                    V.tensor_tensor(rmx, rmx, mst[:, d, :], ALU.max).then_inc(dve_chain, one())
                    dve.wait_ge(dve_chain, noted())
                    V.tensor_tensor(t12[:, 0:4], mst[:, d, :], rmx, ALU.subtract).then_inc(dve_chain, one())
                    V.tensor_scalar(nMp, rmx, -1.0, None, ALU.mult).then_inc(dve_chain, one())
                    dve.wait_ge(dve_chain, noted())
                    V.tensor_tensor(t12[:, 4:8], bt[:, b, 4 * d:4 * d + 4], nMp, ALU.add).then_inc(maxima, 1)
                    dve.wait_ge(tile_full, full(1))
                    t = tile(1)
                    dve.wait_ge(probs_raw, next_of(probs_raw))
                    Wf = W.rearrange("p h n -> p (h n)")
                    V.scalar_tensor_tensor(Wf, t[:], KSCALE, Wf, ALU.mult, ALU.mult).then_inc(dve_freed, 1)
                elif k == "MLB":
                    _, g, d, b = s
                    for h in range(MH):
                        if g == "S":
                            dve.wait_ge(by(2 * h), emptied(2 * h))
                            dve.wait_ge(tile_full, full(2 * h + 1))
                            t = tile(2 * h + 1)
                            V.tensor_tensor(Nn[:, h, :], t[:, 0:DV + 1], Nn[:, h, :], ALU.add).then_inc(dve_freed, 1)
                            dve.wait_ge(by(2 * h + 1), emptied(2 * h + 1))
                        else:
                            dve.wait_ge(tile_full, full(h))
                            t = tile(h)
                            V.tensor_copy(Nn[:, h, :], t[:, 0:DV + 1]).then_inc(dve_freed, 1)
                            dve.wait_ge(by(h), emptied(h))
                    V.tensor_scalar(den, Nn[:, :, DV], -1.0, None, ALU.mult).then_inc(dve_chain, one())
                    dve.wait_ge(dve_chain, noted())
                    V.tensor_tensor(den, den, Nn[:, :, DV], ALU.max).then_inc(dve_chain, one())
                    dve.wait_ge(dve_chain, noted())
                    V.tensor_tensor(den, den, ae[:, 4:8], ALU.max).then_inc(dve_chain, one())
                    dve.wait_ge(dve_chain, noted())
                    V.reciprocal(rden, den).then_inc(dve_chain, one())
                    dve.wait_ge(dve_chain, noted())
                    out = hm[:, b, :].rearrange("p (h v) -> p h v", v=DV)
                    if d == 0:
                        V.tensor_tensor(out, Nn[:, :, 0:DV], bc(rden, DV), ALU.mult).then_inc(dve_step, 1)
                    else:
                        V.tensor_tensor(Nn[:, :, 0:DV], Nn[:, :, 0:DV], bc(rden, DV), ALU.mult).then_inc(dve_chain, one())
                        dve.wait_ge(dve_chain, noted())
                        V.tensor_tensor(out, out, Nn[:, :, 0:DV], ALU.add).then_inc(dve_step, 1)
                elif k == "MLC":
                    _, g, d, b = s
                    V.tensor_tensor(mpp, mst[:, d, :], rall, ALU.max).then_inc(dve_chain, one())
                    dve.wait_ge(dve_chain, noted())
                    V.tensor_tensor(dww[:, 0:4], mst[:, d, :], mpp, ALU.subtract).then_inc(dve_chain, one())
                    dve.wait_ge(dve_chain, noted())
                    V.tensor_tensor(dww[:, 4:8], rcol[:, b, d, :], mpp, ALU.subtract).then_inc(carry_in, 1)
                    V.tensor_tensor(mst[:, d, :], mpp, bt[:, b, 8 + 4 * d:12 + 4 * d], ALU.subtract).then_inc(dve_chain, one())
                    dve.wait_ge(dve_chain, noted())
                    dve.wait_ge(carry_exp, next_of(carry_exp))
                    V.tensor_scalar(dw[:, 4:8], dw[:, 4:8], KSCALE, None, ALU.mult).then_inc(dve_chain, one())
                    dve.wait_ge(dve_chain, noted())
                    dve.wait_ge(tile_full, full(0))
                    t = tile(0)
                    V.tensor_tensor(W, t[:].rearrange("p (h n) -> p h n", n=P), bc(dw[:, 4:8], P), ALU.mult).then_inc(dve_freed, 1)
                    if g == "P" and d == 1:
                        dve.wait_ge(state_out, 48)
                    for h in range(MH):
                        dve.wait_ge(tile_full, full(1 + h))
                        t = tile(1 + h)
                        if g == "P":
                            last = V.tensor_copy(Cst[:, h, :], t[:, 0:DV + 1])
                        else:
                            last = V.scalar_tensor_tensor(Cst[:, h, :], Cst[:, h, :], dw[:, h:h + 1], t[:, 0:DV + 1],
                                                          ALU.mult, ALU.add)
                        last.then_inc(dve_freed, 1)
                elif k == "MLN":
                    if s[1] == "P":
                        dve.wait_ge(state_out, 96)
                    for b in range(len(BLOCKS[s[1]])):
                        h4 = hm[:, b, :].rearrange("p (h v) -> p h v", v=DV)
                        V.tensor_tensor(Nn[:, :, 0:DV], h4, h4, ALU.mult).then_inc(dve_chain, one())
                        dve.wait_ge(dve_chain, noted())
                        V.tensor_reduce(ssq[:, 0:MH], Nn[:, :, 0:DV], AX.X, ALU.add).then_inc(dve_chain, one())
                        dve.wait_ge(dve_chain, noted())
                        rsqrt(MH, DV)
                        last = V.tensor_tensor(h4, h4, bc(rstd[:, 0:MH], DV), ALU.mult)
                        if b < len(BLOCKS[s[1]]) - 1:
                            last.then_inc(dve_chain, one())
                            dve.wait_ge(dve_chain, noted())
                    last.then_inc(dve_step, 1)
                elif k == "MLO":
                    _, g, half = s
                    nb = len(BLOCKS[g])
                    for j in range(2):
                        for b in range(nb):
                            i = j * nb + b
                            dve.wait_ge(by(i), emptied(i))
                            h1 = hm[:, b, (2 * half + j) * DV:(2 * half + j + 1) * DV]
                            last = V.tensor_tensor(h1, h1, Nflat[:, i * WC:(i + 1) * WC], ALU.mult)
                    last.then_inc(dve_step, 1)
                elif k == "OUT":
                    _, l, g, half = s
                    nb = len(BLOCKS[g])
                    if l == 1 and g == "P" and half == 0:
                        dve.wait_ge(stored, 32)
                    for j in range(2):
                        for b in range(nb):
                            i = j * nb + b
                            c = slice((2 * half + j) * WC, (2 * half + j + 1) * WC)
                            dve.wait_ge(tile_full, full(i))
                            t = tile(i)
                            tmp = xn[:, i * WC:(i + 1) * WC]
                            V.tensor_tensor(tmp, t[:, 0:WC], gbc[:, c], ALU.mult).then_inc(dve_freed, 1)
                            dve.wait_ge(by(i), emptied(i))
                            xc = x[:, BLOCKS[g][b], c]
                            last = V.tensor_tensor(xc, xc, tmp, ALU.add)
                            if i < 2 * nb - 1:
                                last.then_inc(dve_chain, one())
                    last.then_inc(dve_step, 1)
                elif k == "PS":
                    n = slice(2 * QH * s[4], 2 * QH * (s[4] + 1))
                    dve.wait_ge(tile_full, full(0))
                    V.tensor_copy(sc[:, n, :], tile(0)[:].rearrange("p (e n) -> p e n", n=NKEYS)).then_inc(dve_freed, 1)
                elif k == "PT":
                    q = s[4]
                    n = slice(2 * QH * q, 2 * QH * (q + 1))
                    top16(top1[:, n, :], i1u[:, n, :], [sc[:, e, :] for e in range(n.start, n.stop)])
                elif k == "PC":
                    q = s[4]
                    n = slice(QH * q, QH * (q + 1))
                    t2 = top1.rearrange("p (h a) k -> p h a k", a=2)[:, n]
                    c4 = cand[:, 0:QH, :].rearrange("p h (i j) -> p h i j", j=TOPK)
                    V.tensor_tensor(c4, bc(t2[:, :, 0, :], TOPK),
                                           t2[:, :, 1, :].unsqueeze(2).to_broadcast([P, QH, TOPK, TOPK]), ALU.add).then_inc(dve_chain, one())
                    dve.wait_ge(dve_chain, noted())
                    top16(topc[:, n, :], posu[:, n, :], [cand[:, h, :] for h in range(QH)])
                elif k == "PG":
                    _, l, g, b, part = s
                    blk = BLOCKS[g][b]
                    nh = QH
                    heads = slice(part * nh, (part + 1) * nh)
                    n = slice(part * nh * TOPK, (part + 1) * nh * TOPK)
                    tc = topc[:, heads, :]
                    V.tensor_copy(gsum[:, 0:nh], tc[:, :, 0]).then_inc(dve_chain, one())
                    dve.wait_ge(dve_chain, noted())
                    V.tensor_tensor(tc, tc, bc(gsum[:, 0:nh], TOPK), ALU.subtract).then_inc(tops, 1)
                    pos = posu.rearrange("p h k -> p (h k)")[:, n]
                    V.tensor_scalar(piju[:, 0, n], pos, 4, None, ALU.logical_shift_right).then_inc(dve_chain, one())
                    V.tensor_scalar(piju[:, 1, n], pos, 15, None, ALU.bitwise_and).then_inc(dve_chain, one())
                    keys = i1f[:, 2 * part * nh:2 * (part + 1) * nh, :]
                    V.tensor_copy(keys, i1u[:, 2 * part * nh:2 * (part + 1) * nh, :]).then_inc(dve_chain, one())
                    dve.wait_ge(dve_chain, noted())
                    V.tensor_copy(pij[:, :, n], piju[:, :, n]).then_inc(dve_chain, one())
                    dve.wait_ge(dve_chain, noted())
                    place_of = [cand[:, 0:nh, :].rearrange("p a b -> p (a b)"), sc[:, 2 * part * nh:2 * (part + 1) * nh, :].rearrange("p a b -> p (a b)")]
                    keys = keys.rearrange("p (h a) k -> p h a k", a=2)
                    slots = nh * TOPK
                    for a in range(2):
                        V.tensor_tensor(place_of[a].rearrange("p (s e) -> p s e", e=TOPK), bc(pij[:, a, n], TOPK),
                                             cst("iota").unsqueeze(1).to_broadcast([P, slots, TOPK]), ALU.is_equal).then_inc(dve_chain, one())
                    dve.wait_ge(dve_chain, noted())
                    for a in range(2):
                        hot4 = place_of[a].rearrange("p (h s e) -> p h s e", h=nh, e=TOPK)
                        V.tensor_tensor(hot4, hot4, keys[:, :, a, :].unsqueeze(2).to_broadcast([P, nh, TOPK, TOPK]), ALU.mult).then_inc(dve_chain, one())
                    dve.wait_ge(dve_chain, noted())
                    for a in range(2):
                        V.tensor_reduce(e12[:, a, n], place_of[a].rearrange("p (s e) -> p s e", e=TOPK), AX.X, ALU.add).then_inc(dve_chain, one())
                    dve.wait_ge(dve_chain, noted())
                    V.scalar_tensor_tensor(e12[:, 0, n], e12[:, 0, n], float(NKEYS), e12[:, 1, n], ALU.mult, ALU.add).then_inc(dve_chain, one())
                    dve.wait_ge(dve_chain, noted())
                    V.tensor_scalar(eidx[:, blk, n], e12[:, 0, n], float(l * EXPERTS), None, ALU.add).then_inc(experts_chosen, 1)
                    dve.wait_ge(top_exp, next_of(top_exp))
                    V.tensor_reduce(gsum[:, 0:nh], tc, AX.X, ALU.add).then_inc(dve_chain, one())
                    dve.wait_ge(dve_chain, noted())
                    V.reciprocal(grec[:, 0:nh], gsum[:, 0:nh]).then_inc(dve_chain, one())
                    dve.wait_ge(dve_chain, noted())
                    V.tensor_tensor(gate[:, blk, n].rearrange("p (h k) -> p h k", k=TOPK), tc, bc(grec[:, 0:nh], TOPK), ALU.mult)\
                        .then_inc(dve_step, 1)
                elif k == "AN":
                    _, g, b = s
                    heads = AH + AKV
                    w = qkv[:, b, 0:heads * HD]
                    w3 = w.rearrange("p (h n) -> p h n", n=HD)
                    V.tensor_tensor(sq20, w, w, ALU.mult).then_inc(dve_chain, one())
                    dve.wait_ge(dve_chain, noted())
                    V.tensor_reduce(ssq, sq20.rearrange("p (h n) -> p h n", n=HD), AX.X, ALU.add).then_inc(dve_chain, one())
                    dve.wait_ge(dve_chain, noted())
                    rsqrt(heads, HD)
                    V.tensor_tensor(w3, w3, bc(rstd, HD), ALU.mult).then_inc(dve_chain, one())
                    dve.wait_ge(dve_chain, noted())
                    V.tensor_tensor(w3[:, 0:AH], w3[:, 0:AH], cst("q_g").unsqueeze(1).to_broadcast([P, AH, HD]), ALU.mult).then_inc(dve_chain, one())
                    dve.wait_ge(dve_chain, noted())
                    last = V.tensor_tensor(w3[:, AH:], w3[:, AH:], cst("k_g").unsqueeze(1).to_broadcast([P, AKV, HD]), ALU.mult)
                    if g == "P":
                        last.then_inc(kv_done, 1)
                        dve.wait_ge(kv_done, next_of(kv_done))
                        V.tensor_copy(ssq, rstd).then_inc(dve_step, 1)
                    else:
                        last.then_inc(dve_chain, one())
                        dve.wait_ge(dve_chain, noted())
                        wr = w.rearrange("p (h a r n) -> p h a r n", a=2, r=2, n=16)
                        t = sq20.rearrange("p (r h a n) -> p r h a n", r=2, a=2, n=16)
                        for a in range(2):
                            x1, x2 = wr[:, :, a, 0, :], wr[:, :, a, 1, :]
                            t1, t2 = t[:, 0, :, a, :], t[:, 1, :, a, :]
                            o = b * 32 + a * 16
                            cc = cst("cos")[:, o:o + 16].unsqueeze(1).to_broadcast([P, heads, 16])
                            ss = cst("sin")[:, o:o + 16].unsqueeze(1).to_broadcast([P, heads, 16])
                            V.tensor_tensor(t1, x1, ss, ALU.mult).then_inc(dve_chain, one())
                            V.tensor_tensor(t2, x2, ss, ALU.mult).then_inc(dve_chain, one())
                            dve.wait_ge(dve_chain, noted())
                            V.tensor_tensor(x1, x1, cc, ALU.mult).then_inc(dve_chain, one())
                            V.tensor_tensor(x2, x2, cc, ALU.mult).then_inc(dve_chain, one())
                            dve.wait_ge(dve_chain, noted())
                            V.tensor_tensor(x1, x1, t2, ALU.subtract).then_inc(dve_chain, one())
                            last = V.tensor_tensor(x2, x2, t1, ALU.add)
                            if a == 0:
                                last.then_inc(dve_chain, one())
                                dve.wait_ge(dve_chain, noted())
                        last.then_inc(dve_step, 1)
                elif k == "AT":
                    _, g, b = s
                    keys = qkv[:, b, AH * HD:(AH + AKV) * HD].rearrange("p (v n) -> p v n", n=HD)
                    V.tensor_copy(kdup[:, :, 0, :], keys).then_inc(dve_chain, one())
                    dve.wait_ge(dve_chain, noted())
                    V.tensor_copy(kdup[:, :, 1, :], keys).then_inc(key_pairs, 1)
                elif k == "AS":
                    _, g, b, kv = s
                    n = P if g == "P" else 3 * P
                    for i in range(4):
                        dve.wait_ge(tile_full, full(i))
                        t = tile(i)
                        V.tensor_reduce(smx[:, i:i + 1], t[:, 0:n], AX.X, ALU.max).then_inc(dve_chain, one())
                        dve.wait_ge(dve_chain, noted())
                        V.tensor_scalar(nsmx[:, i:i + 1], smx[:, i:i + 1], -ASCALE, None, ALU.mult).then_inc(row_max, 1)
                    for i in range(4):
                        dve.wait_ge(tile_full, full(4 + i))
                        t = tile(4 + i)
                        V.tensor_copy(pTa[i % 2][:, 0:n], t[:, 0:n]).then_inc(dve_freed, 1)
                    V.reciprocal(rrs, rsum).then_inc(dve_chain, one())
                    dve.wait_ge(dve_chain, noted())
                    dve.wait_ge(tile_full, full(8))
                    t = tile(8)
                    o = qkv[:, b, kv * 4 * HD:(kv * 4 + 4) * HD].rearrange("p (h n) -> p h n", n=HD)
                    V.tensor_tensor(o, t[:, 0:4 * HD].rearrange("p (h n) -> p h n", n=HD), bc(rrs, HD), ALU.mult).then_inc(dve_freed, 1)
                elif k == "FIN":
                    _, l, b = s
                    dve.wait_ge(summed, (GORDER.index((l, b)) + 1) * GROUPS)
                    dve.wait_ge(side_summed, side_sums((GORDER.index((l, b)) + 1) * GROUPS))
                    V.tensor_tensor(xn, acc[:], side[:], ALU.add).then_inc(sum_read, 1)
                    dve.wait_ge(sum_read, next_of(sum_read))
                    V.tensor_tensor(xn, xn, gbc, ALU.mult).then_inc(dve_chain, one())
                    dve.wait_ge(dve_chain, noted())
                    V.tensor_tensor(x[:, b, :], x[:, b, :], xn, ALU.add).then_inc(dve_step, 1)
                elif k == "YOUT":
                    b = s[1]
                    dve.wait_ge(squares, next_of(squares))
                    rsqrt(1, D)
                    V.scalar_tensor_tensor(x[:, b, :], x[:, b, :], rstd[:, 0:1], final_gain, ALU.mult, ALU.mult).then_inc(y_done, 1)
                    dve.wait_ge(y_done, next_of(y_done))
                    V.tensor_copy(ssq[:, 0:1], rstd[:, 0:1]).then_inc(dve_step, 1)


_OUTS = [("y_prompt", (1, 128, 1024)), ("y_sample", (1, 256, 1024)), ("new_C", (1, 1, 2, 4, 128, 256)),
         ("new_n", (1, 1, 2, 4, 128)), ("new_m", (1, 1, 2, 4)), ("new_k", (1, 1, 4, 128, 64)), ("new_v", (1, 1, 4, 128, 64))]


def small_inputs(v):
    f = np.float32
    s = np.arange(P)

    def by_feature(a):
        return np.ascontiguousarray(a).reshape(-1, P).T

    def everywhere(a):
        return np.broadcast_to(np.ascontiguousarray(a).reshape(1, -1), (P, a.size))

    half = HD // 4
    inv = 10000.0 ** (-np.arange(half, dtype=f) / half)
    t = np.arange(2 * P)
    ang = np.concatenate([(t // 64).astype(f)[:, None] * inv, (t % 64).astype(f)[:, None] * inv], -1).astype(f)
    rope = lambda a: a.astype(f).reshape(2, P, 32).transpose(1, 0, 2).reshape(P, 64)
    upto, since = s[:, None] <= s[None, :], s[:, None] >= s[None, :]
    parts = {
        "ident": np.eye(P, dtype=f), "ones": np.ones((P, P), f),
        "tri": np.concatenate([upto, since], 1).astype(f),
        "mask": np.where(np.concatenate([since, upto], 1), 0.0, NEG).astype(f),
        "pick": (s[:, None] % 32 == np.arange(2)).astype(f), "iota": everywhere(np.arange(TOPK, dtype=f)), "cos": rope(np.cos(ang)), "sin": rope(np.sin(ang)),
        "cond": np.stack([v["c_ctx"].reshape(P, KC), v["c"].reshape(P, KC)], -1).reshape(P, 2 * KC),
        "ada_b": by_feature(v["ada_b"]), "norm_g": by_feature(v["norm_g"]), "final_g": by_feature(v["final_g"]),
        "head_g": by_feature(v["mlstm_head_g"]),
        "conv_w": v["mlstm_conv_w"][0].reshape(3, KC, P).transpose(2, 1, 0).reshape(P, 3 * KC),
        "conv_b": by_feature(v["mlstm_conv_b"]), "gate_b": everywhere(v["mlstm_gate_b"]),
        "q_g": everywhere(v["attn_q_g"]), "k_g": everywhere(v["attn_k_g"]), "m0": everywhere(v["state_mlstm_m"]),
        "w_gate": v["mlstm_w_in"][0, :, 3072:].reshape(KC, P, 16).transpose(1, 0, 2).reshape(P, KC * 16),
    }
    return np.ascontiguousarray(np.concatenate([parts[n] for n in SMALL], 1))


def kernel(**inputs):
    import concourse.bacc as _bacc
    from concourse.bass_utils import run_bass_kernel_spmd as _run

    v = {k: np.asarray(a) for k, a in inputs.items()}
    arrays = {n: np.ascontiguousarray(v[n]) for n in (
        "x_prompt", "x_sample", "state_mlstm_C", "state_mlstm_n", "cache_attn_k", "cache_attn_v", "ada_w",
        "mlstm_w_in", "mlstm_w_out", "attn_w_qkv", "attn_w_out", "peer_w_q")}
    arrays["uv"] = np.concatenate([v["peer_u"], v["peer_v"]], -1).reshape(DEPTH * EXPERTS, 2 * D)
    arrays["subkeys"] = np.ascontiguousarray(v["peer_subkeys"].transpose(0, 4, 1, 2, 3)).reshape(DEPTH, P, NSETS * NKEYS)
    arrays["small"] = small_inputs(v)
    nc = _bacc.Bacc("TRN2", target_bir_lowering=False, num_devices=1)
    A = {n: nc.dram_tensor(f"in_{n}", a.shape, mybir.dt.from_np(a.dtype), kind="ExternalInput").ap() for n, a in arrays.items()}
    O = {n: nc.dram_tensor(f"out_{n}", shape, F32, kind="ExternalOutput").ap() for n, shape in _OUTS}
    trunk(nc, A, O)
    r = _run(nc, [{f"in_{n}": a for n, a in arrays.items()}], core_ids=[0])
    return tuple(r.results[0][f"out_{n}"] for n, _ in _OUTS)
```
